# Optimizing a Trainium2 kernel written in Bass

```python
import math
import jax
import jax.numpy as jnp
from jax import lax
import numpy as np

D_MODEL = 1024
BATCH = 1
SEQ = 1024
DEPTH = 1

D_MIX = D_MODEL
GROUP_WIDTH = D_MIX // 4
BLOCK_Q = 128

SB_HEADS = 4
SB_HEAD_DIM = GROUP_WIDTH // SB_HEADS

DA_HEADS = 4
DA_V_DIM = GROUP_WIDTH // DA_HEADS
DA_QK_DIM = DA_V_DIM // 2
DA_SUBLN_EPS = 1e-5

CONV_WIDTH = 3

RW_HEADS = 4
RW_HEAD_DIM = GROUP_WIDTH // RW_HEADS
RW_DECAY_RANK = 32
RW_A_RANK = 32
RW_GATE_RANK = 64
RW_LN_EPS = 64e-5

REL_BUCKETS = 32
REL_MAX_DIST = 128

N_EXPERTS = 16
N_EXPERT_GROUPS = 4
EXPERTS_PER_GROUP = N_EXPERTS // N_EXPERT_GROUPS
TOP_K = 2
D_EXPERT = 256

LN_EPS = 1e-5
DEEPNORM_ALPHA = (2 * DEPTH) ** 0.25
DEEPNORM_BETA = (8 * DEPTH) ** -0.25

SB_COLS = 3 * GROUP_WIDTH
DA_COLS = 3 * GROUP_WIDTH
SC_COLS = 3 * GROUP_WIDTH
RW_COLS = 3 * GROUP_WIDTH + RW_DECAY_RANK + RW_A_RANK + RW_GATE_RANK
P_IN = SB_COLS + DA_COLS + SC_COLS + RW_COLS
IN_SPLITS = [SB_COLS, SB_COLS + DA_COLS, SB_COLS + DA_COLS + SC_COLS]
RW_SPLITS = [GROUP_WIDTH, 2 * GROUP_WIDTH, 3 * GROUP_WIDTH,
             3 * GROUP_WIDTH + RW_DECAY_RANK,
             3 * GROUP_WIDTH + RW_DECAY_RANK + RW_A_RANK]

kernel_name = 'hybrid_parallel_groups_grouped_moe'

def _heads(t, n_heads):
    b, s, _ = t.shape
    return t.reshape(b, s, n_heads, -1).transpose(0, 2, 1, 3)

def _merge(t):
    b, n, s, d = t.shape
    return t.transpose(0, 2, 1, 3).reshape(b, s, n * d)

def layer_norm(x, gain, bias):
    xf = x.astype(jnp.float32)
    mu = xf.mean(-1, keepdims=True)
    var = jnp.square(xf - mu).mean(-1, keepdims=True)
    return ((xf - mu) * lax.rsqrt(var + LN_EPS) * gain + bias).astype(x.dtype)

def relative_bias_by_distance(rel_table, seq):
    n = jnp.arange(seq)
    max_exact = REL_BUCKETS // 2
    nf = jnp.maximum(n, 1).astype(jnp.float32)
    large = max_exact + (jnp.log(nf / max_exact) / math.log(REL_MAX_DIST / max_exact)
                         * (REL_BUCKETS - max_exact)).astype(jnp.int32)
    large = jnp.minimum(large, REL_BUCKETS - 1)
    bucket = jnp.where(n < max_exact, n, large)
    return rel_table[bucket].T

def stick_breaking_attention(q, k, v):
    q = _heads(q, SB_HEADS).astype(jnp.float32) * SB_HEAD_DIM ** -0.5
    k = _heads(k, SB_HEADS).astype(jnp.float32)
    v = _heads(v, SB_HEADS).astype(jnp.float32)
    seq = q.shape[2]
    outs = []
    for i in range(seq // BLOCK_Q):
        q0 = i * BLOCK_Q
        end = q0 + BLOCK_Q
        z = jnp.einsum('bhqd,bhkd->bhqk', q[:, :, q0:end], k[:, :, :end])
        strict = jnp.arange(end)[None, :] < (q0 + jnp.arange(BLOCK_Q))[:, None]
        sp = jnp.where(strict, jax.nn.softplus(z), 0.0)
        log_w = jnp.where(strict, z - lax.cumsum(sp, axis=3, reverse=True), -jnp.inf)
        outs.append(jnp.einsum('bhqk,bhkd->bhqd', jnp.exp(log_w), v[:, :, :end]))
    return _merge(jnp.concatenate(outs, axis=2))

def diff_attention(q, k, v, lam_params, sub_gain, bias_dist, lam_init):
    b, s, _ = q.shape
    q = q.reshape(b, s, DA_HEADS, 2, DA_QK_DIM).transpose(0, 2, 3, 1, 4).astype(jnp.float32) * DA_QK_DIM ** -0.5
    k = k.reshape(b, s, DA_HEADS, 2, DA_QK_DIM).transpose(0, 2, 3, 1, 4).astype(jnp.float32)
    v = _heads(v, DA_HEADS).astype(jnp.float32)
    lp = lam_params.astype(jnp.float32)
    lam = jnp.exp(jnp.sum(lp[0] * lp[1])) - jnp.exp(jnp.sum(lp[2] * lp[3])) + lam_init
    bias_dist = bias_dist.astype(jnp.float32)
    outs = []
    for i in range(s // BLOCK_Q):
        q0 = i * BLOCK_Q
        end = q0 + BLOCK_Q
        logits = jnp.einsum('bhmqd,bhmkd->bhmqk', q[:, :, :, q0:end], k[:, :, :, :end])
        dist = (q0 + jnp.arange(BLOCK_Q))[:, None] - jnp.arange(end)[None, :]
        bias = bias_dist[:, jnp.maximum(dist, 0)]
        logits = jnp.where(dist >= 0, logits + bias[None, :, None], -jnp.inf)
        probs = jax.nn.softmax(logits, axis=-1)
        attn = probs[:, :, 0] - lam * probs[:, :, 1]
        outs.append(jnp.einsum('bhqk,bhkd->bhqd', attn, v[:, :, :end]))
    o = jnp.concatenate(outs, axis=2)
    o = o * lax.rsqrt(jnp.square(o).mean(-1, keepdims=True) + DA_SUBLN_EPS) * sub_gain * (1.0 - lam_init)
    return _merge(o)

def short_conv_mixer(b_gate, c_gate, h, conv_w):
    u = c_gate * h
    y = lax.conv_general_dilated(
        u, conv_w[:, None, :].astype(u.dtype), window_strides=(1,),
        padding=[(CONV_WIDTH - 1, 0)], dimension_numbers=('NWC', 'WIO', 'NWC'),
        feature_group_count=u.shape[-1])
    return b_gate * y

def rwkv7_time_mix(proj, mu, vecs, w_up, a_up, g_up):
    proj = proj.astype(jnp.float32)
    b, s, _ = proj.shape
    shifted = jnp.pad(proj, ((0, 0), (1, 0), (0, 0)))[:, :-1]
    xs = proj + (shifted - proj) * mu
    r, k, v, xw, xa, xg = jnp.split(xs, RW_SPLITS, axis=-1)
    vecs = vecs.astype(jnp.float32)
    w0, a0, k_k, k_a, r_k, lnx_g, lnx_b = [vecs[i] for i in range(7)]
    log_decay = -math.exp(-0.5) * jax.nn.sigmoid(w0 + jnp.tanh(xw) @ w_up)
    a = jax.nn.sigmoid(a0 + xa @ a_up)
    g = jax.nn.sigmoid(xg) @ g_up
    kk = (k * k_k).reshape(b, s, RW_HEADS, RW_HEAD_DIM)
    kk = kk / jnp.maximum(jnp.sqrt(jnp.sum(kk * kk, -1, keepdims=True)), 1e-12)
    k = k * (1.0 + (a - 1.0) * k_a)
    hd = lambda t: t.reshape(b, s, RW_HEADS, RW_HEAD_DIM)
    r_h, k_h, v_h, a_h = hd(r), hd(k), hd(v), hd(a)
    tm = lambda t: jnp.moveaxis(t, 1, 0)

    def step(state, inp):
        r_t, w_t, k_t, v_t, kk_t, ab_t = inp
        sa = jnp.einsum('bhij,bhj->bhi', state, -kk_t)
        state = (state * w_t[:, :, None, :] + sa[..., None] * ab_t[:, :, None, :]
                 + v_t[..., None] * k_t[:, :, None, :])
        return state, jnp.einsum('bhij,bhj->bhi', state, r_t)

    state0 = jnp.zeros((b, RW_HEADS, RW_HEAD_DIM, RW_HEAD_DIM), jnp.float32)
    xs_scan = (tm(r_h), tm(jnp.exp(hd(log_decay))), tm(k_h), tm(v_h), tm(kk), tm(kk * a_h))
    _, y = lax.scan(step, state0, xs_scan)
    y = jnp.moveaxis(y, 0, 1)
    mean = y.mean(-1, keepdims=True)
    var = jnp.square(y - mean).mean(-1, keepdims=True)
    y = ((y - mean) * lax.rsqrt(var + RW_LN_EPS)).reshape(b, s, GROUP_WIDTH) * lnx_g + lnx_b
    bonus = jnp.sum(r_h * k_h * r_k.reshape(RW_HEADS, RW_HEAD_DIM), -1, keepdims=True) * v_h
    return (y + bonus.reshape(b, s, GROUP_WIDTH)) * g

def grouped_moe(x, router_w, router_b, w_in, w_down):
    b, s, d = x.shape
    xf = x.reshape(b * s, d)
    affinity = jax.nn.sigmoid((xf @ router_w).astype(jnp.float32))
    select = affinity + router_b.astype(jnp.float32)
    grouped = select.reshape(-1, N_EXPERT_GROUPS, EXPERTS_PER_GROUP)
    group_score = lax.top_k(grouped, TOP_K)[0].sum(-1)
    best_group = jnp.argmax(group_score, axis=-1)
    in_group = (jnp.arange(N_EXPERTS) // EXPERTS_PER_GROUP)[None, :] == best_group[:, None]
    _, idx = lax.top_k(jnp.where(in_group, select, -jnp.inf), TOP_K)
    gate = jnp.take_along_axis(affinity, idx, axis=1)
    gate = gate / gate.sum(-1, keepdims=True)
    combine = (jax.nn.one_hot(idx, N_EXPERTS, dtype=jnp.float32) * gate[..., None]).sum(1)
    out = jnp.zeros((b * s, d), jnp.float32)
    for e in range(N_EXPERTS):
        gu = xf @ w_in[e]
        h = jax.nn.silu(gu[:, :D_EXPERT]) * gu[:, D_EXPERT:]
        out = out + combine[:, e:e + 1] * (h @ w_down[e]).astype(jnp.float32)
    return out.reshape(b, s, d).astype(x.dtype)

def setup_inputs(seed: int = 0) -> dict:
    key = jax.random.key(seed)
    ks = jax.random.split(key, 24)
    f32 = jnp.float32

    def nrm(k, shape, scale):
        return jax.random.normal(k, shape, f32) * scale

    x = nrm(ks[0], (BATCH, SEQ, D_MODEL), 1.0)
    w_in = nrm(ks[1], (DEPTH, D_MODEL, P_IN), D_MODEL ** -0.5)
    w_out = nrm(ks[2], (DEPTH, D_MIX, D_MODEL), D_MIX ** -0.5 * DEEPNORM_BETA)
    da_lambda = nrm(ks[3], (DEPTH, 4, DA_QK_DIM), 0.1)
    da_subln = 1.0 + nrm(ks[4], (DEPTH, DA_V_DIM), 0.02)
    sc_conv = nrm(ks[5], (DEPTH, CONV_WIDTH, GROUP_WIDTH), CONV_WIDTH ** -0.5)
    rw_mu = jax.random.uniform(ks[6], (DEPTH, RW_COLS), f32)
    vshape = (DEPTH, GROUP_WIDTH)
    rw_vecs = jnp.stack([
        nrm(ks[7], vshape, 0.5),
        nrm(ks[8], vshape, 0.1),
        0.85 + nrm(ks[9], vshape, 0.05),
        1.0 + nrm(ks[10], vshape, 0.05),
        nrm(ks[11], vshape, 0.1),
        1.0 + nrm(ks[12], vshape, 0.02),
        nrm(ks[13], vshape, 0.02),
    ], axis=1)
    rw_w_up = nrm(ks[14], (DEPTH, RW_DECAY_RANK, GROUP_WIDTH), 0.1 * RW_DECAY_RANK ** -0.5)
    rw_a_up = nrm(ks[15], (DEPTH, RW_A_RANK, GROUP_WIDTH), 0.1 * RW_A_RANK ** -0.5)
    rw_g_up = nrm(ks[16], (DEPTH, RW_GATE_RANK, GROUP_WIDTH), RW_GATE_RANK ** -0.5)
    ln_gain = 1.0 + nrm(ks[17], (DEPTH, 2, D_MODEL), 0.02)
    ln_bias = nrm(ks[18], (DEPTH, 2, D_MODEL), 0.02)
    rel_bias = nrm(ks[19], (REL_BUCKETS, DA_HEADS), 0.3)
    router_w = nrm(ks[20], (D_MODEL, N_EXPERTS), D_MODEL ** -0.5)
    router_b = nrm(ks[21], (N_EXPERTS,), 0.01)
    moe_w_in = nrm(ks[22], (DEPTH, N_EXPERTS, D_MODEL, 2 * D_EXPERT), D_MODEL ** -0.5)
    moe_w_down = nrm(ks[23], (DEPTH, N_EXPERTS, D_EXPERT, D_MODEL), D_EXPERT ** -0.5 * DEEPNORM_BETA)
    return {'x': x, 'w_in': w_in, 'w_out': w_out, 'da_lambda': da_lambda, 'da_subln': da_subln,
            'sc_conv': sc_conv, 'rw_mu': rw_mu, 'rw_vecs': rw_vecs, 'rw_w_up': rw_w_up,
            'rw_a_up': rw_a_up, 'rw_g_up': rw_g_up, 'ln_gain': ln_gain, 'ln_bias': ln_bias,
            'rel_bias': rel_bias, 'router_w': router_w, 'router_b': router_b,
            'moe_w_in': moe_w_in, 'moe_w_down': moe_w_down}

def reference(x, w_in, w_out, da_lambda, da_subln, sc_conv, rw_mu, rw_vecs, rw_w_up,
              rw_a_up, rw_g_up, ln_gain, ln_bias, rel_bias, router_w, router_b,
              moe_w_in, moe_w_down):
    bias_dist = relative_bias_by_distance(rel_bias, x.shape[1])
    for l in range(DEPTH):
        proj = x @ w_in[l]
        p_sb, p_da, p_sc, p_rw = jnp.split(proj, IN_SPLITS, axis=-1)
        q, k, v = jnp.split(p_sb, 3, axis=-1)
        y_sb = stick_breaking_attention(q, k, v).astype(x.dtype)
        q, k, v = jnp.split(p_da, 3, axis=-1)
        lam_init = 0.8 - 0.6 * math.exp(-0.3 * l)
        y_da = diff_attention(q, k, v, da_lambda[l], da_subln[l], bias_dist, lam_init).astype(x.dtype)
        b_gate, c_gate, h = jnp.split(p_sc, 3, axis=-1)
        y_sc = short_conv_mixer(b_gate, c_gate, h, sc_conv[l]).astype(x.dtype)
        y_rw = rwkv7_time_mix(p_rw, rw_mu[l], rw_vecs[l], rw_w_up[l], rw_a_up[l], rw_g_up[l]).astype(x.dtype)
        mixed = jnp.concatenate([y_sb, y_da, y_sc, y_rw], axis=-1) @ w_out[l]
        x = layer_norm(DEEPNORM_ALPHA * x + mixed, ln_gain[l, 0], ln_bias[l, 0])
        ffn = grouped_moe(x, router_w, router_b, moe_w_in[l], moe_w_down[l])
        x = layer_norm(DEEPNORM_ALPHA * x + ffn, ln_gain[l, 1], ln_bias[l, 1])
    return x


_drawn_inputs = setup_inputs


def setup_inputs(seed=0):
    import zlib

    import numpy as np

    out = dict(_drawn_inputs(seed))
    spreads = {}
    factors = {'da_subln': 3.9, 'rw_w_up': 16.926, 'rw_a_up': 3.197}
    for name, (base, spread) in spreads.items():
        noise = np.random.default_rng([zlib.crc32(name.encode()), seed]).standard_normal(out[name].shape)
        drawn = base * np.exp(spread * noise) if base else spread * noise
        out[name] = jnp.asarray(drawn.astype(out[name].dtype))
    for name, factor in factors.items():
        out[name] = (out[name] * factor).astype(out[name].dtype)
    return out
```

```python
import math
from contextlib import ExitStack

import numpy as np
import concourse.bass as bass
from concourse import mybir

F32 = mybir.dt.float32
I32 = mybir.dt.int32
ALU = mybir.AluOpType
ACT = mybir.ActivationFunctionType
AX = mybir.AxisListType

D, T, P = 1024, 1024, 128
KD = D // P
NT = T // P
GW = 256
HD = 64
RW_COLS = 3 * GW + 128
P_IN = 9 * GW + RW_COLS
NE, FE = 16, 256
EPG = 4
ALPHA = 2 ** 0.25
LAM_INIT = 0.8 - 0.6
DECAY = math.exp(-0.5)
NEG = -1e30
BLOCKS = NE + (2 * T - NE) // P
NBP = 32
SB0, DA0, SC0, RW0 = 0, 3 * GW, 6 * GW, 9 * GW
BUCKETS, MAX_DIST = 32, 128
LT5 = T + P

IDENT, SU, UI, SL, ONES, BO, BM, M1, M1T, MB, NEGD, SCANM, NCST = 0, 1, 2, 3, 4, 5, 6, 7, 8, 9, 15, 16, 17


def constants():
    r = np.arange(P)
    row, col = r[:, None], r[None, :]
    c = np.zeros((P, NCST, P), np.float32)
    c[:, IDENT] = row == col
    c[:, SU] = row < col
    c[:, UI] = row <= col
    c[:, SL] = row > col
    c[:, ONES] = 1
    c[:, BO] = row // HD == col // HD
    c[:, BM] = (row // HD == col // HD) / HD

    def level(b):
        return (row // (2 * b) == col // (2 * b)) & (row // b % 2 == 1) & (col // b % 2 == 0)
    c[:, M1] = level(1)
    c[:, M1T] = level(1).T
    for n in range(6):
        c[:, MB + n] = level(2 << n)
    c[:, NEGD] = np.where(row > col, 0.0, NEG)
    c[:, SCANM] = np.broadcast_to(col != 0, (P, P))
    d = T - 1 - np.arange(LT5)
    n = np.maximum(d, 0)
    nf = np.maximum(n, 1).astype(np.float32)
    big = 16 + (np.log(nf / np.float32(16)) / np.float32(math.log(MAX_DIST / 16)) * np.float32(16)).astype(np.int32)
    bucket = np.where(n < 16, n, np.minimum(big, BUCKETS - 1))
    hot = np.zeros((BUCKETS + 1, LT5), np.float32)
    hot[bucket[d >= 0], np.nonzero(d >= 0)[0]] = 1
    hot[BUCKETS, d < 0] = NEG
    s = np.zeros((P, 64), np.float32)
    s[:, 0:NBP] = np.arange(NBP)
    s[0:32, 32] = -2.0
    s[32:, 32] = -1.0
    s[:, 33], s[:, 34], s[:, 35] = 64e-5, 1e-5, 1.0
    tok = (np.arange(NT)[None, :] * P + r[:, None]).astype(np.int32)
    return {"c_mats": c.reshape(P, NCST * P), "c_hot": hot, "c_small": s, "c_tok": tok}


def layer_kernel(nc, x, w_in, w_out, da_lambda, da_subln, sc_conv, rw_mu, rw_vecs, rw_w_up, rw_a_up, rw_g_up,
                 ln_gain, ln_bias, rel_bias, router_w, router_b, moe_w_in, moe_w_down,
                 c_mats, c_hot, c_small, c_tok, out):
    ctx = ExitStack()
    with ctx:
        ctx.enter_context(nc.allow_non_contiguous_dma("small parameter columns"))

        def sb(name, shape, dt=F32):
            return ctx.enter_context(nc.sbuf_tensor(name, shape, dt))

        def sem(name):
            return ctx.enter_context(nc.semaphore(name))

        bias_d = nc.dram_tensor("bias_d", [4, P * LT5], F32)
        x1_d = nc.dram_tensor("x1_d", [T, D], F32)
        y_d = nc.dram_tensor("y_d", [BLOCKS * P, D], F32)
        slot_d = nc.dram_tensor("slot_d", [NBP * P, 1], I32)

        cst = sb("cst", [P, NCST, P])
        small = sb("small", [P, 64])
        tok = sb("tok", [P, NT], I32)
        mu = sb("mu", [P, 7])
        vecs = sb("vecs", [P, 7, 2])
        conv = sb("conv", [P, 3, 2])
        subg = sb("subg", [P, 1])
        relb = sb("relb", [BUCKETS, 4])
        lp = sb("lp", [P, 4, 32])
        lam = sb("lam", [P, 8])
        low_up = sb("low_up", [P, GW])
        rwr = sb("rwr", [P, KD, NE])
        rbias = sb("rbias", [P, NE])
        dfac = sb("dfac", [P, 2, NT])
        smid = sb("smid", [P, 2, NT])
        stat = sb("stat", [P, 64])
        mixT = sb("mixT", [P, 8, T])
        qk = sb("qk", [P, 8, T])
        vt = sb("vt", [P, NT, 2 * GW])
        mid = sb("mid", [P, 6 * T + 7 * (T + 1)])
        sc = mid[:, 0:6 * T].rearrange("p (j t) -> p j t", j=6)
        rw = mid[:, 6 * T:].rearrange("p (j t) -> p j t", j=7)
        arena = sb("arena", [P, 16 * 1024])

        def region(at, *dims):
            n = 1
            for d in dims:
                n *= d
            v = arena[:, at:at + n]
            if len(dims) == 2:
                return v.rearrange("p (a b) -> p a b", a=dims[0])
            if len(dims) == 3:
                return v.rearrange("p (a b c) -> p a b c", a=dims[0], b=dims[1])
            return v

        def C(i):
            return cst[:, i, :]

        pz = [ctx.enter_context(nc.psum_tensor(f"pz{i}", [P, 1024], F32)) for i in range(2)]
        pb = [ctx.enter_context(nc.psum_tensor(f"pb{i}", [P, 512], F32)) for i in range(4)]
        bank = [pz[0][:, 0:512], pz[0][:, 512:1024], pz[1][:, 0:512], pz[1][:, 512:1024]] + [b[:, :] for b in pb]

        names = """kk_scale ln_done rw_rstd da_rstd var_ready row_rstd mats_in consts zeroed x_turned xT_ready fill_done fill_evac mix_diff mixed low_exp low_ready aux_done aux_evac
            aux_devac conv_u conv_done sq_ready decay_ready decays bonus_ready rwe_done
            bias_up bias_rows bias_evac bias_st bias_sb
            x_init rw_init mean_done centred squared var_done rw_out
            sb_z sb_soft sb_logw sb_w sb_t sb_wT sb_o sb_evac
            da_z da_logit da_exp da_attn da_t da_wT da_o da_evac da_sq da_ms da_done lam_prod lam_exp
            wout_in op_done op_sum x1_ready x1_st x1_t x1_tev rl_done rl_ev route_exp route_sel cnt_done
            slot_zero slot_sc slot_in gather up_done exp_g gated h_t h_tev down_done y_ev xg_t xg_tev
            fin_ready out_st gb_in ids_ready vchain achain pchain""".split()
        S = {n: sem(n) for n in names}
        x_in = [sem(f"x_in{i}") for i in range(2)]
        w_arr = [sem(f"w_arr{i}") for i in range(4)]
        wv_in = sem("wv_in")
        rw_fill = [sem(f"rw_fill{h}") for h in range(2)]
        rw_evac = [sem(f"rw_evac{h}") for h in range(2)]
        t5_in = sem("t5_in")
        xr_in = [sem(f"xr_in{i}") for i in range(2)]
        we_in = [sem(f"we_in{i}") for i in range(2)]
        xg_in = [sem(f"xg_in{i}") for i in range(2)]
        y_st = [sem(f"y_st{i}") for i in range(2)]
        yg_in = [sem(f"yg_in{i}") for i in range(2)]

        block = ctx.enter_context(nc.Block())

        xT = region(0, KD, T)
        wring = region(8192, 4, KD, P)
        xs = region(12288, 2, T)
        wv = region(12288, KD, 512)
        tiles = []
        for s, c in ((6, 768), (2, 256), (3, 384), (0, 0), (1, 128), (4, 512), (5, 640)):
            tiles.append((RW0 + c, rw[:, s, 1:T + 1], 1.0))
        for s in range(6):
            tiles.append((SC0 + s * P, sc[:, s, :], 1.0))
        for s in range(4):
            tiles.append((SB0 + s * P, qk[:, s, :], HD ** -0.5 if s < 2 else 1.0))
        for s in range(4):
            tiles.append((DA0 + s * P, qk[:, 4 + s, :], 32 ** -0.5 if s < 2 else 1.0))
        NTILE, V_AT = len(tiles), 13
        NFILL = 2 * NTILE + NT
        rw_order = [6, 2, 3, 0, 1, 4, 5]

        def fill_of(t):
            return 2 * t + (NT if t >= V_AT else 0)

        fills = []
        for t in range(NTILE):
            if t == V_AT:
                fills += [("v", i, 0) for i in range(NT)]
            fills += [("f", t, 0), ("f", t, 1)]
        M01, M23, M67 = mixT[:, 0:2, :], mixT[:, 2:4, :], mixT[:, 6:8, :]
        S1, S2, S3 = sc[:, 0:2, :], sc[:, 2:4, :], sc[:, 4:6, :]
        D1, D2 = qk[:, 4:6, :], qk[:, 6:8, :]
        rR, rK, rV = rw[:, 0:2, 1:T + 1], rw[:, 2:4, 1:T + 1], rw[:, 4:6, 1:T + 1]
        brows = qk[:, :, :].rearrange("p j t -> p (j t)")[:, 0:LT5]
        hot = qk[:, :, :].rearrange("p j t -> p (j t)")[0:BUCKETS + 1, 2 * T:2 * T + LT5]
        bias_l = qk[0:BUCKETS + 1, 4, 0:512].rearrange("p (h c) -> p h c", h=4)
        NCONST = 17

        NF = [33, 29]
        mats = ["LT", "X", "RbT", "AkT", "RkT", "XT", "W", "U"]
        chb = [{n: region((h * 8 + i) * 512, 4, P) for i, n in enumerate(mats)} for h in range(2)]
        for h in range(2):
            chb[h]["AkV"] = region(8192 + h * 256, 4, HD)
            chb[h]["RP"] = region(8704 + h * 512, 4, P)
            chb[h]["NG"] = region(9728 + h * 512, 4, P)
        tm = {n: region(10752 + i * 512, 4, P) for i, n in enumerate("abkv")}
        YT = region(12800, 2, T)
        st = region(14848, 2, NT + 1, HD)
        PT = region(0, 2, T)
        PT2 = region(2048, 2, T)

        sbE = [region(i * 1024, T) for i in range(2)]
        sbS = [region(2048 + i * 1024, T) for i in range(2)]
        sbW = [region(4096 + i * 1024, T) for i in range(2)]
        sbT = [region(6144 + i * 1024, NT, P) for i in range(2)]
        lg = [[region((2 * i + m) * 1024, T) for m in range(2)] for i in range(2)]
        daT = [region(4096 + i * 1024, NT, P) for i in range(2)]
        ODA = region(8192, 2, T)
        t5 = region(12288, 4, T)
        items = [(i, hh) for i in range(NT) for hh in range(4)]
        wout = mid[:, 0:8192].rearrange("p (k n) -> p k n", k=KD)
        x1 = region(0, NT, T)
        gb = region(8192, 4, T)
        xr = qk[:, 0:2, :]
        x1T = qk[:, 2, :].rearrange("p (k t) -> p k t", k=KD)
        rl = qk[:, 3, 0:128].rearrange("p (i e) -> p i e", i=NT)
        rt = qk[:, 4, :]
        rt2 = qk[:, 5, :]
        we = [mid[:, i * 6144:(i + 1) * 6144] for i in range(2)]
        weu = [w[:, 0:4096].rearrange("p (k n) -> p k n", k=KD) for w in we]
        wed = [w[:, 4096:6144].rearrange("p (k n) -> p k n", k=2) for w in we]
        xg = [mixT[:, i, :] for i in range(2)]
        xgT = [mixT[:, 2 + i, :].rearrange("p (k t) -> p k t", k=KD) for i in range(2)]
        yb = [mixT[:, 4 + i, :] for i in range(2)]
        hb = [mixT[:, 6, i * 512:i * 512 + 256] for i in range(2)]
        eb = [mixT[:, 6, i * 512 + 256:i * 512 + 512] for i in range(2)]
        hTb = [mixT[:, 7, i * 256:(i + 1) * 256].rearrange("p (k t) -> p k t", k=2) for i in range(2)]
        slots = sb("slots", [P, 2, NT], I32)
        gates = sb("gates", [P, 2, NT])
        ids = sb("ids", [P, NBP], I32)
        slot_tok = sb("slot_tok", [P, NBP], I32)

        @block.sync
        def _(sp):
            const = S["consts"]
            sp.dma_start(cst[:, :, :], c_mats.rearrange("p (i c) -> p i c", c=P)).then_inc(S["mats_in"], 16)

            def load_w(t):
                if t >= 4:
                    sp.wait_ge(S["fill_done"], fill_of(t - 4) + 2)
                c0 = tiles[t][0]
                sp.dma_start(wring[:, t % 4], w_in[0, :, c0:c0 + P].rearrange("(k p) c -> p k c", p=P)).then_inc(w_arr[t % 4], 16)

            for i in range(NT):
                if i >= 2:
                    sp.wait_ge(S["x_turned"], 2 * (i - 1))
                sp.dma_start(xs[:, i % 2], x[0, i * P:(i + 1) * P, :]).then_inc(x_in[i % 2], 16)
                if i < 4:
                    load_w(i)
            sp.dma_start(small[:, :], c_small).then_inc(const, 16)
            sp.dma_start(tok[:, :], c_tok).then_inc(const, 16)
            sp.dma_start(mu[:, :], rw_mu.rearrange("o (j p) -> p (o j)", p=P)).then_inc(const, 16)
            sp.dma_start(hot, c_hot).then_inc(const, 16)
            sp.dma_start(relb[:, :], rel_bias).then_inc(const, 16)
            sp.dma_start(lp[:, :, :], da_lambda[0].rearrange("a b -> (a b)").partition_broadcast(P).rearrange("p (a b) -> p a b", a=4)).then_inc(S["consts"], 16)
            sp.dma_start(rbias[:, :], router_b.partition_broadcast(P)).then_inc(S["consts"], 16)
            sp.dma_start(vecs[:, :, 0], rw_vecs[0, :, 0:P].rearrange("v p -> p v")).then_inc(const, 16)
            sp.dma_start(vecs[:, :, 1], rw_vecs[0, :, P:GW].rearrange("v p -> p v")).then_inc(const, 16)
            sp.dma_start(low_up[0:32, :], rw_w_up[0]).then_inc(const, 16)
            sp.dma_start(low_up[32:64, :], rw_a_up[0]).then_inc(const, 16)
            sp.dma_start(low_up[64:128, :], rw_g_up[0]).then_inc(const, 16)
            sp.dma_start(conv[:, :, 0], sc_conv[0, :, 0:P].rearrange("v p -> p v")).then_inc(const, 16)
            sp.dma_start(conv[:, :, 1], sc_conv[0, :, P:GW].rearrange("v p -> p v")).then_inc(const, 16)
            sp.dma_start(rwr[:, :, :], router_w.rearrange("(k p) e -> p k e", p=P)).then_inc(const, 16)
            for h in range(2):
                sp.dma_start(subg[HD * h:HD * h + HD, :], da_subln.rearrange("o p -> p o")).then_inc(const, 16)
            sp.wait_ge(S["x_turned"], 16)
            sp.dma_start(wv[:, :, 0:GW], w_in[0, :, SB0 + 2 * GW:SB0 + 3 * GW].rearrange("(k p) c -> p k c", p=P)).then_inc(wv_in, 16)
            sp.dma_start(wv[:, :, GW:], w_in[0, :, DA0 + 2 * GW:DA0 + 3 * GW].rearrange("(k p) c -> p k c", p=P)).then_inc(wv_in, 16)
            for t in range(4, NTILE):
                load_w(t)
            sp.wait_ge(S["rw_out"], 1)
            sp.wait_ge(S["bias_st"], 16)
            for h in range(4):
                src = bass.AP(bias_d, h * P * LT5 + P - 1, [[LT5 - 1, P], [1, T]])
                sp.dma_start(t5[:, h, :], src).then_inc(t5_in, 16)
            sp.dma_start(wout, w_out[0].rearrange("(k p) n -> p k n", p=P)).then_inc(S["wout_in"], 16)
            sp.wait_ge(S["da_o"], len(items))
            sp.wait_ge(S["da_done"], 1)
            for n, g in enumerate((ln_gain, ln_bias)):
                for l in range(2):
                    sp.dma_start(gb[:, 2 * l + n, :], g[0, l, :].partition_broadcast(P)).then_inc(S["gb_in"], 16)
            for i in range(NT):
                if i >= 2:
                    sp.wait_ge(S["op_sum"], i - 1)
                sp.dma_start(xr[:, i % 2], x[0, i * P:(i + 1) * P, :]).then_inc(xr_in[i % 2], 16)
                if i >= 1:
                    sp.wait_ge(S["x1_ready"], i)
                    sp.dma_start(x1_d[(i - 1) * P:i * P, :], x1[:, i - 1, :]).then_inc(S["x1_st"], 16)
            sp.wait_ge(S["x1_ready"], NT)
            sp.dma_start(x1_d[(NT - 1) * P:, :], x1[:, NT - 1, :]).then_inc(S["x1_st"], 16)
            sp.wait_ge(S["ids_ready"], 1)
            for b in range(BLOCKS):
                if b >= 2:
                    sp.wait_ge(S["down_done"], b - 1)
                e = sp.value_load(ids[0:1, b:b + 1], min_val=0, max_val=NE - 1)
                sp.dma_start(weu[b % 2], moe_w_in[0, bass.ds(e, 1), :, :].rearrange("o (k p) n -> p (o k) n", p=P)).then_inc(we_in[b % 2], 16)
                sp.dma_start(wed[b % 2], moe_w_down[0, bass.ds(e, 1), :, :].rearrange("o (k p) n -> p (o k) n", p=P)).then_inc(we_in[b % 2], 16)
                if b >= 2:
                    sp.wait_ge(S["y_ev"], 2 * (b - 1))
                    sp.dma_start(y_d[(b - 2) * P:(b - 1) * P, :], yb[b % 2]).then_inc(y_st[b % 2], 16)
            for b in (BLOCKS - 2, BLOCKS - 1):
                sp.wait_ge(S["y_ev"], 2 * (b + 1))
                sp.dma_start(y_d[b * P:(b + 1) * P, :], yb[b % 2]).then_inc(y_st[b % 2], 16)
            for i in range(NT):
                sp.wait_ge(S["fin_ready"], i + 1)
                sp.dma_start(out[0, i * P:(i + 1) * P, :], x1[:, i, :]).then_inc(S["out_st"], 16)
            sp.wait_ge(S["out_st"], 16 * NT)

        @block.gpsimd
        def _(pool):
            pool.memset(rw[:, :, 0:1], 0.0)
            pool.memset(ids[:, :], 0).then_inc(S["zeroed"], 1)
            pool.wait_ge(S["zeroed"], 1)
            pool.dma_start(slot_d[:, :].rearrange("(b p) o -> p (b o)", p=P), ids[:, :]).then_inc(S["slot_zero"], 16)
            for m, s in enumerate(rw_order):
                pool.wait_ge(S["fill_evac"], 2 * (m + 1))
                if m >= 4:
                    pool.wait_ge(S["mixed"], m - 3)
                pool.tensor_tensor(mixT[:, m % 4, :], rw[:, s, 0:T], rw[:, s, 1:T + 1], ALU.subtract).then_inc(S["mix_diff"], 1)
            pool.wait_ge(S["fill_evac"], 26)
            for j in range(2):
                pool.tensor_tensor(sc[:, 2 + j, :], sc[:, 2 + j, :], sc[:, 4 + j, :], ALU.mult).then_inc(S["conv_u"], 1)
            for m in range(NT // 2):
                for h in range(2):
                    g = m * NF[h] + (4 if h == 0 else 0)
                    pool.wait_ge(rw_evac[h], g + 2)
                    b = chb[h]
                    idb = C(IDENT).unsqueeze(1).to_broadcast([P, 4, P])
                    pool.tensor_tensor(b["X"], b["X"], idb, ALU.add)
                    pool.tensor_tensor(b["XT"], b["LT"], C(M1T).unsqueeze(1).to_broadcast([P, 4, P]), ALU.mult).then_inc(S["pchain"], 1)
                    pool.wait_ge(S["pchain"], 2 * m + h + 1)
                    pool.tensor_tensor(b["XT"], b["XT"], idb, ALU.add).then_inc(S["rw_init"], 1)
            pool.wait_ge(S["ids_ready"], 1)
            pool.wait_ge(S["slot_zero"], 16)
            for i in range(NT):
                for s in range(2):
                    pool.indirect_dma_start(slot_d[:, :], bass.IndirectOffsetOnAxis(ap=slots[:, s, i:i + 1], axis=0),
                                            tok[:, i:i + 1], None).then_inc(S["slot_sc"], 16)
            pool.wait_ge(S["slot_sc"], 16 * 2 * NT)
            pool.dma_start(slot_tok[:, :], slot_d[:, :].rearrange("(b p) o -> p (b o)", p=P)).then_inc(S["slot_in"], 16)
            pool.wait_ge(S["slot_in"], 16)
            pool.wait_ge(S["x1_st"], 16 * NT)
            for b in range(BLOCKS):
                if b >= 2:
                    pool.wait_ge(S["xg_t"], b - 1)
                pool.indirect_dma_start(xg[b % 2], None, x1_d[:, :],
                                        bass.IndirectOffsetOnAxis(ap=slot_tok[:, b:b + 1], axis=0)).then_inc(xg_in[b % 2], 16)
            nst = [(BLOCKS + 1) // 2, BLOCKS // 2]
            for i in range(2):
                pool.wait_ge(y_st[i], 16 * nst[i])
            for i in range(NT):
                if i >= 2:
                    pool.wait_ge(S["fin_ready"], i - 1)
                for s in range(2):
                    pool.indirect_dma_start(mixT[:, 2 * (i % 2) + s, :], None, y_d[:, :],
                                            bass.IndirectOffsetOnAxis(ap=slots[:, s, i:i + 1], axis=0)).then_inc(yg_in[i % 2], 16)

        @block.scalar
        def _(act):
            A = nc.scalar.activation
            act.wait_ge(S["consts"], 16 * NCONST)
            act.wait_ge(S["lam_prod"], 1)
            A(lam[:, 2:4], lam[:, 0:2], ACT.Exp).then_inc(S["lam_exp"], 1)

            def evac(n):
                kind, t, half = fills[n]
                act.wait_ge(S["fill_done"], n + 1)
                src = bank[4 + n % 4]
                if kind == "v":
                    A(vt[:, t, :], src, ACT.Copy).then_inc(S["fill_evac"], 1)
                else:
                    if t == V_AT and half == 0:
                        act.wait_ge(S["bias_st"], 64)
                    if n == NFILL - 8:
                        act.wait_ge(S["rwe_done"], 1)
                    A(tiles[t][1][:, half * 512:(half + 1) * 512], src, ACT.Copy, scale=tiles[t][2]).then_inc(S["fill_evac"], 1)

            for n in range(NFILL):
                evac(n)
                if n == 3:
                    for h in range(4):
                        for c in range(3):
                            q = 3 * h + c
                            act.wait_ge(S["bias_rows"], q + 1)
                            if q in (3, 6, 9):
                                act.wait_ge(S["bias_st"], 16 * (q // 3))
                            A(brows[:, c * 384:(c + 1) * 384], bank[c][:, 0:384], ACT.Copy).then_inc(S["bias_evac"], 1)
                        act.wait_ge(S["bias_evac"], 3 * (h + 1))
                        act.dma_start(bias_d[h, :].rearrange("(p m) -> p m", p=P), brows).then_inc(S["bias_st"], 16)
                if n == 15:
                    act.wait_ge(S["mixed"], 1)
                    A(rw[0:32, 6, 1:T + 1], rw[0:32, 6, 1:T + 1], ACT.Exp, scale=-2.0)
                    A(rw[64:128, 6, 1:T + 1], rw[64:128, 6, 1:T + 1], ACT.Exp, scale=-1.0).then_inc(S["low_exp"], 1)
                if n == 18:
                    act.wait_ge(S["mixed"], 7)
                    for a in range(12):
                        what, j, half = a // 4, a // 2 % 2, a % 2
                        act.wait_ge(S["aux_done"], a + 1)
                        dst = (M01, M23, M67)[what][:, j, half * 512:(half + 1) * 512]
                        if what < 2:
                            A(dst, bank[a % 4], ACT.Exp, bias=stat[:, 2 * what + j:2 * what + j + 1], scale=-1.0).then_inc(S["aux_evac"], 1)
                        else:
                            A(dst, bank[a % 4], ACT.Copy).then_inc(S["aux_evac"], 1)
                if n == 29:
                    act.wait_ge(S["aux_devac"], 4)
                    A(S2, S2, ACT.Ln).then_inc(S["ln_done"], 1)
                    act.wait_ge(S["ln_done"], 1)
                    A(S2, S2, ACT.Exp, scale=-0.5).then_inc(S["kk_scale"], 1)
                if n == 28:
                    act.wait_ge(S["decay_ready"], 1)
                    A(D2, D1, ACT.Exp, scale=DECAY)
                    A(M01, M01, ACT.Exp, scale=-DECAY)
                    A(dfac[:, :, :], dfac[:, :, :], ACT.Exp, scale=-DECAY).then_inc(S["achain"], 1)
                    act.wait_ge(S["achain"], 1)
                    A(D1, D1, ACT.Exp, scale=-DECAY).then_inc(S["decays"], 1)
            for q in range(4):
                j, half = q // 2, q % 2
                act.wait_ge(S["centred"], q + 1)
                A(PT[:, j, half * 512:(half + 1) * 512], YT[:, j, half * 512:(half + 1) * 512], ACT.Square).then_inc(S["squared"], 1)

            for q in range(4):
                j, half = q // 2, q % 2
                act.wait_ge(S["var_done"], q + 1)
                a = A(PT2[:, j, half * 512:(half + 1) * 512], bank[4 + q], ACT.Ln, bias=small[:, 33:34])
            a.then_inc(S["ln_done"], 1)
            act.wait_ge(S["ln_done"], 2)
            A(PT2, PT2, ACT.Exp, scale=-0.5).then_inc(S["rw_rstd"], 1)

            act.wait_ge(S["rw_out"], 1)

            def sb_soft(it):
                i, hh = items[it]
                n, p = (i + 1) * P, it % 2
                act.wait_ge(S["sb_z"], it + 1)
                if it >= 2:
                    act.wait_ge(S["sb_logw"], it - 1)
                A(sbE[p][:, 0:n], pz[p][:, 0:n], ACT.Abs).then_inc(S["achain"], 1)
                act.wait_ge(S["achain"], 2 * it + 2)
                A(sbE[p][:, 0:n], sbE[p][:, 0:n], ACT.Exp, scale=-1.0).then_inc(S["achain"], 1)
                act.wait_ge(S["achain"], 2 * it + 3)
                A(sbE[p][:, 0:n], sbE[p][:, 0:n], ACT.Ln, bias=1.0).then_inc(S["sb_soft"], 1)

            def sb_exp(it):
                n, p = (items[it][0] + 1) * P, it % 2
                act.wait_ge(S["sb_logw"], it + 1)
                A(sbW[p][:, 0:n], sbW[p][:, 0:n], ACT.Exp).then_inc(S["sb_w"], 1)

            def sb_turn(it):
                n, p = (items[it][0] + 1) * P, it % 2
                act.wait_ge(S["sb_t"], it + 1)
                if it >= 2:
                    act.wait_ge(S["sb_o"], it - 1)
                for c in range(0, n, 512):
                    e = min(n, c + 512)
                    a = A(sbT[p][:, c // P:e // P, :], bank[4 + c // 512][:, 0:e - c].rearrange("p (k t) -> p k t", t=P), ACT.Copy)
                a.then_inc(S["sb_wT"], 1)

            sb_soft(0)
            for it in range(len(items)):
                if it + 1 < len(items):
                    sb_soft(it + 1)
                sb_exp(it)
                sb_turn(it)

            def da_exp(it):
                n, p = (items[it][0] + 1) * P, it % 2
                act.wait_ge(S["da_logit"], it + 1)
                for m in range(2):
                    a = A(lg[p][m][:, 0:n], lg[p][m][:, 0:n], ACT.Exp, bias=stat[:, 16 + 4 * p + m:17 + 4 * p + m],
                          accum_out=stat[:, 18 + 4 * p + m:19 + 4 * p + m])
                a.then_inc(S["da_exp"], 1)

            def da_turn(it):
                n, p = (items[it][0] + 1) * P, it % 2
                act.wait_ge(S["da_t"], it + 1)
                if it >= 2:
                    act.wait_ge(S["da_o"], it - 1)
                for c in range(0, n, 512):
                    e = min(n, c + 512)
                    a = A(daT[p][:, c // P:e // P, :], bank[4 + c // 512][:, 0:e - c].rearrange("p (k t) -> p k t", t=P), ACT.Copy)
                a.then_inc(S["da_wT"], 1)

            act.wait_ge(S["sb_evac"], len(items))
            da_exp(0)
            for it in range(len(items)):
                if it + 1 < len(items):
                    da_exp(it + 1)
                da_turn(it)
            act.wait_ge(S["da_evac"], len(items))
            A(PT[:, :, :], ODA, ACT.Square).then_inc(S["da_sq"], 1)
            for q in range(4):
                j, half = q // 2, q % 2
                act.wait_ge(S["da_ms"], q + 1)
                a = A(PT2[:, j, half * 512:(half + 1) * 512], bank[q], ACT.Ln, bias=small[:, 34:35])
            a.then_inc(S["ln_done"], 1)
            act.wait_ge(S["ln_done"], 3)
            A(PT2, PT2, ACT.Exp, scale=-0.5).then_inc(S["da_rstd"], 1)

            def row_scale(n):
                act.wait_ge(S["var_ready"], n + 1)
                A(stat[:, 14:15], stat[:, 13:14], ACT.Ln, bias=small[:, 34:35]).then_inc(S["ln_done"], 1)
                act.wait_ge(S["ln_done"], n + 4)
                A(stat[:, 14:15], stat[:, 14:15], ACT.Exp, scale=-0.5).then_inc(S["row_rstd"], 1)

            row_scale(0)
            for i in range(NT):
                if i + 1 < NT:
                    row_scale(i + 1)
                act.wait_ge(S["x1_t"], i + 1)
                if i >= 1:
                    act.wait_ge(S["rl_done"], i)
                for c in range(2):
                    a = A(x1T[:, 4 * c:4 * c + 4, :], bank[4 + c].rearrange("p (k t) -> p k t", t=P), ACT.Copy)
                a.then_inc(S["x1_tev"], 1)
                act.wait_ge(S["rl_done"], i + 1)
                A(rl[:, i, :], bank[6][:, 0:NE], ACT.Exp, scale=-1.0).then_inc(S["rl_ev"], 1)

            def xg_copy(b):
                act.wait_ge(S["xg_t"], b + 1)
                if b >= 2:
                    act.wait_ge(S["up_done"], b - 1)
                for c in range(2):
                    a = A(xgT[b % 2][:, 4 * c:4 * c + 4, :], bank[c].rearrange("p (k t) -> p k t", t=P), ACT.Copy)
                a.then_inc(S["xg_tev"], 1)

            def gate_exp(b):
                act.wait_ge(S["up_done"], b + 1)
                A(eb[b % 2], bank[4 + b % 2][:, 0:FE], ACT.Exp, scale=-1.0).then_inc(S["exp_g"], 1)

            act.wait_ge(S["ids_ready"], 1)
            xg_copy(0)
            for b in range(BLOCKS):
                gate_exp(b)
                if b + 1 < BLOCKS:
                    xg_copy(b + 1)
                act.wait_ge(S["h_t"], b + 1)
                A(hTb[b % 2], bank[6][:, 0:FE].rearrange("p (k t) -> p k t", t=P), ACT.Copy).then_inc(S["h_tev"], 1)
                act.wait_ge(S["down_done"], b + 1)
                if b >= 2:
                    act.wait_ge(y_st[b % 2], 16 * (b // 2))
                A(yb[b % 2][:, 0:512], bank[2], ACT.Copy).then_inc(S["y_ev"], 1)
            for i in range(NT):
                row_scale(NT + i)

        @block.vector
        def _(v):
            V = nc.vector
            chain = [0]

            def link(ins):
                chain[0] += 1
                ins.then_inc(S["vchain"], 1)
                v.wait_ge(S["vchain"], chain[0])

            TT, TS, STT = V.tensor_tensor, V.tensor_scalar, V.scalar_tensor_tensor

            def sigmoid(a):
                link(TS(a, a, 1.0, None, ALU.add))
                return V.reciprocal(a, a)

            for n in range(16):
                i, c = n // 2, n % 2
                v.wait_ge(S["x_turned"], n + 1)
                V.tensor_copy(xT[:, 4 * c:4 * c + 4, i * P:(i + 1) * P], bank[n % 4].rearrange("p (k t) -> p k t", t=P)).then_inc(S["xT_ready"], 1)
            v.wait_ge(S["consts"], 16 * NCONST)
            link(V.memset(bias_l, 1.0))
            V.tensor_copy(bias_l[0:BUCKETS], relb[:, :].unsqueeze(2).to_broadcast([BUCKETS, 4, P])).then_inc(S["bias_up"], 1)
            link(TT(lp[:, 0:3:2, :], lp[:, 0:3:2, :], lp[:, 1:4:2, :], ALU.mult))
            V.tensor_reduce(lam[:, 0:2], lp[:, 0:3:2, :], AX.X, ALU.add).then_inc(S["lam_prod"], 1)
            v.wait_ge(S["lam_exp"], 1)
            link(TT(lam[:, 4:5], lam[:, 3:4], lam[:, 2:3], ALU.subtract))
            link(TS(lam[:, 4:5], lam[:, 4:5], -LAM_INIT, None, ALU.add))
            for w in range(2):
                TS(stat[:, 2 * w:2 * w + 2], vecs[:, w, :], -1.0, None, ALU.mult)
            link(TS(stat[:, 4:6], vecs[:, 3, :], -1.0, 1.0, ALU.mult, ALU.add))
            link(TS(subg[:, :], subg[:, :], 1.0 - LAM_INIT, None, ALU.mult))
            for m, s in enumerate(rw_order):
                v.wait_ge(S["mix_diff"], m + 1)
                STT(rw[:, s, 1:T + 1], mixT[:, m % 4, :], mu[:, s:s + 1], rw[:, s, 1:T + 1], ALU.mult, ALU.add).then_inc(S["mixed"], 1)
            v.wait_ge(S["low_exp"], 1)
            for lo, hi in ((0, 32), (64, 128)):
                last = sigmoid(rw[lo:hi, 6, 1:T + 1])
            link(last)
            TS(rw[0:32, 6, 1:T + 1], rw[0:32, 6, 1:T + 1], 2.0, -1.0, ALU.mult, ALU.add).then_inc(S["low_ready"], 1)
            v.wait_ge(S["aux_evac"], 4)
            link(sigmoid(M01))
            for j in range(2):
                for n in range(NT):
                    last = V.tensor_tensor_scan(D1[:, j, n * P:(n + 1) * P], C(ONES), M01[:, j, n * P:(n + 1) * P], 0.0, ALU.mult, ALU.add)
            link(last)
            d1c = D1.rearrange("p j (n c) -> p j n c", c=P)
            V.tensor_copy(smid[:, :, :], d1c[:, :, :, HD - 1])
            link(V.tensor_copy(dfac[:, :, :], d1c[:, :, :, P - 1]))
            link(TT(dfac[:, :, :], dfac[:, :, :], smid[:, :, :], ALU.subtract))
            link(TT(dfac[:, :, 0:NT - 1], dfac[:, :, 0:NT - 1], smid[:, :, 1:NT], ALU.add))
            for j in range(2):
                last = TT(D1[:, j, :].rearrange("p (n c) -> p n c", c=P), D1[:, j, :].rearrange("p (n c) -> p n c", c=P),
                          smid[:, j, :].unsqueeze(2).to_broadcast([P, NT, P]), ALU.subtract)
            link(last)
            TT(M01, D1, M01, ALU.subtract).then_inc(S["decay_ready"], 1)
            v.wait_ge(S["aux_evac"], 8)
            sigmoid(M23)
            v.wait_ge(S["conv_u"], 2)
            for j in range(2):
                y, u = mixT[:, 4 + j, :], sc[:, 2 + j, :]
                link(TS(y, u, conv[:, 2, j:j + 1], None, ALU.mult))
                link(STT(y[:, 1:], u[:, 0:T - 1], conv[:, 1, j:j + 1], y[:, 1:], ALU.mult, ALU.add))
                link(STT(y[:, 2:], u[:, 0:T - 2], conv[:, 0, j:j + 1], y[:, 2:], ALU.mult, ALU.add))
                link(TT(y, y, sc[:, j, :], ALU.mult))
            for j in range(2):
                last = TS(S1[:, j, :], rK[:, j, :], vecs[:, 2, j:j + 1], None, ALU.mult)
            link(last)
            TT(S2, S1, S1, ALU.mult).then_inc(S["sq_ready"], 1)
            for q in range(4):
                j, half = q // 2, q % 2
                v.wait_ge(S["aux_done"], 12 + q + 1)
                TS(S2[:, j, half * 512:(half + 1) * 512], bank[q], 1e-24, None, ALU.max).then_inc(S["aux_devac"], 1)
            v.wait_ge(S["kk_scale"], 1)
            link(TT(S1, S1, S2, ALU.mult))
            link(TT(S2, S1, M23, ALU.mult))
            for j in range(2):
                last = TS(M23[:, j, :], M23[:, j, :], vecs[:, 3, j:j + 1], stat[:, 4 + j:5 + j], ALU.mult, ALU.add)
            link(last)
            link(TT(rK, rK, M23, ALU.mult))
            for j in range(2):
                last = STT(S3[:, j, :], rR[:, j, :], vecs[:, 4, j:j + 1], rK[:, j, :], ALU.mult, ALU.mult)
            last.then_inc(S["bonus_ready"], 1)
            v.wait_ge(S["bonus_ready"], 1)
            v.wait_ge(S["decays"], 1)
            TT(S2, S2, D2, ALU.mult)
            TT(rK, rK, D2, ALU.mult)
            TT(rR, rR, D1, ALU.mult)
            for j in range(2):
                last = STT(S1[:, j, :], S1[:, j, :], -1.0, M01[:, j, :], ALU.mult, ALU.mult)
            last.then_inc(S["rwe_done"], 1)
            for q in range(4):
                j, half = q // 2, q % 2
                v.wait_ge(S["aux_done"], 16 + q + 1)
                h_ = slice(half * 512, (half + 1) * 512)
                TT(S3[:, j, h_], bank[q], rV[:, j, h_], ALU.mult).then_inc(S["aux_devac"], 1)

            v.wait_ge(S["fill_done"], NFILL)
            def bc(i):
                return C(i).unsqueeze(1).to_broadcast([P, 4, P])

            def rw_ev(m, h, k):
                g = m * NF[h] + k + (4 if h == 0 else 0)
                b, lo, hi = chb[h], HD * h, HD * h + HD
                src = bank[4 * h + g % 4].rearrange("p (q c) -> p q c", q=4)
                v.wait_ge(rw_fill[h], g + 1)
                done = rw_evac[h]
                if k < 0:
                    V.tensor_copy(tm["abkv"[k + 4]], src).then_inc(done, 1)
                elif k == 0:
                    TT(b["LT"], src, bc(SU), ALU.mult).then_inc(done, 1)
                elif k == 1:
                    TT(b["X"], src, bc(M1), ALU.mult).then_inc(done, 1)
                elif k in (2, 3, 4):
                    TT(b[("RbT", "AkT", "RkT")[k - 2]], src, bc((UI, SU, UI)[k - 2]), ALU.mult).then_inc(done, 1)
                elif k == 5:
                    V.tensor_copy(b["AkV"], src.rearrange("p q c -> p (q c)")[:, 0:4 * HD].rearrange("p (q c) -> p q c", q=4)).then_inc(done, 1)
                elif k < 23:
                    lev, what = (k - 6) // 3, (k - 6) % 3
                    if lev == 5 and what == 1:
                        what = 2
                    if what == 0:
                        TT(b["W"], src, bc(MB + lev), ALU.mult).then_inc(done, 1)
                    elif what == 1:
                        TT(b["X"], b["X"], src, ALU.add).then_inc(done, 1)
                    else:
                        TT(b["XT"], b["XT"], src, ALU.add).then_inc(done, 1)
                elif k == 23:
                    V.tensor_copy(b["U"], src).then_inc(done, 1)
                elif k == 24:
                    for n2 in range(2):
                        c0 = (2 * m + n2) * P
                        last = TT(b["RP"][lo:hi, 2 * n2:2 * n2 + 2, :], src[lo:hi, 2 * n2:2 * n2 + 2, :], rR[lo:hi, :, c0:c0 + P], ALU.add)
                    last.then_inc(done, 1)
                elif k == 25:
                    for n2 in range(2):
                        d = dfac[lo:hi, :, 2 * m + n2:2 * m + n2 + 1].to_broadcast([HD, 2, HD])
                        TT(b["NG"][lo:hi, 2 * n2:2 * n2 + 2, 0:HD], src[lo:hi, 2 * n2:2 * n2 + 2, 0:HD], d, ALU.mult)
                    TT(b["NG"][lo:hi, :, HD:P], src[lo:hi, :, HD:P], C(IDENT)[lo:hi, lo:hi].unsqueeze(1).to_broadcast([HD, 4, HD]), ALU.add).then_inc(done, 1)
                elif k in (26, 27):
                    n2 = k - 26
                    n = 2 * m + n2
                    v.wait_ge(done, g)
                    for j in range(2):
                        last = STT(st[lo:hi, j, n + 1, :], src[lo:hi, j, 0:HD], dfac[lo:hi, j, n:n + 1], b["NG"][lo:hi, 2 * n2 + j, 0:HD], ALU.mult, ALU.add)
                    last.then_inc(done, 1)
                else:
                    for n2 in range(2):
                        c0 = (2 * m + n2) * P
                        last = V.tensor_copy(YT[lo:hi, :, c0:c0 + P], src[lo:hi, 2 * n2:2 * n2 + 2, :])
                    last.then_inc(done, 1)

            link(V.memset(st[:, :, 0, :], 0.0))
            for m in range(NT // 2):
                for k in range(-4, 0):
                    rw_ev(m, 0, k)
                for k in range(29):
                    for h in range(2):
                        if k == 7:
                            v.wait_ge(S["rw_init"], 2 * m + h + 1)
                        rw_ev(m, h, k)
            for h in range(2):
                v.wait_ge(rw_evac[h], NT // 2 * NF[h])
            for q in range(4):
                j, half = q // 2, q % 2
                h_ = slice(half * 512, (half + 1) * 512)
                v.wait_ge(S["mean_done"], q + 1)
                TT(YT[:, j, h_], YT[:, j, h_], bank[q], ALU.subtract).then_inc(S["centred"], 1)
            v.wait_ge(S["rw_rstd"], 1)
            link(TT(YT, YT, PT2, ALU.mult))
            for j in range(2):
                last = TS(YT[:, j, :], YT[:, j, :], vecs[:, 5, j:j + 1], vecs[:, 6, j:j + 1], ALU.mult, ALU.add)
            link(last)
            link(TT(YT, YT, S3, ALU.add))
            TT(M67, YT, M67, ALU.mult).then_inc(S["rw_out"], 1)
            v.wait_ge(S["rw_out"], 1)

            def sb_log(it):
                i, hh = items[it]
                n, p = (i + 1) * P, it % 2
                q0 = i * P
                v.wait_ge(S["sb_soft"], it + 1)
                if it >= 2:
                    v.wait_ge(S["sb_t"], it - 1)
                link(STT(sbS[p][:, 0:n], pz[p][:, 0:n], 0.0, sbE[p][:, 0:n], ALU.max, ALU.add))
                link(TT(sbS[p][:, q0:n], sbS[p][:, q0:n], C(SL), ALU.mult))
                rev = slice(n - 1, None, -1)
                link(V.tensor_tensor_scan(sbE[p][:, rev], cst[:, ONES, 0:1].to_broadcast([P, n]), sbS[p][:, rev], 0.0, ALU.mult, ALU.add))
                if i:
                    TT(sbW[p][:, 0:q0], pz[p][:, 0:q0], sbE[p][:, 0:q0], ALU.subtract)
                link(TT(sbW[p][:, q0:n], pz[p][:, q0:n], sbE[p][:, q0:n], ALU.subtract))
                TT(sbW[p][:, q0:n], sbW[p][:, q0:n], C(NEGD), ALU.add).then_inc(S["sb_logw"], 1)

            def sb_out(it):
                i, hh = items[it]
                h, j = hh % 2, hh // 2
                v.wait_ge(S["sb_o"], it + 1)
                V.tensor_copy(mixT[HD * h:HD * h + HD, j, i * P:(i + 1) * P], bank[6 + h][HD * h:HD * h + HD, 0:P]).then_inc(S["sb_evac"], 1)

            for it in range(len(items)):
                sb_log(it)
                if it >= 2:
                    sb_out(it - 2)
            sb_out(len(items) - 2)
            sb_out(len(items) - 1)

            v.wait_ge(t5_in, 64)

            def da_logits(it):
                i, hh = items[it]
                n, p = (i + 1) * P, it % 2
                v.wait_ge(S["da_z"], it + 1)
                if it >= 2:
                    v.wait_ge(S["da_t"], it - 1)
                for m in range(2):
                    last = V.tensor_tensor_reduce(out=lg[p][m][:, 0:n], in0=pz[m][:, 0:n], in1=t5[:, hh, T - n:T], scale=1.0, scalar=-3e38, op0=ALU.add, op1=ALU.max,
                                                  accum_out=stat[:, 20 + 8 + 4 * p + m:21 + 8 + 4 * p + m])
                link(last)
                TS(stat[:, 16 + 4 * p:18 + 4 * p], stat[:, 28 + 4 * p:30 + 4 * p], -1.0, None, ALU.mult).then_inc(S["da_logit"], 1)

            def da_combine(it):
                i, hh = items[it]
                n, p = (i + 1) * P, it % 2
                r = stat[:, 40 + 4 * p:44 + 4 * p]
                v.wait_ge(S["da_exp"], it + 1)
                link(V.reciprocal(r[:, 0:2], stat[:, 18 + 4 * p:20 + 4 * p]))
                link(TT(r[:, 2:3], r[:, 1:2], lam[:, 4:5], ALU.mult))
                link(TS(lg[p][0][:, 0:n], lg[p][0][:, 0:n], r[:, 0:1], None, ALU.mult))
                STT(lg[p][0][:, 0:n], lg[p][1][:, 0:n], r[:, 2:3], lg[p][0][:, 0:n], ALU.mult, ALU.add).then_inc(S["da_attn"], 1)

            def da_out(it):
                i, hh = items[it]
                h, j = hh % 2, hh // 2
                v.wait_ge(S["da_o"], it + 1)
                V.tensor_copy(ODA[HD * h:HD * h + HD, j, i * P:(i + 1) * P], bank[6 + h][HD * h:HD * h + HD, 0:P]).then_inc(S["da_evac"], 1)

            da_logits(0)
            for it in range(len(items)):
                if it + 1 < len(items):
                    da_logits(it + 1)
                da_combine(it)
                if it >= 2:
                    da_out(it - 2)
            da_out(len(items) - 2)
            da_out(len(items) - 1)
            v.wait_ge(S["da_rstd"], 1)
            for j in range(2):
                last = STT(mixT[:, 2 + j, :], ODA[:, j, :], subg[:, 0:1], PT2[:, j, :], ALU.mult, ALU.mult)
            last.then_inc(S["da_done"], 1)

            norms = [0]

            def norm(s, dst, l):
                norms[0] += 1
                bn = stat[:, 0:12].rearrange("p (c k) -> p c k", k=6)
                for c in range(2):
                    last = V.bn_stats(bn[:, c, :], s[:, c * 512:(c + 1) * 512])
                link(last)
                V.bn_aggr(stat[:, 12:14], bn).then_inc(S["var_ready"], 1)
                v.wait_ge(S["row_rstd"], norms[0])
                link(TS(s, s, stat[:, 12:13], stat[:, 14:15], ALU.subtract, ALU.mult))
                link(TT(s, s, gb[:, 2 * l, :], ALU.mult))
                return TT(dst, s, gb[:, 2 * l + 1, :], ALU.add)

            v.wait_ge(S["gb_in"], 64)
            for i in range(NT):
                v.wait_ge(S["op_done"], i + 1)
                v.wait_ge(xr_in[i % 2], 16 * (i // 2 + 1))
                s = x1[:, i, :]
                last = STT(s, xr[:, i % 2, :], ALPHA, pz[i % 2][:, :], ALU.mult, ALU.add)
                last.then_inc(S["op_sum"], 1)
                v.wait_ge(S["op_sum"], i + 1)
                norm(s, s, 0).then_inc(S["x1_ready"], 1)

            v.wait_ge(S["rl_ev"], NT)

            def r3(n):
                return rt[:, n * 128:(n + 1) * 128].rearrange("p (i e) -> p i e", i=NT)

            aff, sel, rk, cmb, pos, tmp = r3(0), r3(1), r3(2), r3(3), r3(4), r3(5)
            gs, tq = rt2[:, 0:32], [rt2[:, 32 * (k + 1):32 * (k + 2)] for k in range(6)]
            cmp_, grk = rt2[:, 224:256], rt2[:, 256:288]
            link(TS(rl, rl, 1.0, None, ALU.add))
            link(V.reciprocal(aff, rl))
            link(TT(sel, aff, rbias[:, :].unsqueeze(1).to_broadcast([P, NT, NE]), ALU.add))
            s4 = sel.rearrange("p i (g j) -> p (i g) j", j=EPG)
            TT(tq[0], s4[:, :, 0], s4[:, :, 1], ALU.max)
            TT(tq[1], s4[:, :, 0], s4[:, :, 1], ALU.min)
            TT(tq[2], s4[:, :, 2], s4[:, :, 3], ALU.max)
            link(TT(tq[3], s4[:, :, 2], s4[:, :, 3], ALU.min))
            TT(gs, tq[0], tq[2], ALU.max)
            TT(tq[4], tq[0], tq[2], ALU.min)
            link(TT(tq[5], tq[1], tq[3], ALU.max))
            link(TT(tq[4], tq[4], tq[5], ALU.max))
            link(TT(gs, gs, tq[4], ALU.add))

            def ranks(val, rank, n):
                for j in range(EPG):
                    last = V.memset(rank[:, :, j], float(EPG - 1 - j))
                link(last)
                for a in range(EPG):
                    for b in range(a + 1, EPG):
                        link(TT(cmp_[:, 0:n], val[:, :, a], val[:, :, b], ALU.is_ge))
                        TT(rank[:, :, b], rank[:, :, b], cmp_[:, 0:n], ALU.add)
                        link(TT(rank[:, :, a], rank[:, :, a], cmp_[:, 0:n], ALU.subtract))

            rk4 = rk.rearrange("p i (g j) -> p (i g) j", j=EPG)
            ranks(s4, rk4, 32)
            ranks(gs.rearrange("p (i g) -> p i g", g=EPG), grk.rearrange("p (i g) -> p i g", g=EPG), NT)
            link(TS(rk, rk, 2.0, None, ALU.is_lt))
            link(TS(grk, grk, 1.0, None, ALU.is_lt))
            TT(rk4, rk4, grk.unsqueeze(2).to_broadcast([P, 32, EPG]), ALU.mult).then_inc(S["route_sel"], 1)
            v.wait_ge(S["route_sel"], 1)
            link(TT(cmb, aff, rk, ALU.mult))
            den = rt2[:, 320:328]
            link(V.tensor_reduce(den, cmb, AX.X, ALU.add))
            link(V.reciprocal(den, den))
            v.wait_ge(S["cnt_done"], 1)
            tot = bank[1][:, 0:128].rearrange("p (i e) -> p i e", i=NT)
            toff = tmp
            link(V.memset(toff[:, 0, :], 0.0))
            for i in range(NT - 1):
                link(TT(toff[:, i + 1, :], toff[:, i, :], tot[:, i, :], ALU.add))
            cnt, nb, ends, starts = (rt2[:, 336 + 16 * k:352 + 16 * k] for k in range(4))
            link(TT(cnt, toff[:, NT - 1, :], tot[:, NT - 1, :], ALU.add))
            link(V.memset(nb, 1.0))
            for j in range(1, NT):
                link(STT(nb, cnt, float(P * j), nb, ALU.is_gt, ALU.add))
            link(V.tensor_tensor_scan(ends, cst[:, ONES, 0:NE], nb, 0.0, ALU.mult, ALU.add))
            link(TT(starts, ends, nb, ALU.subtract))
            link(TS(starts, starts, float(P), 1.0, ALU.mult, ALU.add))
            link(TT(pos, toff, bank[0][:, 0:128].rearrange("p (i e) -> p i e", i=NT), ALU.add))
            link(TT(pos, pos, starts.unsqueeze(1).to_broadcast([P, NT, NE]), ALU.add))
            link(TT(pos, pos, rk, ALU.mult))
            hi, lo = rt2[:, 400:408], rt2[:, 408:416]
            V.tensor_reduce(hi, pos, AX.X, ALU.max)
            link(V.tensor_reduce(lo, pos, AX.X, ALU.add))
            link(TT(lo, lo, hi, ALU.subtract))
            for s, w in enumerate((hi, lo)):
                link(TT(tmp, pos, w.unsqueeze(2).to_broadcast([P, NT, NE]), ALU.is_equal))
                link(TT(tmp, tmp, cmb, ALU.mult))
                link(V.tensor_reduce(gates[:, s, :], tmp, AX.X, ALU.add))
                link(TT(gates[:, s, :], gates[:, s, :], den, ALU.mult))
                link(TS(w, w, -1.0, None, ALU.add))
                V.tensor_copy(slots[:, s, :], w)
            eh = mixT[:, 7, 0:NBP * NE].rearrange("p (b e) -> p b e", b=NBP)
            v.wait_ge(S["op_done"], NT)
            link(TT(eh, small[:, 0:NBP].unsqueeze(2).to_broadcast([P, NBP, NE]), ends.unsqueeze(1).to_broadcast([P, NBP, NE]), ALU.is_ge))
            ef = rt2[:, 416:448]
            link(V.tensor_reduce(ef, eh, AX.X, ALU.add))
            link(TS(ef, ef, float(NE - 1), None, ALU.min))
            v.wait_ge(S["slot_zero"], 16)
            V.tensor_copy(ids[:, :], ef).then_inc(S["ids_ready"], 1)

            def gated(b):
                v.wait_ge(S["exp_g"], b + 1)
                g, e, h = bank[4 + b % 2], eb[b % 2], hb[b % 2]
                if b >= 2:
                    v.wait_ge(S["h_t"], b - 1)
                link(sigmoid(e))
                link(TT(e, e, g[:, 0:FE], ALU.mult))
                TT(h, e, g[:, FE:2 * FE], ALU.mult).then_inc(S["gated"], 1)

            gated(0)
            for b in range(BLOCKS):
                if b + 1 < BLOCKS:
                    gated(b + 1)
                v.wait_ge(S["down_done"], b + 1)
                if b >= 2:
                    v.wait_ge(y_st[b % 2], 16 * (b // 2))
                V.tensor_copy(yb[b % 2][:, 512:1024], bank[3]).then_inc(S["y_ev"], 1)

            for i in range(NT):
                v.wait_ge(yg_in[i % 2], 32 * (i // 2 + 1))
                ya, yb2 = mixT[:, 2 * (i % 2), :], mixT[:, 2 * (i % 2) + 1, :]
                s = x1[:, i, :]
                link(TS(s, s, ALPHA, None, ALU.mult))
                link(TS(ya, ya, gates[:, 0, i:i + 1], None, ALU.mult))
                link(STT(ya, yb2, gates[:, 1, i:i + 1], ya, ALU.mult, ALU.add))
                link(TT(s, s, ya, ALU.add))
                norm(s, s, 1).then_inc(S["fin_ready"], 1)

        @block.tensor
        def _(pe):
            MM = nc.tensor.matmul

            def turn(o, i):
                return nc.tensor.transpose(o, i, C(IDENT))

            pe.wait_ge(S["mats_in"], 16)
            for n in range(16):
                i, c = n // 2, n % 2
                if c == 0:
                    pe.wait_ge(x_in[i % 2], 16 * (i // 2 + 1))
                if n >= 4:
                    pe.wait_ge(S["xT_ready"], n - 3)
                for k in range(4):
                    last = turn(bank[n % 4][:, k * P:(k + 1) * P], xs[:, i % 2, (4 * c + k) * P:(4 * c + k + 1) * P])
                last.then_inc(S["x_turned"], 1)

            def fill(n):
                kind, t, half = fills[n]
                if n >= 4:
                    pe.wait_ge(S["fill_evac"], n - 3)
                o = bank[4 + n % 4]
                if n < 2:
                    pe.wait_ge(S["xT_ready"], 8 * (n + 1))
                if kind == "v":
                    if t == 0:
                        pe.wait_ge(wv_in, 32)
                    for k in range(KD):
                        last = MM(o, xT[:, k, t * P:(t + 1) * P], wv[:, k, :], start=k == 0, stop=k == KD - 1)
                else:
                    if half == 0:
                        pe.wait_ge(w_arr[t % 4], 16 * (t // 4 + 1))
                    for k in range(KD):
                        last = MM(o, wring[:, t % 4, k, :], xT[:, k, half * 512:(half + 1) * 512], start=k == 0, stop=k == KD - 1)
                last.then_inc(S["fill_done"], 1)

            def aux(a):
                j, half = a // 2 % 2, a % 2
                h_ = slice(half * 512, (half + 1) * 512)
                if a < 12:
                    if a >= 4:
                        pe.wait_ge(S["aux_evac"], a - 3)
                    lo, hi = ((0, 32), (32, 64), (64, 128))[a // 4]
                    mm = MM(bank[a % 4], low_up[lo:hi, j * P:(j + 1) * P], rw[lo:hi, 6, 1 + half * 512:1 + (half + 1) * 512], start=True, stop=True)
                elif a < 16:
                    pe.wait_ge(S["aux_evac"], a - 3)
                    mm = MM(bank[a % 4], C(BO), S2[:, j, h_], start=True, stop=True)
                else:
                    pe.wait_ge(S["aux_devac"], a - 15)
                    mm = MM(bank[a % 4], C(BO), S3[:, j, h_], start=True, stop=True)
                mm.then_inc(S["aux_done"], 1)

            for n in range(NFILL):
                fill(n)
                if n == 3:
                    pe.wait_ge(S["bias_up"], 1)
                    pe.wait_ge(S["xT_ready"], 16)
                    for h in range(4):
                        for c in range(3):
                            if h:
                                pe.wait_ge(S["bias_evac"], 3 * (h - 1) + c + 1)
                            MM(bank[c][:, 0:384], bias_l[:, h, :], hot[:, c * 384:(c + 1) * 384], start=True, stop=True).then_inc(S["bias_rows"], 1)
                if n == 18:
                    pe.wait_ge(S["low_ready"], 1)
                    pe.wait_ge(S["bias_evac"], 12)
                    for a in range(12):
                        aux(a)
                if n == 29:
                    pe.wait_ge(S["sq_ready"], 1)
                    for a in range(12, 16):
                        aux(a)
                if n == 36:
                    pe.wait_ge(S["bonus_ready"], 1)
                    for a in range(16, 20):
                        aux(a)

            pe.wait_ge(S["rwe_done"], 1)
            pe.wait_ge(S["aux_devac"], 8)
            pe.wait_ge(S["fill_evac"], NFILL)

            def rw_fill_of(m, h, k):
                g = m * NF[h] + k + (4 if h == 0 else 0)
                base = m * NF[h] + (4 if h == 0 else 0)
                b, lo, hi = chb[h], HD * h, HD * h + HD
                o = bank[4 * h + g % 4].rearrange("p (q c) -> p q c", q=4)
                if g >= 4:
                    pe.wait_ge(rw_evac[h], g - 3)
                need = {5: 4, 23: 23, 24: 24, 25: 24, 26: 26, 27: 27, 28: 27}.get(k)
                if 6 <= k < 23:
                    need = {6: 1, 22: k}.get(k, k if (k - 6) % 3 == 1 else k - 1)
                if need:
                    pe.wait_ge(rw_evac[h], base + need)
                if k == 6:
                    pe.wait_ge(S["rw_init"], 2 * m + h + 1)
                for q in range(4):
                    n2, j = q // 2, q % 2
                    n = 2 * m + n2
                    ck = slice(n * P, (n + 1) * P)
                    a_, b_, k_, r_ = S1[lo:hi, j, ck], S2[lo:hi, j, ck], rK[lo:hi, j, ck], rR[lo:hi, j, ck]
                    if k < 0:
                        src = (S1, S2, rK, rV)[k + 4][:, j, ck]
                        last = turn(o[:, q, :], src)
                    elif k < 5:
                        l_, m_ = ((b_, a_), (a_, b_), (b_, r_), (k_, a_), (k_, r_))[k]
                        last = MM(o[:, q, :], l_, m_, start=True, stop=True)
                    elif k == 5:
                        last = MM(bank[4 * h + g % 4][:, q * HD:(q + 1) * HD], b["AkT"][:, q, :], tm["v"][:, q, lo:hi], start=True, stop=True)
                    elif k < 23:
                        lev, what = (k - 6) // 3, (k - 6) % 3
                        if lev == 5 and what == 1:
                            what = 2
                        l_, m_ = (("LT", "X"), ("XT", "W"), ("W", "XT"))[what]
                        last = MM(o[:, q, :], b[l_][:, q, :], b[m_][:, q, :], start=True, stop=True)
                    elif k == 23:
                        MM(o[:, q, 0:HD], b["XT"][:, q, :], tm["a"][:, q, lo:hi], start=True, stop=True)
                        last = MM(o[:, q, HD:P], b["XT"][:, q, :], b["AkV"][:, q, :], start=True, stop=True)
                    elif k == 24:
                        last = MM(o[lo:hi, q, :], b["U"][:, q, 0:HD], b["RbT"][:, q, :], start=True, stop=True)
                    elif k == 25:
                        MM(o[lo:hi, q, 0:HD], tm["b"][:, q, lo:hi], b["U"][:, q, HD:P], start=True, stop=False)
                        MM(o[lo:hi, q, 0:HD], tm["k"][:, q, lo:hi], tm["v"][:, q, lo:hi], start=False, stop=True)
                        last = MM(o[lo:hi, q, HD:P], b["U"][:, q, 0:HD], tm["b"][:, q, lo:hi], start=True, stop=True)
                    elif k in (26, 27):
                        if n2 == k - 26:
                            last = MM(o[lo:hi, j, 0:HD], b["NG"][lo:hi, q, HD:P], st[lo:hi, j, n, :], start=True, stop=True)
                    else:
                        MM(o[lo:hi, q, :], b["U"][:, q, HD:P], b["RbT"][:, q, :], start=True, stop=False)
                        MM(o[lo:hi, q, :], tm["v"][:, q, lo:hi], b["RkT"][:, q, :], start=False, stop=False)
                        last = MM(o[lo:hi, q, :], st[lo:hi, j, n, :], b["RP"][lo:hi, q, :], start=False, stop=True)
                last.then_inc(rw_fill[h], 1)

            for m in range(NT // 2):
                for k in range(-4, 0):
                    rw_fill_of(m, 0, k)
                for k in range(29):
                    for h in range(2):
                        if h == 1 and k == 5:
                            pe.wait_ge(rw_evac[0], m * NF[0] + 4)
                        rw_fill_of(m, h, k)
            for h in range(2):
                pe.wait_ge(rw_evac[h], NT // 2 * NF[h])
            for q in range(4):
                j, half = q // 2, q % 2
                MM(bank[q], C(BM), YT[:, j, half * 512:(half + 1) * 512], start=True, stop=True).then_inc(S["mean_done"], 1)
            for q in range(4):
                j, half = q // 2, q % 2
                pe.wait_ge(S["squared"], q + 1)
                MM(bank[4 + q], C(BM), PT[:, j, half * 512:(half + 1) * 512], start=True, stop=True).then_inc(S["var_done"], 1)

            pe.wait_ge(S["rw_out"], 1)

            def sb_z(it):
                i, hh = items[it]
                h, j, n, p = hh % 2, hh // 2, (i + 1) * P, it % 2
                lo, hi = HD * h, HD * h + HD
                if it >= 2:
                    pe.wait_ge(S["sb_logw"], it - 1)
                for c in range(0, n, 512):
                    e = min(n, c + 512)
                    last = MM(pz[p][:, c:e], qk[lo:hi, j, i * P:(i + 1) * P], qk[lo:hi, 2 + j, c:e], start=True, stop=True)
                last.then_inc(S["sb_z"], 1)

            def weights_out(it, src, wT, ready, turned, copied, evac, done, v0):
                i, hh = items[it]
                h, p = hh % 2, it % 2
                lo, hi = HD * h, HD * h + HD
                pe.wait_ge(ready, it + 1)
                if it >= 1:
                    pe.wait_ge(copied, it)
                for k in range(i + 1):
                    last = turn(bank[4 + k // 4][:, (k % 4) * P:(k % 4 + 1) * P], src[:, k * P:(k + 1) * P])
                last.then_inc(turned, 1)
                pe.wait_ge(copied, it + 1)
                if it >= 2:
                    pe.wait_ge(evac, it - 1)
                for k in range(i + 1):
                    last = MM(bank[6 + h][lo:hi, 0:P], vt[:, k, v0 + hh * HD:v0 + (hh + 1) * HD], wT[:, k, :], start=k == 0, stop=k == i)
                last.then_inc(done, 1)

            sb_z(0)
            for it in range(len(items)):
                if it + 1 < len(items):
                    sb_z(it + 1)
                weights_out(it, sbW[it % 2], sbT[it % 2], S["sb_w"], S["sb_t"], S["sb_wT"], S["sb_evac"], S["sb_o"], 0)

            def da_z(it):
                i, hh = items[it]
                h, j, n = hh % 2, hh // 2, (i + 1) * P
                if it >= 1:
                    pe.wait_ge(S["da_logit"], it)
                for m in range(2):
                    lo = HD * h + 32 * m
                    for c in range(0, n, 512):
                        e = min(n, c + 512)
                        last = MM(pz[m][:, c:e], qk[lo:lo + 32, 4 + j, i * P:(i + 1) * P], qk[lo:lo + 32, 6 + j, c:e], start=True, stop=True)
                last.then_inc(S["da_z"], 1)

            pe.wait_ge(S["sb_evac"], len(items))
            da_z(0)
            for it in range(len(items)):
                if it + 1 < len(items):
                    da_z(it + 1)
                weights_out(it, lg[it % 2][0], daT[it % 2], S["da_attn"], S["da_t"], S["da_wT"], S["da_evac"], S["da_o"], GW)
            pe.wait_ge(S["da_sq"], 1)
            for q in range(4):
                j, half = q // 2, q % 2
                MM(bank[q], C(BM), PT[:, j, half * 512:(half + 1) * 512], start=True, stop=True).then_inc(S["da_ms"], 1)

            pe.wait_ge(S["wout_in"], 16)
            pe.wait_ge(S["da_done"], 1)

            def project(i):
                if i >= 2:
                    pe.wait_ge(S["op_sum"], i - 1)
                for c in range(2):
                    for k in range(8):
                        last = MM(pz[i % 2][:, c * 512:(c + 1) * 512], mixT[:, k, i * P:(i + 1) * P], wout[:, k, c * 512:(c + 1) * 512], start=k == 0, stop=k == 7)
                last.then_inc(S["op_done"], 1)

            def router(i):
                pe.wait_ge(S["x1_ready"], i + 1)
                if i >= 1:
                    pe.wait_ge(S["x1_tev"], i)
                for k in range(KD):
                    last = turn(bank[4 + k // 4][:, (k % 4) * P:(k % 4 + 1) * P], x1[:, i, k * P:(k + 1) * P])
                last.then_inc(S["x1_t"], 1)
                pe.wait_ge(S["x1_tev"], i + 1)
                if i >= 1:
                    pe.wait_ge(S["rl_ev"], i)
                for k in range(KD):
                    last = MM(bank[6][:, 0:NE], x1T[:, k, :], rwr[:, k, :], start=k == 0, stop=k == KD - 1)
                last.then_inc(S["rl_done"], 1)

            project(0)
            project(1)
            for i in range(NT):
                if i + 2 < NT:
                    project(i + 2)
                router(i)
            pe.wait_ge(S["route_sel"], 1)
            selm = rt[:, 256:384]
            MM(bank[0][:, 0:128], C(SU), selm, start=True, stop=True)
            MM(bank[1][:, 0:128], C(ONES), selm, start=True, stop=True).then_inc(S["cnt_done"], 1)

            def gather_turn(b):
                pe.wait_ge(xg_in[b % 2], 16 * (b // 2 + 1))
                if b >= 1:
                    pe.wait_ge(S["xg_tev"], b)
                for k in range(KD):
                    last = turn(bank[k // 4][:, (k % 4) * P:(k % 4 + 1) * P], xg[b % 2][:, k * P:(k + 1) * P])
                last.then_inc(S["xg_t"], 1)

            def up(b):
                pe.wait_ge(S["xg_tev"], b + 1)
                pe.wait_ge(we_in[b % 2], 32 * (b // 2 + 1))
                if b >= 2:
                    pe.wait_ge(S["gated"], b - 1)
                for k in range(KD):
                    last = MM(bank[4 + b % 2], xgT[b % 2][:, k, :], weu[b % 2][:, k, :], start=k == 0, stop=k == KD - 1)
                last.then_inc(S["up_done"], 1)

            def down(b):
                pe.wait_ge(S["gated"], b + 1)
                if b >= 1:
                    pe.wait_ge(S["h_tev"], b)
                for k in range(2):
                    last = turn(bank[6][:, k * P:(k + 1) * P], hb[b % 2][:, k * P:(k + 1) * P])
                last.then_inc(S["h_t"], 1)
                pe.wait_ge(S["h_tev"], b + 1)
                if b >= 1:
                    pe.wait_ge(S["y_ev"], 2 * b)
                for c in range(2):
                    for k in range(2):
                        last = MM(bank[2 + c], hTb[b % 2][:, k, :], wed[b % 2][:, k, c * 512:(c + 1) * 512], start=k == 0, stop=k == 1)
                last.then_inc(S["down_done"], 1)

            pe.wait_ge(S["ids_ready"], 1)
            gather_turn(0)
            up(0)
            for b in range(BLOCKS):
                if b + 1 < BLOCKS:
                    gather_turn(b + 1)
                    up(b + 1)
                down(b)


_INS = ['x', 'w_in', 'w_out', 'da_lambda', 'da_subln', 'sc_conv', 'rw_mu', 'rw_vecs', 'rw_w_up', 'rw_a_up', 'rw_g_up',
        'ln_gain', 'ln_bias', 'rel_bias', 'router_w', 'router_b', 'moe_w_in', 'moe_w_down']


def kernel(**inputs):
    import concourse.bacc as _bacc
    from concourse.bass_utils import run_bass_kernel_spmd as _run

    nc = _bacc.Bacc("TRN2", target_bir_lowering=False, num_devices=1)
    arrays, args = {}, []
    values = {n: np.ascontiguousarray(inputs[n]) for n in _INS}
    values.update(constants())
    for name, a in values.items():
        arrays[f"in_{name}"] = a
        args.append(nc.dram_tensor(f"in_{name}", a.shape, mybir.dt.from_np(a.dtype), kind="ExternalInput").ap())
    args.append(nc.dram_tensor("out_0", (1, T, D), F32, kind="ExternalOutput").ap())
    layer_kernel(nc, *args)
    r = _run(nc, [arrays], core_ids=[0])
    return r.results[0]["out_0"]
```

```python
import math
from contextlib import ExitStack, nullcontext

import numpy as np
import concourse.bass as bass
from concourse import mybir

F32 = mybir.dt.float32
I32 = mybir.dt.int32
ALU = mybir.AluOpType
ACT = mybir.ActivationFunctionType
AX = mybir.AxisListType

D, T, P = 1024, 1024, 128
KD = D // P
NT = T // P
GW = 256
HD = 64
RW_COLS = 3 * GW + 128
P_IN = 9 * GW + RW_COLS
NE, FE = 16, 256
EPG = 4
ALPHA = 2 ** 0.25
LAM_INIT = 0.8 - 0.6
DECAY = math.exp(-0.5)
NEG = -1e30
BLOCKS = NE + (2 * T - NE) // P
NBP = 32
SB0, DA0, SC0, RW0 = 0, 3 * GW, 6 * GW, 9 * GW
BUCKETS, MAX_DIST = 32, 128
LT5 = 3 * P

RW_SHARE = 0.9

IDENT, SU, UI, SL, ONES, BO, BM, M1, M1T, MB, NEGD, SCANM, NCST = 0, 1, 2, 3, 4, 5, 6, 7, 8, 9, 15, 16, 17


def constants():
    r = np.arange(P)
    row, col = r[:, None], r[None, :]
    c = np.zeros((P, NCST, P), np.float32)
    c[:, IDENT] = row == col
    c[:, SU] = row < col
    c[:, UI] = row <= col
    c[:, SL] = row > col
    c[:, ONES] = 1
    c[:, BO] = row // HD == col // HD
    c[:, BM] = (row // HD == col // HD) / HD

    def level(b):
        return (row // (2 * b) == col // (2 * b)) & (row // b % 2 == 1) & (col // b % 2 == 0)
    c[:, M1] = level(1)
    c[:, M1T] = level(1).T
    for n in range(6):
        c[:, MB + n] = level(2 << n)
    c[:, NEGD] = np.where(row > col, 0.0, NEG)
    c[:, SCANM] = np.broadcast_to(col != 0, (P, P))
    d = 2 * P - 1 - np.arange(LT5)
    n = np.maximum(d, 0)
    nf = np.maximum(n, 1).astype(np.float32)
    big = 16 + (np.log(nf / np.float32(16)) / np.float32(math.log(MAX_DIST / 16)) * np.float32(16)).astype(np.int32)
    bucket = np.where(n < 16, n, np.minimum(big, BUCKETS - 1))
    hot = np.zeros((BUCKETS + 1, LT5), np.float32)
    hot[bucket[d >= 0], np.nonzero(d >= 0)[0]] = 1
    hot[BUCKETS, d < 0] = NEG
    s = np.zeros((P, 64), np.float32)
    s[:, 0:NBP] = np.arange(NBP)
    s[0:32, 32] = -2.0
    s[32:, 32] = -1.0
    s[:, 33], s[:, 34], s[:, 35] = 64e-5, 1e-5, 1.0
    tok = (np.arange(NT)[None, :] * P + r[:, None]).astype(np.int32)
    return {"c_mats": c.reshape(P, NCST * P), "c_hot": hot, "c_small": s, "c_tok": tok}


def layer_kernel(nc, x, w_in, w_out, da_lambda, da_subln, sc_conv, rw_mu, rw_vecs, rw_w_up, rw_a_up, rw_g_up,
                 ln_gain, ln_bias, rel_bias, router_w, router_b, moe_w_in, moe_w_down,
                 c_mats, c_hot, c_small, c_tok, out):
    ctx = ExitStack()
    with ctx:
        ctx.enter_context(nc.allow_non_contiguous_dma("small parameter columns"))

        def sb(name, shape, dt=F32):
            return ctx.enter_context(nc.sbuf_tensor(name, shape, dt))

        def sem(name):
            return ctx.enter_context(nc.semaphore(name))

        bias_d = nc.dram_tensor("bias_d", [4, P * LT5], F32)
        x1_d = nc.dram_tensor("x1_d", [T, D], F32)
        y_d = nc.dram_tensor("y_d", [BLOCKS * P, D], F32)
        slot_d = nc.dram_tensor("slot_d", [NBP * P, 1], I32)

        cst = sb("cst", [P, NCST, P])
        small = sb("small", [P, 64])
        tok = sb("tok", [P, NT], I32)
        mu = sb("mu", [P, 7])
        vecs = sb("vecs", [P, 7, 2])
        conv = sb("conv", [P, 3, 2])
        subg = sb("subg", [P, 1])
        relb = sb("relb", [BUCKETS, 4])
        lp = sb("lp", [P, 4, 32])
        lam = sb("lam", [P, 8])
        low_up = sb("low_up", [P, GW])
        rwr = sb("rwr", [P, KD, NE])
        rbias = sb("rbias", [P, NE])
        dfac = sb("dfac", [P, 2, NT])
        smid = sb("smid", [P, 2, NT])
        stat = sb("stat", [P, 64])
        mixT = sb("mixT", [P, 8, T])
        qk = sb("qk", [P, 8, T])
        vt = sb("vt", [P, NT, 2 * GW])
        mid = sb("mid", [P, 6 * T + 7 * (T + 1)])
        sc = mid[:, 0:6 * T].rearrange("p (j t) -> p j t", j=6)
        rw = mid[:, 6 * T:].rearrange("p (j t) -> p j t", j=7)
        arena = sb("arena", [P, 16 * 1024])

        def region(at, *dims):
            n = 1
            for d in dims:
                n *= d
            v = arena[:, at:at + n]
            if len(dims) == 2:
                return v.rearrange("p (a b) -> p a b", a=dims[0])
            if len(dims) == 3:
                return v.rearrange("p (a b c) -> p a b c", a=dims[0], b=dims[1])
            return v

        def C(i):
            return cst[:, i, :]

        pz = [ctx.enter_context(nc.psum_tensor(f"pz{i}", [P, 1024], F32)) for i in range(2)]
        pb = [ctx.enter_context(nc.psum_tensor(f"pb{i}", [P, 512], F32)) for i in range(4)]
        bank = [pz[0][:, 0:512], pz[0][:, 512:1024], pz[1][:, 0:512], pz[1][:, 512:1024]] + [b[:, :] for b in pb]

        names = """kk_scale ln_done rw_rstd da_rstd var_ready row_rstd mats_in consts zeroed x_turned xT_ready fill_done fill_evac mix_diff mixed low_exp low_ready aux_done aux_evac
            aux_devac conv_u conv_done sq_ready decay_ready decays bonus_ready rwe_done
            bias_up bias_rows bias_evac bias_st bias_far
            x_init rw_init mean_done centred squared var_done rw_out
            sb_z sb_soft sb_log sb_w da_z da_max da_prob da_attn at_t at_wT at_o at_evac
            da_sq da_ms da_done lam_prod lam_exp rw_fill rw_evac rw_copied rw_vevac
            wout_in op_done op_sum x1_ready x1_st x1_t x1_tev rl_done rl_ev route_exp route_sel cnt_done
            slot_zero slot_sc slot_in gather up_done exp_g gate_step gated h_t h_tev down_done y_ev xg_t xg_tev
            y_zero y_scaled fin_stat fin_norm fin_gain fin_ready out_st gb_in ids_ready vchain achain pchain""".split()
        S = {n: sem(n) for n in names}
        x_in = [sem(f"x_in{i}") for i in range(2)]
        w_arr = [sem(f"w_arr{i}") for i in range(4)]
        wv_in = sem("wv_in")
        t5_in = sem("t5_in")
        xr_in = [sem(f"xr_in{i}") for i in range(2)]
        wd_in = [sem(f"wd_in{i}") for i in range(2)]
        we_in = [sem(f"we_in{i}") for i in range(2)]
        xg_in = [sem(f"xg_in{i}") for i in range(2)]
        y_st = [sem(f"y_st{i}") for i in range(2)]
        yg_in = [sem(f"yg_in{i}") for i in range(4)]

        block = ctx.enter_context(nc.Block())

        xT = region(0, KD, T)
        wring = region(8192, 4, KD, P)
        xs = region(12288, 2, T)
        wv = region(12288, KD, 512)
        tiles = []
        for s, c in ((6, 768), (2, 256), (3, 384), (0, 0), (1, 128), (4, 512), (5, 640)):
            tiles.append((RW0 + c, rw[:, s, 1:T + 1], 1.0))
        for s in range(6):
            tiles.append((SC0 + s * P, sc[:, s, :], 1.0))
        for s in range(4):
            tiles.append((SB0 + s * P, qk[:, s, :], HD ** -0.5 if s < 2 else 1.0))
        for s in range(4):
            tiles.append((DA0 + s * P, qk[:, 4 + s, :], 32 ** -0.5 if s < 2 else 1.0))
        NTILE, V_AT = len(tiles), 13
        NFILL = 2 * NTILE + NT
        rw_order = [6, 2, 3, 0, 1, 4, 5]

        def fill_of(t):
            return 2 * t + (NT if t >= V_AT else 0)

        fills = []
        for t in range(NTILE):
            if t == V_AT:
                fills += [("v", i, 0) for i in range(NT)]
            fills += [("f", t, 0), ("f", t, 1)]
        M01, M23, M67 = mixT[:, 0:2, :], mixT[:, 2:4, :], mixT[:, 6:8, :]
        S1, S2, S3 = sc[:, 0:2, :], sc[:, 2:4, :], sc[:, 4:6, :]
        D1, D2 = qk[:, 4:6, :], qk[:, 6:8, :]
        rR, rK, rV = rw[:, 0:2, 1:T + 1], rw[:, 2:4, 1:T + 1], rw[:, 4:6, 1:T + 1]
        brows = qk[:, 0:2, :].rearrange("p j t -> p (j t)")[:, 0:4 * LT5].rearrange("p (h m) -> p h m", h=4)
        hot = qk[0:BUCKETS + 1, 2, 0:LT5]
        bias_l = qk[0:BUCKETS + 1, 4, 0:512].rearrange("p (h c) -> p h c", h=4)
        NCONST = 17

        shared = [("LT", "RP"), ("X", "U"), ("RbT",), ("RkT",), ("XT",), ("AkT", "W", "NG")]
        cbs = [{n: region(h * 3328 + i * 512, 4, P) for i, names_ in enumerate(shared) for n in names_} for h in range(2)]
        for h in range(2):
            cbs[h]["AkV"] = region(h * 3328 + 3072, 4, HD)
        tm = {n: region(6656 + i * 512, 4, P) for i, n in enumerate("abkv")}
        st = rw[:, 6, 1:T + 1].rearrange("p (j n c) -> p j n c", j=2, n=NT)
        KEYS = ["LT", "L", "RbT", "AkT", "RkT", "AkV"]
        for lev in range(6):
            KEYS += [f"W{lev}", f"X{lev}", f"XT{lev}"] if lev < 5 else ["W5", "XT5"]
        KEYS += ["U", "RP", "NG", "S0", "S1", "Y"]
        rw_fills = []
        for m in range(NT // 2):
            rw_fills += [(m, 0, key) for key in ("Ta", "Tb", "Tk", "Tv")]
            for key in KEYS:
                if key == "S1" and m == NT // 2 - 1:
                    continue
                rw_fills += [(m, 0, key), (m, 1, key)]
        at = {f: g for g, f in enumerate(rw_fills)}
        NRW = len(rw_fills)
        bufE = [region(8704 + i * 1024, T) for i in range(2)]
        bufS = [region(10752 + i * 1024, T) for i in range(2)]
        bufT = [region(12800 + i * 1024, NT, P) for i in range(2)]
        t5 = region(14848, 4, 2 * P)

        def da_logits(it, m):
            i = items[it][1]
            c0 = 512 * (it % 2) if i < 4 else 0
            return pz[m][:, c0:c0 + (i + 1) * P]
        items = [("sb", i, hh) for i in range(NT) for hh in range(4)] + [("da", i, hh) for i in range(NT) for hh in range(4)]
        NI, NSB = len(items), len(items) // 2
        turn_at, halves = [], 0
        for _, i, _ in items:
            turn_at.append(halves)
            halves += 1 + i // 4

        def evacuator(g):
            return "act" if rw_fills[g][2] in ("Ta", "Tb", "Tk", "Tv", "AkV", "U", "Y") else "dve"

        evacs = {e: [sum(evacuator(f) == e for f in range(g + 1)) for g in range(NRW)] for e in ("act", "dve")}

        def rw_operands(g):
            m, h, key = rw_fills[g]
            lev = int(key[-1]) if key[-1].isdigit() else 0
            need = {"AkV": "AkT", "U": "XT5", "RP": "U", "NG": "U", "S0": "NG", "S1": "S0", "Y": "S0"}.get(key)
            if key[0] == "W":
                need = f"X{lev - 1}" if lev else "LT"
            elif key[0] == "X":
                need = f"W{lev}"
            return max(g - 2, at[m, h, need] if need else 0)

        def parts(it):
            return 1 + items[it][1] // 4

        def make_plan():
            lanes = {}
            HOP = 0.15

            def add(eng, step, cost, *deps):
                lanes.setdefault((eng, step[0]), []).append((step, cost, [d for d in deps if d]))

            def vec(n):
                return 0.06 + n / 960

            def sca(n):
                return 0.2 + n / 1200

            for g in range(NRW):
                m, h, key = rw_fills[g]
                last = rw_operands(g)
                deps = [("rwe", f) for f in range(max(0, last - 3), last + 1)] if g >= 2 else []
                if key == "W0":
                    deps.append(("init", 2 * m + h))
                add("pe", ("rw", g), {"Y": 2.6, "NG": 1.3, "AkV": 0.43, "S0": 0.2, "S1": 0.2}.get(key, 0.86), *deps)
                add(evacuator(g), ("rwe", g), {"NG": 0.9, "S0": 0.3, "S1": 0.3}.get(key, 0.6), ("rw", g),
                    ("init", 2 * m + h) if key == "X0" else None, ("rwe", g - 2) if key[0] == "S" else None)
                if key == "L":
                    add("pool", ("init", 2 * m + h), 3.6, ("rwe", g))
            add("pe", ("rwpost", 0), 8.0, ("rwe", NRW - 1))
            add("dve", ("rwpost", 0), 10.0, ("rwe", NRW - 1))
            add("act", ("rwpost", 0), 8.0, ("rwe", NRW - 1))
            for it in range(NI):
                kind, i, _ = items[it]
                n, np_ = (i + 1) * P, parts(it)
                two_ago = it - 2 if it >= 2 else None
                freed = ("t", two_ago, parts(two_ago) - 1) if it >= 2 else None
                if kind == "sb":
                    add("pe", ("z", it), n / 600, ("l3", two_ago) if it >= 2 else None)
                    add("act", ("a", it), 3 * sca(n) + 0.2, ("z", it), ("l3", two_ago) if it >= 2 else None)
                    add("dve", ("l1", it), vec(n) + 0.5, ("a", it), freed)
                    add("dve", ("l2", it), vec(n) + 0.1, ("l1", it))
                    add("dve", ("l3", it), vec(n) + 0.4, ("l2", it))
                    add("act", ("e", it), sca(n), ("l3", it))
                    weights = ("e", it)
                else:
                    for m in range(2):
                        back = 2 if i < 4 and it - 2 >= NSB else 1
                        used = ("l3", NSB - 2 + m) if it - back < NSB else ("p", it - back, m)
                        add("pe", ("s", it, m), n / 600, used)
                        add("dve", ("x", it, m), vec(n) + 0.5, ("s", it, m))
                        add("act", ("p", it, m), sca(n) + 0.1, ("x", it, m), freed)
                    add("dve", ("c1", it), vec(n) + 0.4, ("p", it, 0), ("p", it, 1))
                    add("dve", ("c2", it), vec(n), ("c1", it))
                    weights = ("c2", it)
                prev = ("t", it - 1, parts(it - 1) - 1) if it else None
                for part in range(np_):
                    k = min(i + 1, 4 * part + 4) - 4 * part
                    before = ("ct", it, part - 1) if part else ("ct", it - 1, parts(it - 1) - 1) if it else None
                    add("pe", ("t", it, part), 0.213 * k, weights, before)
                    add("act", ("ct", it, part), sca(k * P), ("t", it, part), ("v", it - 2, parts(it - 2) - 1) if it >= 2 else None)
                    add("pe", ("v", it, part), 0.213 * k, ("ct", it, part), ("o", it - 4) if it >= 4 else None)
                add("dve", ("o", it), 0.2, ("v", it, np_ - 1))

            work = {r: sum(c for (e, k), q in lanes.items() if e == "pe" and (k in ("rw", "rwpost")) == r for _, c, _ in q) for r in (True, False)}
            spent = {True: 0.0, False: 0.0}
            done, free = {}, {e: 0.0 for e in ("pe", "dve", "act", "pool")}
            plan = {e: [] for e in free}
            head = {lane: 0 for lane in lanes}
            rank = {"o": 0, "v": 1, "ct": 1, "t": 2, "e": 3, "c2": 3, "c1": 4, "l3": 4, "l2": 5, "l1": 6, "p": 6, "x": 6, "a": 7, "z": 8, "s": 8}
            while len(done) < sum(map(len, lanes.values())):
                best = None
                for (eng, kind), q in lanes.items():
                    h = head[eng, kind]
                    if h == len(q) or any(d not in done for d in q[h][2]):
                        continue
                    start = max([free[eng]] + [done[d] + HOP for d in q[h][2]])
                    rwkv = kind in ("rw", "rwe", "rwpost", "init")
                    ahead = spent[True] / work[True] > RW_SHARE * spent[False] / work[False]
                    key = (start, rwkv == ahead, rank.get(kind, 0), q[h][0][1])
                    if best is None or key < best[0]:
                        best = (key, eng, kind)
                key, eng, kind = best
                step, cost, _ = lanes[eng, kind][head[eng, kind]]
                head[eng, kind] += 1
                free[eng] = done[step if kind != "rwpost" else (step, eng)] = key[0] + cost
                plan[eng].append(step)
                if eng == "pe":
                    spent[kind in ("rw", "rwpost")] += cost
            return plan, done

        plan, done_at = make_plan()
        PT, PT2 = region(0, 2, T), region(2048, 2, T)
        wout = mid[:, 0:8192].rearrange("p (k n) -> p k n", k=KD)
        x1 = region(0, NT, T)
        gb = qk[:, 0:4, :]
        xr = qk[:, 4:6, :]
        x1T = qk[:, 6, :].rearrange("p (k t) -> p k t", k=KD)
        rt = region(8192, 768)
        rt2 = region(8960, 480)
        rl = region(9440, NT, NE)
        we = [mid[:, i * 6144:(i + 1) * 6144] for i in range(2)]
        weu = [w[:, 0:4096].rearrange("p (k n) -> p k n", k=KD) for w in we]
        wed = [w[:, 4096:6144].rearrange("p (k n) -> p k n", k=2) for w in we]
        xg = [mixT[:, i, :] for i in range(2)]
        xgT = [mixT[:, 2 + i, :].rearrange("p (k t) -> p k t", k=KD) for i in range(2)]
        yb = [mixT[:, 4 + i, :] for i in range(2)]
        hb = [mixT[:, 6, i * 512:i * 512 + 256] for i in range(2)]
        eb = [mixT[:, 6, i * 512 + 256:i * 512 + 512] for i in range(2)]
        hTb = [mixT[:, 7, i * 256:(i + 1) * 256].rearrange("p (k t) -> p k t", k=2) for i in range(2)]
        slots = sb("slots", [P, 2, NT], I32)
        gates = sb("gates", [P, 2, NT])
        ids = sb("ids", [P, NBP], I32)
        slot_tok = sb("slot_tok", [P, NBP], I32)

        def used_blocks(eng):
            return eng.value_load(ids[0:1, NBP - 1:NBP], min_val=NE, max_val=BLOCKS)

        def when_used(eng, used, b):
            return eng.If(used > b) if b >= NE else nullcontext()

        def sum_bufs(i):
            return mixT[:, 2 * (i % 4), :], mixT[:, 2 * (i % 4) + 1, :]

        def fin_stat(i):
            return [stat[:, 48 + 4 * (i % 4) + k:49 + 4 * (i % 4) + k] for k in range(4)]

        @block.sync
        def _(sp):
            const = S["consts"]
            sp.dma_start(cst[:, :, :], c_mats.rearrange("p (i c) -> p i c", c=P)).then_inc(S["mats_in"], 16)

            def load_w(t):
                if t >= 4:
                    sp.wait_ge(S["fill_done"], fill_of(t - 4) + 2)
                c0 = tiles[t][0]
                sp.dma_start(wring[:, t % 4], w_in[0, :, c0:c0 + P].rearrange("(k p) c -> p k c", p=P)).then_inc(w_arr[t % 4], 16)

            for i in range(NT):
                if i >= 2:
                    sp.wait_ge(S["x_turned"], 2 * (i - 1))
                sp.dma_start(xs[:, i % 2], x[0, i * P:(i + 1) * P, :]).then_inc(x_in[i % 2], 16)
                if i < 4:
                    load_w(i)
            sp.dma_start(small[:, :], c_small).then_inc(const, 16)
            sp.dma_start(tok[:, :], c_tok).then_inc(const, 16)
            sp.dma_start(mu[:, :], rw_mu.rearrange("o (j p) -> p (o j)", p=P)).then_inc(const, 16)
            sp.dma_start(hot, c_hot).then_inc(const, 16)
            sp.dma_start(relb[:, :], rel_bias).then_inc(const, 16)
            sp.dma_start(lp[:, :, :], da_lambda[0].rearrange("a b -> (a b)").partition_broadcast(P).rearrange("p (a b) -> p a b", a=4)).then_inc(S["consts"], 16)
            sp.dma_start(rbias[:, :], router_b.partition_broadcast(P)).then_inc(S["consts"], 16)
            sp.dma_start(vecs[:, :, 0], rw_vecs[0, :, 0:P].rearrange("v p -> p v")).then_inc(const, 16)
            sp.dma_start(vecs[:, :, 1], rw_vecs[0, :, P:GW].rearrange("v p -> p v")).then_inc(const, 16)
            sp.dma_start(low_up[0:32, :], rw_w_up[0]).then_inc(const, 16)
            sp.dma_start(low_up[32:64, :], rw_a_up[0]).then_inc(const, 16)
            sp.dma_start(low_up[64:128, :], rw_g_up[0]).then_inc(const, 16)
            sp.dma_start(conv[:, :, 0], sc_conv[0, :, 0:P].rearrange("v p -> p v")).then_inc(const, 16)
            sp.dma_start(conv[:, :, 1], sc_conv[0, :, P:GW].rearrange("v p -> p v")).then_inc(const, 16)
            sp.dma_start(rwr[:, :, :], router_w.rearrange("(k p) e -> p k e", p=P)).then_inc(const, 16)
            for h in range(2):
                sp.dma_start(subg[HD * h:HD * h + HD, :], da_subln.rearrange("o p -> p o")).then_inc(const, 16)
            sp.wait_ge(S["x_turned"], 16)
            sp.dma_start(wv[:, :, 0:GW], w_in[0, :, SB0 + 2 * GW:SB0 + 3 * GW].rearrange("(k p) c -> p k c", p=P)).then_inc(wv_in, 16)
            sp.dma_start(wv[:, :, GW:], w_in[0, :, DA0 + 2 * GW:DA0 + 3 * GW].rearrange("(k p) c -> p k c", p=P)).then_inc(wv_in, 16)
            for t in range(4, NTILE):
                if t == 6:
                    sp.wait_ge(S["zeroed"], 1)
                    zeros = vt[:, 0:2, :].rearrange("p a n -> p (a n)").unsqueeze(1).to_broadcast([P, BLOCKS - NE, D])
                    sp.dma_start(y_d[NE * P:, :].rearrange("(b p) n -> p b n", p=P), zeros).then_inc(S["y_zero"], 16)
                    sp.wait_ge(S["bias_evac"], 4)
                    sp.dma_start(bias_d[:, :].rearrange("h (p m) -> p h m", p=P), brows).then_inc(S["bias_st"], 16)
                load_w(t)
            sp.wait_ge(S["bias_st"], 16)
            sp.wait_ge(S["y_zero"], 16)
            sp.wait_ge(S["fill_done"], 2 * V_AT + NT)
            for h in range(4):
                src = bass.AP(bias_d, h * P * LT5 + P - 1, [[LT5 - 1, P], [1, 2 * P]])
                sp.dma_start(t5[:, h, :], src).then_inc(t5_in, 16)
            sp.wait_ge(S["sb_z"], NSB)
            for n, g in enumerate((ln_gain, ln_bias)):
                for l in range(2):
                    sp.dma_start(gb[:, 2 * l + n, :], g[0, l, :].partition_broadcast(P)).then_inc(S["gb_in"], 16)
            sp.wait_ge(S["rw_out"], 1)
            sp.dma_start(wout, w_out[0].rearrange("(k p) n -> p k n", p=P)).then_inc(S["wout_in"], 16)
            sp.wait_ge(S["da_z"], 2 * (NI - NSB))
            for i in range(NT):
                if i >= 2:
                    sp.wait_ge(S["op_sum"], i - 1)
                sp.dma_start(xr[:, i % 2], x[0, i * P:(i + 1) * P, :]).then_inc(xr_in[i % 2], 16)
                if i >= 1:
                    sp.wait_ge(S["x1_ready"], i)
                    sp.dma_start(x1_d[(i - 1) * P:i * P, :], x1[:, i - 1, :]).then_inc(S["x1_st"], 16)
            sp.wait_ge(S["x1_ready"], NT)
            sp.dma_start(x1_d[(NT - 1) * P:, :], x1[:, NT - 1, :]).then_inc(S["x1_st"], 16)
            def load_up(b, e):
                if b >= 2:
                    sp.wait_ge(S["up_done"], b - 1)
                sp.dma_start(weu[b % 2], moe_w_in[0, bass.ds(e, 1), :, :].rearrange("o (k p) n -> p (o k) n", p=P)).then_inc(we_in[b % 2], 16)

            def load_down(b, e):
                if b >= 2:
                    sp.wait_ge(S["down_done"], b - 1)
                sp.dma_start(wed[b % 2], moe_w_down[0, bass.ds(e, 1), :, :].rearrange("o (k p) n -> p (o k) n", p=P)).then_inc(wd_in[b % 2], 16)

            def store_y(b):
                sp.wait_ge(S["y_ev"], 2 * (b + 1))
                sp.dma_start(y_d[b * P:(b + 1) * P, :], yb[b % 2]).then_inc(y_st[b % 2], 16)

            sp.wait_ge(S["op_done"], NT)
            load_up(0, 0)
            load_down(0, 0)
            sp.wait_ge(S["ids_ready"], 1)
            used = used_blocks(sp)
            for b in range(1, BLOCKS):
                with when_used(sp, used, b):
                    e = sp.value_load(ids[0:1, b:b + 1], min_val=0, max_val=NE - 1)
                    load_up(b, e)
                    load_down(b, e)
                if b >= 2:
                    with when_used(sp, used, b - 2):
                        store_y(b - 2)
            for b in (BLOCKS - 2, BLOCKS - 1):
                with when_used(sp, used, b):
                    store_y(b)
            for i in range(NT):
                sp.wait_ge(S["fin_ready"], i + 1)
                sp.dma_start(out[0, i * P:(i + 1) * P, :], x1[:, i, :]).then_inc(S["out_st"], 16)
            sp.wait_ge(S["out_st"], 16 * NT)

        @block.gpsimd
        def _(pool):
            pool.memset(rw[:, :, 0:1], 0.0)
            pool.memset(vt[:, 0:2, :], 0.0)
            pool.memset(ids[:, :], 0).then_inc(S["zeroed"], 1)
            pool.wait_ge(S["zeroed"], 1)
            pool.dma_start(slot_d[:, :].rearrange("(b p) o -> p (b o)", p=P), ids[:, :]).then_inc(S["slot_zero"], 16)
            for m, s in enumerate(rw_order):
                pool.wait_ge(S["fill_evac"], 2 * (m + 1))
                if m >= 4:
                    pool.wait_ge(S["mixed"], m - 3)
                pool.tensor_tensor(mixT[:, m % 4, :], rw[:, s, 0:T], rw[:, s, 1:T + 1], ALU.subtract).then_inc(S["mix_diff"], 1)
            pool.wait_ge(S["fill_evac"], 26)
            for j in range(2):
                pool.tensor_tensor(sc[:, 2 + j, :], sc[:, 2 + j, :], sc[:, 4 + j, :], ALU.mult).then_inc(S["conv_u"], 1)
            for m in range(NT // 2):
                for h in range(2):
                    pool.wait_ge(S["rw_evac"], evacs["dve"][at[m, h, "L"]])
                    idb = C(IDENT).unsqueeze(1).to_broadcast([P, 4, P])
                    cb = cbs[h]
                    pool.tensor_tensor(cb["X"], cb["X"], idb, ALU.add)
                    pool.tensor_tensor(cb["XT"], cb["LT"], C(M1T).unsqueeze(1).to_broadcast([P, 4, P]), ALU.mult).then_inc(S["pchain"], 1)
                    pool.wait_ge(S["pchain"], 2 * m + h + 1)
                    pool.tensor_tensor(cb["XT"], cb["XT"], idb, ALU.add).then_inc(S["rw_init"], 1)
            pool.wait_ge(S["ids_ready"], 1)
            pool.wait_ge(S["slot_zero"], 16)
            for i in range(NT):
                for s in range(2):
                    pool.indirect_dma_start(slot_d[:, :], bass.IndirectOffsetOnAxis(ap=slots[:, s, i:i + 1], axis=0),
                                            tok[:, i:i + 1], None).then_inc(S["slot_sc"], 16)
            pool.wait_ge(S["slot_sc"], 16 * 2 * NT)
            pool.dma_start(slot_tok[:, :], slot_d[:, :].rearrange("(b p) o -> p (b o)", p=P)).then_inc(S["slot_in"], 16)
            pool.wait_ge(S["slot_in"], 16)
            pool.wait_ge(S["x1_st"], 16 * NT)
            used = used_blocks(pool)
            for b in range(BLOCKS):
                with when_used(pool, used, b):
                    if b >= 2:
                        pool.wait_ge(S["xg_t"], b - 1)
                    pool.indirect_dma_start(xg[b % 2], None, x1_d[:, :],
                                            bass.IndirectOffsetOnAxis(ap=slot_tok[:, b:b + 1], axis=0)).then_inc(xg_in[b % 2], 16)
            for b in range(NE - 2, BLOCKS):
                with when_used(pool, used, b):
                    pool.wait_ge(y_st[b % 2], 16 * (b // 2 + 1))

            def token_rows(i):
                if i >= 4:
                    pool.wait_ge(S["fin_stat"], i - 3)
                for s in range(2):
                    pool.indirect_dma_start(sum_bufs(i)[s], None, y_d[:, :],
                                            bass.IndirectOffsetOnAxis(ap=slots[:, s, i:i + 1], axis=0)).then_inc(yg_in[i % 4], 16)

            for i in range(4):
                token_rows(i)
            for i in range(NT):
                if i + 4 < NT:
                    token_rows(i + 4)
                pool.wait_ge(S["fin_gain"], i + 1)
                pool.tensor_tensor(x1[:, i, :], x1[:, i, :], gb[:, 3, :], ALU.add).then_inc(S["fin_ready"], 1)

        @block.scalar
        def _(act):
            nc.scalar.preload_act_table_set("natural_log_exp_and_others")
            A = nc.scalar.activation
            act.wait_ge(S["consts"], 16 * NCONST)
            act.wait_ge(S["lam_prod"], 1)
            A(lam[:, 2:4], lam[:, 0:2], ACT.Exp).then_inc(S["lam_exp"], 1)

            def evac(n):
                kind, t, half = fills[n]
                act.wait_ge(S["fill_done"], n + 1)
                src = bank[4 + n % 4]
                if kind == "v":
                    if t == 0:
                        act.wait_ge(S["y_zero"], 16)
                    A(vt[:, t, :], src, ACT.Copy).then_inc(S["fill_evac"], 1)
                else:
                    if t == V_AT and half == 0:
                        act.wait_ge(S["bias_st"], 16)
                    if n == NFILL - 8:
                        act.wait_ge(S["rwe_done"], 1)
                    A(tiles[t][1][:, half * 512:(half + 1) * 512], src, ACT.Copy, scale=tiles[t][2]).then_inc(S["fill_evac"], 1)

            for n in range(NFILL):
                evac(n)
                if n == 15:
                    act.wait_ge(S["mixed"], 1)
                    A(rw[0:32, 6, 1:T + 1], rw[0:32, 6, 1:T + 1], ACT.Exp, scale=-2.0)
                    A(rw[64:128, 6, 1:T + 1], rw[64:128, 6, 1:T + 1], ACT.Exp, scale=-1.0).then_inc(S["low_exp"], 1)
                if n == 18:
                    act.wait_ge(S["mixed"], 7)
                    for a in range(12):
                        what, j, half = a // 4, a // 2 % 2, a % 2
                        act.wait_ge(S["aux_done"], a + 1)
                        dst = (M01, M23, M67)[what][:, j, half * 512:(half + 1) * 512]
                        if what < 2:
                            A(dst, bank[a % 4], ACT.Exp, bias=stat[:, 2 * what + j:2 * what + j + 1], scale=-1.0).then_inc(S["aux_evac"], 1)
                        else:
                            A(dst, bank[a % 4], ACT.Copy).then_inc(S["aux_evac"], 1)
                if n == 29:
                    act.wait_ge(S["aux_devac"], 4)
                    A(S2, S2, ACT.Ln).then_inc(S["ln_done"], 1)
                    act.wait_ge(S["ln_done"], 1)
                    A(S2, S2, ACT.Exp, scale=-0.5).then_inc(S["kk_scale"], 1)
                if n == 28:
                    act.wait_ge(S["decay_ready"], 1)
                    A(D2, D1, ACT.Exp, scale=DECAY)
                    A(M01, M01, ACT.Exp, scale=-DECAY)
                    A(dfac[:, :, :], dfac[:, :, :], ACT.Exp, scale=-DECAY).then_inc(S["achain"], 1)
                    act.wait_ge(S["achain"], 1)
                    A(D1, D1, ACT.Exp, scale=-DECAY).then_inc(S["decays"], 1)

            links = [1]

            def soft(it):
                n, p = (items[it][1] + 1) * P, it % 2
                act.wait_ge(S["sb_z"], it + 1)
                if it >= 2:
                    act.wait_ge(S["sb_log"], it - 1)
                A(bufE[p][:, 0:n], pz[p][:, 0:n], ACT.Abs).then_inc(S["achain"], 1)
                links[0] += 2
                act.wait_ge(S["achain"], links[0] - 1)
                A(bufE[p][:, 0:n], bufE[p][:, 0:n], ACT.Exp, scale=-1.0).then_inc(S["achain"], 1)
                act.wait_ge(S["achain"], links[0])
                A(bufE[p][:, 0:n], bufE[p][:, 0:n], ACT.Ln, bias=1.0).then_inc(S["sb_soft"], 1)

            def probs(it, m):
                _, i, _ = items[it]
                n, p = (i + 1) * P, it % 2
                act.wait_ge(S["da_max"], 2 * (it - NSB) + m + 1)
                act.wait_ge(S["at_t"], turn_at[it - 1])
                A((bufS, bufE)[m][p][:, 0:n], da_logits(it, m), ACT.Exp, bias=stat[:, 16 + 4 * p + m:17 + 4 * p + m],
                  accum_out=stat[:, 18 + 4 * p + m:19 + 4 * p + m]).then_inc(S["da_prob"], 1)

            def turned_act(it, part):
                i, p = items[it][1], it % 2
                act.wait_ge(S["at_t"], turn_at[it] + part + 1)
                if it >= 2:
                    act.wait_ge(S["at_o"], it - 1)
                k0, k1 = 4 * part, min(i + 1, 4 * part + 4)
                A(bufT[p][:, k0:k1, :], bank[4][:, 0:(k1 - k0) * P].rearrange("p (k t) -> p k t", t=P), ACT.Copy).then_inc(S["at_wT"], 1)

            def rw_copy(g):
                m, h, key = rw_fills[g]
                b, lo, hi = cbs[h], HD * h, HD * h + HD
                src = bank[6 + g % 2].rearrange("p (q c) -> p q c", q=4)
                act.wait_ge(S["rw_fill"], g + 1)
                if key in ("Ta", "Tb", "Tk", "Tv"):
                    A(tm[key[1]], src, ACT.Copy).then_inc(S["rw_copied"], 1)
                elif key == "AkV":
                    A(b["AkV"], bank[6 + g % 2][:, 0:4 * HD].rearrange("p (q c) -> p q c", q=4), ACT.Copy).then_inc(S["rw_copied"], 1)
                elif key == "U":
                    A(b["U"], src, ACT.Copy).then_inc(S["rw_copied"], 1)
                else:
                    for n2 in range(2):
                        c0 = (2 * m + n2) * P
                        last = A(rV[lo:hi, :, c0:c0 + P], src[lo:hi, 2 * n2:2 * n2 + 2, :], ACT.Copy)
                    last.then_inc(S["rw_copied"], 1)

            def rw_norm_act():
                for q in range(4):
                    j, half = q // 2, q % 2
                    act.wait_ge(S["centred"], q + 1)
                    A(S1[:, j, half * 512:(half + 1) * 512], rV[:, j, half * 512:(half + 1) * 512], ACT.Square).then_inc(S["squared"], 1)
                for q in range(4):
                    j, half = q // 2, q % 2
                    act.wait_ge(S["var_done"], q + 1)
                    a = A(S2[:, j, half * 512:(half + 1) * 512], bank[6 + q % 2], ACT.Ln, bias=small[:, 33:34])
                    a.then_inc(S["rw_vevac"], 1)
                act.wait_ge(S["rw_vevac"], 4)
                A(S2, S2, ACT.Exp, scale=-0.5).then_inc(S["rw_rstd"], 1)

            for step, *which in plan["act"]:
                if step == "a":
                    soft(*which)
                elif step == "e":
                    it, = which
                    n, p = (items[it][1] + 1) * P, it % 2
                    act.wait_ge(S["sb_log"], it + 1)
                    A(bufS[p][:, 0:n], bufS[p][:, 0:n], ACT.Exp).then_inc(S["sb_w"], 1)
                elif step == "p":
                    probs(*which)
                elif step == "ct":
                    turned_act(*which)
                elif step == "rwe":
                    rw_copy(*which)
                elif step == "rwpost":
                    rw_norm_act()
            act.wait_ge(S["at_evac"], NI)
            A(PT, M23, ACT.Square).then_inc(S["da_sq"], 1)
            for q in range(4):
                j, half = q // 2, q % 2
                act.wait_ge(S["da_ms"], q + 1)
                a = A(PT2[:, j, half * 512:(half + 1) * 512], bank[q], ACT.Ln, bias=small[:, 34:35])
            a.then_inc(S["ln_done"], 1)
            act.wait_ge(S["ln_done"], 2)
            A(PT2, PT2, ACT.Exp, scale=-0.5).then_inc(S["da_rstd"], 1)

            def row_scale(n):
                act.wait_ge(S["var_ready"], n + 1)
                A(stat[:, 14:15], stat[:, 13:14], ACT.Ln, bias=small[:, 34:35]).then_inc(S["ln_done"], 1)
                act.wait_ge(S["ln_done"], n + 3)
                A(stat[:, 14:15], stat[:, 14:15], ACT.Exp, scale=-0.5).then_inc(S["row_rstd"], 1)

            row_scale(0)
            for i in range(NT):
                if i + 1 < NT:
                    row_scale(i + 1)
                act.wait_ge(S["x1_t"], i + 1)
                if i >= 1:
                    act.wait_ge(S["rl_done"], i)
                for c in range(2):
                    a = A(x1T[:, 4 * c:4 * c + 4, :], bank[4 + c].rearrange("p (k t) -> p k t", t=P), ACT.Copy)
                a.then_inc(S["x1_tev"], 1)
                act.wait_ge(S["rl_done"], i + 1)
                A(rl[:, i, :], bank[6][:, 0:NE], ACT.Exp, scale=-1.0).then_inc(S["rl_ev"], 1)

            def xg_copy(b):
                act.wait_ge(S["xg_t"], b + 1)
                if b >= 2:
                    act.wait_ge(S["up_done"], b - 1)
                for c in range(2):
                    a = A(xgT[b % 2][:, 4 * c:4 * c + 4, :], bank[c].rearrange("p (k t) -> p k t", t=P), ACT.Copy)
                a.then_inc(S["xg_tev"], 1)

            def gate_exp(b):
                act.wait_ge(S["up_done"], b + 1)
                A(eb[b % 2], bank[4 + b % 2][:, 0:FE], ACT.Exp, scale=-1.0).then_inc(S["exp_g"], 1)

            act.wait_ge(S["ids_ready"], 1)
            used = used_blocks(act)
            xg_copy(0)
            for b in range(BLOCKS):
                with when_used(act, used, b):
                    gate_exp(b)
                if b + 1 < BLOCKS:
                    with when_used(act, used, b + 1):
                        xg_copy(b + 1)
                with when_used(act, used, b):
                    act.wait_ge(S["h_t"], b + 1)
                    A(hTb[b % 2], bank[6][:, 0:FE].rearrange("p (k t) -> p k t", t=P), ACT.Copy).then_inc(S["h_tev"], 1)
                    act.wait_ge(S["down_done"], b + 1)
                    if b >= 2:
                        act.wait_ge(y_st[b % 2], 16 * (b // 2))
                    A(yb[b % 2][:, 0:512], bank[2], ACT.Copy).then_inc(S["y_ev"], 1)

            def scale_rows(i):
                act.wait_ge(yg_in[i % 4], 32 * (i // 4 + 1))
                ya, _ = sum_bufs(i)
                A(ya, ya, ACT.Copy, scale=gates[:, 0, i:i + 1]).then_inc(S["y_scaled"], 1)

            def normalise(i):
                mean, var, minus, rstd = fin_stat(i)
                act.wait_ge(S["fin_stat"], i + 1)
                A(rstd, var, ACT.Ln, bias=small[:, 34:35]).then_inc(S["achain"], 1)
                act.wait_ge(S["achain"], links[0] + 1)
                A(rstd, rstd, ACT.Exp, scale=-0.5).then_inc(S["achain"], 1)
                act.wait_ge(S["achain"], links[0] + 2)
                A(var, minus, ACT.Copy, scale=rstd).then_inc(S["achain"], 1)
                links[0] += 3
                act.wait_ge(S["achain"], links[0])
                A(x1[:, i, :], x1[:, i, :], ACT.Identity, bias=var, scale=rstd).then_inc(S["fin_norm"], 1)

            scale_rows(0)
            for i in range(NT):
                if i + 1 < NT:
                    scale_rows(i + 1)
                normalise(i)

        @block.vector
        def _(v):
            V = nc.vector
            chain = [0]

            def link(ins):
                chain[0] += 1
                ins.then_inc(S["vchain"], 1)
                v.wait_ge(S["vchain"], chain[0])

            TT, TS, STT = V.tensor_tensor, V.tensor_scalar, V.scalar_tensor_tensor

            def sigmoid(a):
                link(TS(a, a, 1.0, None, ALU.add))
                return V.reciprocal(a, a)

            for n in range(16):
                i, c = n // 2, n % 2
                v.wait_ge(S["x_turned"], n + 1)
                V.tensor_copy(xT[:, 4 * c:4 * c + 4, i * P:(i + 1) * P], bank[n % 4].rearrange("p (k t) -> p k t", t=P)).then_inc(S["xT_ready"], 1)
            v.wait_ge(S["consts"], 16 * NCONST)
            link(V.memset(bias_l, 1.0))
            V.tensor_copy(bias_l[0:BUCKETS], relb[:, :].unsqueeze(2).to_broadcast([BUCKETS, 4, P])).then_inc(S["bias_up"], 1)
            link(TT(lp[:, 0:3:2, :], lp[:, 0:3:2, :], lp[:, 1:4:2, :], ALU.mult))
            V.tensor_reduce(lam[:, 0:2], lp[:, 0:3:2, :], AX.X, ALU.add).then_inc(S["lam_prod"], 1)
            v.wait_ge(S["lam_exp"], 1)
            link(TT(lam[:, 4:5], lam[:, 3:4], lam[:, 2:3], ALU.subtract))
            link(TS(lam[:, 4:5], lam[:, 4:5], -LAM_INIT, None, ALU.add))
            for w in range(2):
                TS(stat[:, 2 * w:2 * w + 2], vecs[:, w, :], -1.0, None, ALU.mult)
            link(TS(stat[:, 4:6], vecs[:, 3, :], -1.0, 1.0, ALU.mult, ALU.add))
            link(TS(subg[:, :], subg[:, :], 1.0 - LAM_INIT, None, ALU.mult))
            for h in range(4):
                v.wait_ge(S["bias_rows"], h + 1)
                V.tensor_copy(stat[:, 8 + h:9 + h], bank[h][:, 0:1]).then_inc(S["bias_far"], 1)
                v.wait_ge(S["bias_far"], h + 1)
                TS(brows[:, h, :], bank[h][:, 0:LT5], stat[:, 8 + h:9 + h], None, ALU.subtract).then_inc(S["bias_evac"], 1)
            for m, s in enumerate(rw_order):
                v.wait_ge(S["mix_diff"], m + 1)
                STT(rw[:, s, 1:T + 1], mixT[:, m % 4, :], mu[:, s:s + 1], rw[:, s, 1:T + 1], ALU.mult, ALU.add).then_inc(S["mixed"], 1)
            v.wait_ge(S["low_exp"], 1)
            for lo, hi in ((0, 32), (64, 128)):
                last = sigmoid(rw[lo:hi, 6, 1:T + 1])
            link(last)
            TS(rw[0:32, 6, 1:T + 1], rw[0:32, 6, 1:T + 1], 2.0, -1.0, ALU.mult, ALU.add).then_inc(S["low_ready"], 1)
            v.wait_ge(S["aux_evac"], 4)
            link(sigmoid(M01))
            for j in range(2):
                for n in range(NT):
                    last = V.tensor_tensor_scan(D1[:, j, n * P:(n + 1) * P], C(ONES), M01[:, j, n * P:(n + 1) * P], 0.0, ALU.mult, ALU.add)
            link(last)
            d1c = D1.rearrange("p j (n c) -> p j n c", c=P)
            V.tensor_copy(smid[:, :, :], d1c[:, :, :, HD - 1])
            link(V.tensor_copy(dfac[:, :, :], d1c[:, :, :, P - 1]))
            link(TT(dfac[:, :, :], dfac[:, :, :], smid[:, :, :], ALU.subtract))
            link(TT(dfac[:, :, 0:NT - 1], dfac[:, :, 0:NT - 1], smid[:, :, 1:NT], ALU.add))
            for j in range(2):
                last = TT(D1[:, j, :].rearrange("p (n c) -> p n c", c=P), D1[:, j, :].rearrange("p (n c) -> p n c", c=P),
                          smid[:, j, :].unsqueeze(2).to_broadcast([P, NT, P]), ALU.subtract)
            link(last)
            TT(M01, D1, M01, ALU.subtract).then_inc(S["decay_ready"], 1)
            v.wait_ge(S["aux_evac"], 8)
            sigmoid(M23)
            v.wait_ge(S["conv_u"], 2)
            for j in range(2):
                y, u = mixT[:, 4 + j, :], sc[:, 2 + j, :]
                link(TS(y, u, conv[:, 2, j:j + 1], None, ALU.mult))
                link(STT(y[:, 1:], u[:, 0:T - 1], conv[:, 1, j:j + 1], y[:, 1:], ALU.mult, ALU.add))
                link(STT(y[:, 2:], u[:, 0:T - 2], conv[:, 0, j:j + 1], y[:, 2:], ALU.mult, ALU.add))
                link(TT(y, y, sc[:, j, :], ALU.mult))
            for j in range(2):
                last = TS(S1[:, j, :], rK[:, j, :], vecs[:, 2, j:j + 1], None, ALU.mult)
            link(last)
            TT(S2, S1, S1, ALU.mult).then_inc(S["sq_ready"], 1)
            for q in range(4):
                j, half = q // 2, q % 2
                v.wait_ge(S["aux_done"], 12 + q + 1)
                TS(S2[:, j, half * 512:(half + 1) * 512], bank[q], 1e-24, None, ALU.max).then_inc(S["aux_devac"], 1)
            v.wait_ge(S["kk_scale"], 1)
            link(TT(S1, S1, S2, ALU.mult))
            link(TT(S2, S1, M23, ALU.mult))
            for j in range(2):
                last = TS(M23[:, j, :], M23[:, j, :], vecs[:, 3, j:j + 1], stat[:, 4 + j:5 + j], ALU.mult, ALU.add)
            link(last)
            link(TT(rK, rK, M23, ALU.mult))
            for j in range(2):
                last = STT(S3[:, j, :], rR[:, j, :], vecs[:, 4, j:j + 1], rK[:, j, :], ALU.mult, ALU.mult)
            last.then_inc(S["bonus_ready"], 1)
            v.wait_ge(S["bonus_ready"], 1)
            v.wait_ge(S["decays"], 1)
            TT(S2, S2, D2, ALU.mult)
            TT(rK, rK, D2, ALU.mult)
            TT(rR, rR, D1, ALU.mult)
            for j in range(2):
                last = STT(S1[:, j, :], S1[:, j, :], -1.0, M01[:, j, :], ALU.mult, ALU.mult)
            last.then_inc(S["rwe_done"], 1)
            for q in range(4):
                j, half = q // 2, q % 2
                v.wait_ge(S["aux_done"], 16 + q + 1)
                h_ = slice(half * 512, (half + 1) * 512)
                TT(S3[:, j, h_], bank[q], rV[:, j, h_], ALU.mult).then_inc(S["aux_devac"], 1)

            v.wait_ge(S["fill_done"], NFILL)
            def bc(i):
                return C(i).unsqueeze(1).to_broadcast([P, 4, P])

            def rw_ev(g):
                m, h, key = rw_fills[g]
                b, lo, hi = cbs[h], HD * h, HD * h + HD
                src = bank[6 + g % 2].rearrange("p (q c) -> p q c", q=4)
                v.wait_ge(S["rw_fill"], g + 1)
                done = S["rw_evac"]
                if key == "LT":
                    TT(b["LT"], src, bc(SU), ALU.mult).then_inc(done, 1)
                elif key == "L":
                    TT(b["X"], src, bc(M1), ALU.mult).then_inc(done, 1)
                elif key in ("RbT", "AkT", "RkT"):
                    TT(b[key], src, bc(SU if key == "AkT" else UI), ALU.mult).then_inc(done, 1)
                elif key[0] == "W":
                    TT(b["W"], src, bc(MB + int(key[1])), ALU.mult).then_inc(done, 1)
                elif key[0] == "X":
                    if key == "X0":
                        v.wait_ge(S["rw_init"], 2 * m + h + 1)
                    x_ = b["XT" if key[1] == "T" else "X"]
                    TT(x_, x_, src, ALU.add).then_inc(done, 1)
                elif key == "RP":
                    for n2 in range(2):
                        c0 = (2 * m + n2) * P
                        last = TT(b["RP"][lo:hi, 2 * n2:2 * n2 + 2, :], src[lo:hi, 2 * n2:2 * n2 + 2, :], rR[lo:hi, :, c0:c0 + P], ALU.add)
                    last.then_inc(done, 1)
                elif key == "NG":
                    for n2 in range(2):
                        d = dfac[lo:hi, :, 2 * m + n2:2 * m + n2 + 1].to_broadcast([HD, 2, HD])
                        TT(b["NG"][lo:hi, 2 * n2:2 * n2 + 2, 0:HD], src[lo:hi, 2 * n2:2 * n2 + 2, 0:HD], d, ALU.mult)
                    TT(b["NG"][lo:hi, :, HD:P], src[lo:hi, :, HD:P], C(IDENT)[lo:hi, lo:hi].unsqueeze(1).to_broadcast([HD, 4, HD]), ALU.add).then_inc(done, 1)
                else:
                    n2 = int(key[1])
                    n = 2 * m + n2
                    v.wait_ge(done, evacs["dve"][g] - 1)
                    if n + 1 < NT:
                        for j in range(2):
                            last = STT(st[lo:hi, j, n + 1, :], src[lo:hi, j, 0:HD], dfac[lo:hi, j, n:n + 1], b["NG"][lo:hi, 2 * n2 + j, 0:HD], ALU.mult, ALU.add)
                        last.then_inc(done, 1)

            def rw_norm():
                v.wait_ge(S["rw_evac"], evacs["dve"][NRW - 1])
                v.wait_ge(S["rw_copied"], evacs["act"][NRW - 1])
                for q in range(4):
                    j, half = q // 2, q % 2
                    h_ = slice(half * 512, (half + 1) * 512)
                    v.wait_ge(S["mean_done"], q + 1)
                    TT(rV[:, j, h_], rV[:, j, h_], bank[6 + q % 2], ALU.subtract).then_inc(S["centred"], 1)
                v.wait_ge(S["rw_rstd"], 1)
                link(TT(rV, rV, S2, ALU.mult))
                for j in range(2):
                    last = TS(rV[:, j, :], rV[:, j, :], vecs[:, 5, j:j + 1], vecs[:, 6, j:j + 1], ALU.mult, ALU.add)
                link(last)
                link(TT(rV, rV, S3, ALU.add))
                TT(M67, rV, M67, ALU.mult).then_inc(S["rw_out"], 1)

            def stick(it, step):
                _, i, hh = items[it]
                n, p, q0 = (i + 1) * P, it % 2, i * P
                if step == "l1":
                    v.wait_ge(S["sb_soft"], it + 1)
                    if it >= 2:
                        v.wait_ge(S["at_t"], turn_at[it - 1])
                    link(STT(bufS[p][:, 0:n], pz[p][:, 0:n], 0.0, bufE[p][:, 0:n], ALU.max, ALU.add))
                    link(TT(bufS[p][:, q0:n], bufS[p][:, q0:n], C(SL), ALU.mult))
                elif step == "l2":
                    rev = slice(n - 1, None, -1)
                    link(V.tensor_tensor_scan(bufE[p][:, rev], cst[:, ONES, 0:1].to_broadcast([P, n]), bufS[p][:, rev], 0.0, ALU.mult, ALU.add))
                else:
                    link(TT(bufS[p][:, 0:n], pz[p][:, 0:n], bufE[p][:, 0:n], ALU.subtract))
                    TT(bufS[p][:, q0:n], bufS[p][:, q0:n], C(NEGD), ALU.add).then_inc(S["sb_log"], 1)

            def logits(it, m):
                _, i, hh = items[it]
                n, p = (i + 1) * P, it % 2
                near = min(n, 2 * P)
                z = da_logits(it, m)
                if it == NSB and m == 0:
                    v.wait_ge(t5_in, 64)
                v.wait_ge(S["da_z"], 2 * (it - NSB) + m + 1)
                link(TT(z[:, n - near:n], z[:, n - near:n], t5[:, hh, 2 * P - near:2 * P], ALU.add))
                V.tensor_reduce(stat[:, 16 + 4 * p + m:17 + 4 * p + m], z, AX.X, ALU.max, negate=True).then_inc(S["da_max"], 1)

            def combine(it, step):
                _, i, hh = items[it]
                n, p = (i + 1) * P, it % 2
                r = stat[:, 40 + 4 * p:44 + 4 * p]
                if step == "c1":
                    v.wait_ge(S["da_prob"], 2 * (it - NSB) + 2)
                    link(V.reciprocal(r[:, 0:2], stat[:, 18 + 4 * p:20 + 4 * p]))
                    link(TT(r[:, 2:3], r[:, 1:2], lam[:, 4:5], ALU.mult))
                    link(TS(bufS[p][:, 0:n], bufS[p][:, 0:n], r[:, 0:1], None, ALU.mult))
                else:
                    STT(bufS[p][:, 0:n], bufE[p][:, 0:n], r[:, 2:3], bufS[p][:, 0:n], ALU.mult, ALU.add).then_inc(S["da_attn"], 1)

            link(V.memset(st[:, :, 0, :], 0.0))
            for step, *which in plan["dve"]:
                if step == "rwe":
                    rw_ev(*which)
                elif step == "rwpost":
                    rw_norm()
                elif step in ("l1", "l2", "l3"):
                    stick(*which, step)
                elif step in ("c1", "c2"):
                    combine(*which, step)
                elif step == "x":
                    logits(*which)
                elif step == "o":
                    it, = which
                    kind, i, hh = items[it]
                    h, j = hh % 2, hh // 2
                    v.wait_ge(S["at_o"], it + 1)
                    V.tensor_copy(mixT[HD * h:HD * h + HD, j + (2 if kind == "da" else 0), i * P:(i + 1) * P],
                                  bank[5][HD * h:HD * h + HD, (it % 4) * P:(it % 4 + 1) * P]).then_inc(S["at_evac"], 1)
            v.wait_ge(S["da_rstd"], 1)
            for j in range(2):
                last = STT(M23[:, j, :], M23[:, j, :], subg[:, 0:1], PT2[:, j, :], ALU.mult, ALU.mult)
            last.then_inc(S["da_done"], 1)

            norms = [0]

            def norm(s, dst, l):
                norms[0] += 1
                bn = stat[:, 0:12].rearrange("p (c k) -> p c k", k=6)
                for c in range(2):
                    last = V.bn_stats(bn[:, c, :], s[:, c * 512:(c + 1) * 512])
                link(last)
                V.bn_aggr(stat[:, 12:14], bn).then_inc(S["var_ready"], 1)
                v.wait_ge(S["row_rstd"], norms[0])
                link(TS(s, s, stat[:, 12:13], stat[:, 14:15], ALU.subtract, ALU.mult))
                link(TT(s, s, gb[:, 2 * l, :], ALU.mult))
                return TT(dst, s, gb[:, 2 * l + 1, :], ALU.add)

            v.wait_ge(S["gb_in"], 64)
            for i in range(NT):
                v.wait_ge(S["op_done"], i + 1)
                v.wait_ge(xr_in[i % 2], 16 * (i // 2 + 1))
                s = x1[:, i, :]
                last = STT(s, xr[:, i % 2, :], ALPHA, pz[i % 2][:, :], ALU.mult, ALU.add)
                last.then_inc(S["op_sum"], 1)
                v.wait_ge(S["op_sum"], i + 1)
                norm(s, s, 0).then_inc(S["x1_ready"], 1)

            v.wait_ge(S["rl_ev"], NT)

            def r3(n):
                return rt[:, n * 128:(n + 1) * 128].rearrange("p (i e) -> p i e", i=NT)

            aff, sel, rk, cmb, pos, tmp = r3(0), r3(1), r3(2), r3(3), r3(4), r3(5)
            gs, tq = rt2[:, 0:32], [rt2[:, 32 * (k + 1):32 * (k + 2)] for k in range(6)]
            cmp_, grk = rt2[:, 224:256], rt2[:, 256:288]
            link(TS(rl, rl, 1.0, None, ALU.add))
            link(V.reciprocal(aff, rl))
            link(TT(sel, aff, rbias[:, :].unsqueeze(1).to_broadcast([P, NT, NE]), ALU.add))
            s4 = sel.rearrange("p i (g j) -> p (i g) j", j=EPG)
            TT(tq[0], s4[:, :, 0], s4[:, :, 1], ALU.max)
            TT(tq[1], s4[:, :, 0], s4[:, :, 1], ALU.min)
            TT(tq[2], s4[:, :, 2], s4[:, :, 3], ALU.max)
            link(TT(tq[3], s4[:, :, 2], s4[:, :, 3], ALU.min))
            TT(gs, tq[0], tq[2], ALU.max)
            TT(tq[4], tq[0], tq[2], ALU.min)
            link(TT(tq[5], tq[1], tq[3], ALU.max))
            link(TT(tq[4], tq[4], tq[5], ALU.max))
            link(TT(gs, gs, tq[4], ALU.add))

            def ranks(val, rank, n):
                for j in range(EPG):
                    last = V.memset(rank[:, :, j], float(EPG - 1 - j))
                link(last)
                for a in range(EPG):
                    for b in range(a + 1, EPG):
                        link(TT(cmp_[:, 0:n], val[:, :, a], val[:, :, b], ALU.is_ge))
                        TT(rank[:, :, b], rank[:, :, b], cmp_[:, 0:n], ALU.add)
                        link(TT(rank[:, :, a], rank[:, :, a], cmp_[:, 0:n], ALU.subtract))

            rk4 = rk.rearrange("p i (g j) -> p (i g) j", j=EPG)
            ranks(s4, rk4, 32)
            ranks(gs.rearrange("p (i g) -> p i g", g=EPG), grk.rearrange("p (i g) -> p i g", g=EPG), NT)
            link(TS(rk, rk, 2.0, None, ALU.is_lt))
            link(TS(grk, grk, 1.0, None, ALU.is_lt))
            TT(rk4, rk4, grk.unsqueeze(2).to_broadcast([P, 32, EPG]), ALU.mult).then_inc(S["route_sel"], 1)
            v.wait_ge(S["route_sel"], 1)
            link(TT(cmb, aff, rk, ALU.mult))
            den = rt2[:, 320:328]
            link(V.tensor_reduce(den, cmb, AX.X, ALU.add))
            link(V.reciprocal(den, den))
            v.wait_ge(S["cnt_done"], 1)
            tot = bank[1][:, 0:128].rearrange("p (i e) -> p i e", i=NT)
            toff = tmp
            link(V.memset(toff[:, 0, :], 0.0))
            for i in range(NT - 1):
                link(TT(toff[:, i + 1, :], toff[:, i, :], tot[:, i, :], ALU.add))
            cnt, nb, ends, starts = (rt2[:, 336 + 16 * k:352 + 16 * k] for k in range(4))
            link(TT(cnt, toff[:, NT - 1, :], tot[:, NT - 1, :], ALU.add))
            link(V.memset(nb, 1.0))
            for j in range(1, NT):
                link(STT(nb, cnt, float(P * j), nb, ALU.is_gt, ALU.add))
            link(V.tensor_tensor_scan(ends, cst[:, ONES, 0:NE], nb, 0.0, ALU.mult, ALU.add))
            link(TT(starts, ends, nb, ALU.subtract))
            link(TS(starts, starts, float(P), 1.0, ALU.mult, ALU.add))
            link(TT(pos, toff, bank[0][:, 0:128].rearrange("p (i e) -> p i e", i=NT), ALU.add))
            link(TT(pos, pos, starts.unsqueeze(1).to_broadcast([P, NT, NE]), ALU.add))
            link(TT(pos, pos, rk, ALU.mult))
            hi, lo = rt2[:, 400:408], rt2[:, 408:416]
            V.tensor_reduce(hi, pos, AX.X, ALU.max)
            link(V.tensor_reduce(lo, pos, AX.X, ALU.add))
            link(TT(lo, lo, hi, ALU.subtract))
            for s, w in enumerate((hi, lo)):
                link(TT(tmp, pos, w.unsqueeze(2).to_broadcast([P, NT, NE]), ALU.is_equal))
                link(TT(tmp, tmp, cmb, ALU.mult))
                link(V.tensor_reduce(gates[:, s, :], tmp, AX.X, ALU.add))
                link(TT(gates[:, s, :], gates[:, s, :], den, ALU.mult))
                link(TS(w, w, -1.0, None, ALU.add))
                V.tensor_copy(slots[:, s, :], w)
            eh = mixT[:, 7, 0:NBP * NE].rearrange("p (b e) -> p b e", b=NBP)
            v.wait_ge(S["op_done"], NT)
            link(TT(eh, small[:, 0:NBP].unsqueeze(2).to_broadcast([P, NBP, NE]), ends.unsqueeze(1).to_broadcast([P, NBP, NE]), ALU.is_ge))
            ef = rt2[:, 416:448]
            link(V.tensor_reduce(ef, eh, AX.X, ALU.add))
            link(TS(ef, ef, float(NE - 1), None, ALU.min))
            link(V.tensor_copy(ef[:, NBP - 1:NBP], ends[:, NE - 1:NE]))
            v.wait_ge(S["slot_zero"], 16)
            V.tensor_copy(ids[:, :], ef).then_inc(S["ids_ready"], 1)

            def gated(b):
                v.wait_ge(S["exp_g"], b + 1)
                g, e, h = bank[4 + b % 2], eb[b % 2], hb[b % 2]
                if b >= 2:
                    v.wait_ge(S["h_t"], b - 1)
                TS(e, e, 1.0, None, ALU.add).then_inc(S["gate_step"], 1)
                v.wait_ge(S["gate_step"], 3 * b + 1)
                V.reciprocal(e, e).then_inc(S["gate_step"], 1)
                v.wait_ge(S["gate_step"], 3 * b + 2)
                TT(e, e, g[:, 0:FE], ALU.mult).then_inc(S["gate_step"], 1)
                v.wait_ge(S["gate_step"], 3 * b + 3)
                TT(h, e, g[:, FE:2 * FE], ALU.mult).then_inc(S["gated"], 1)

            v.wait_ge(S["ids_ready"], 1)
            used = used_blocks(v)
            gated(0)
            for b in range(BLOCKS):
                if b + 1 < BLOCKS:
                    with when_used(v, used, b + 1):
                        gated(b + 1)
                with when_used(v, used, b):
                    v.wait_ge(S["down_done"], b + 1)
                    if b >= 2:
                        v.wait_ge(y_st[b % 2], 16 * (b // 2))
                    V.tensor_copy(yb[b % 2][:, 512:1024], bank[3]).then_inc(S["y_ev"], 1)

            def gain(i):
                v.wait_ge(S["fin_norm"], i + 1)
                TT(x1[:, i, :], x1[:, i, :], gb[:, 2, :], ALU.mult).then_inc(S["fin_gain"], 1)

            for i in range(NT):
                v.wait_ge(S["y_scaled"], i + 1)
                ya, yb2 = sum_bufs(i)
                s = x1[:, i, :]
                link(STT(ya, yb2, gates[:, 1, i:i + 1], ya, ALU.mult, ALU.add))
                link(STT(s, s, ALPHA, ya, ALU.mult, ALU.add))
                bn = stat[:, 0:12].rearrange("p (c k) -> p c k", k=6)
                for c in range(2):
                    last = V.bn_stats(bn[:, c, :], s[:, c * 512:(c + 1) * 512])
                link(last)
                mean, _, minus, _ = fin_stat(i)
                link(V.bn_aggr(stat[:, 48 + 4 * (i % 4):50 + 4 * (i % 4)], bn))
                TS(minus, mean, -1.0, None, ALU.mult).then_inc(S["fin_stat"], 1)
                if i >= 1:
                    gain(i - 1)
            gain(NT - 1)

        @block.tensor
        def _(pe):
            MM = nc.tensor.matmul

            def turn(o, i):
                return nc.tensor.transpose(o, i, C(IDENT))

            pe.wait_ge(S["mats_in"], 16)
            for n in range(16):
                i, c = n // 2, n % 2
                if c == 0:
                    pe.wait_ge(x_in[i % 2], 16 * (i // 2 + 1))
                if n >= 4:
                    pe.wait_ge(S["xT_ready"], n - 3)
                for k in range(4):
                    last = turn(bank[n % 4][:, k * P:(k + 1) * P], xs[:, i % 2, (4 * c + k) * P:(4 * c + k + 1) * P])
                last.then_inc(S["x_turned"], 1)

            def fill(n):
                kind, t, half = fills[n]
                if n >= 4:
                    pe.wait_ge(S["fill_evac"], n - 3)
                o = bank[4 + n % 4]
                if n < 2:
                    pe.wait_ge(S["xT_ready"], 8 * (n + 1))
                if kind == "v":
                    if t == 0:
                        pe.wait_ge(wv_in, 32)
                    for k in range(KD):
                        last = MM(o, xT[:, k, t * P:(t + 1) * P], wv[:, k, :], start=k == 0, stop=k == KD - 1)
                else:
                    if half == 0:
                        pe.wait_ge(w_arr[t % 4], 16 * (t // 4 + 1))
                    for k in range(KD):
                        last = MM(o, wring[:, t % 4, k, :], xT[:, k, half * 512:(half + 1) * 512], start=k == 0, stop=k == KD - 1)
                last.then_inc(S["fill_done"], 1)

            def aux(a):
                j, half = a // 2 % 2, a % 2
                h_ = slice(half * 512, (half + 1) * 512)
                if a < 12:
                    if a >= 4:
                        pe.wait_ge(S["aux_evac"], a - 3)
                    lo, hi = ((0, 32), (32, 64), (64, 128))[a // 4]
                    mm = MM(bank[a % 4], low_up[lo:hi, j * P:(j + 1) * P], rw[lo:hi, 6, 1 + half * 512:1 + (half + 1) * 512], start=True, stop=True)
                elif a < 16:
                    pe.wait_ge(S["aux_evac"], a - 3)
                    mm = MM(bank[a % 4], C(BO), S2[:, j, h_], start=True, stop=True)
                else:
                    pe.wait_ge(S["aux_devac"], a - 15)
                    mm = MM(bank[a % 4], C(BO), S3[:, j, h_], start=True, stop=True)
                mm.then_inc(S["aux_done"], 1)

            for n in range(NFILL):
                fill(n)
                if n == 3:
                    pe.wait_ge(S["bias_up"], 1)
                    pe.wait_ge(S["xT_ready"], 16)
                    for h in range(4):
                        MM(bank[h][:, 0:LT5], bias_l[:, h, :], hot, start=True, stop=True).then_inc(S["bias_rows"], 1)
                if n == 18:
                    pe.wait_ge(S["low_ready"], 1)
                    pe.wait_ge(S["bias_evac"], 4)
                    for a in range(12):
                        aux(a)
                if n == 29:
                    pe.wait_ge(S["sq_ready"], 1)
                    for a in range(12, 16):
                        aux(a)
                if n == 36:
                    pe.wait_ge(S["bonus_ready"], 1)
                    for a in range(16, 20):
                        aux(a)

            pe.wait_ge(S["rwe_done"], 1)
            pe.wait_ge(S["aux_devac"], 8)
            pe.wait_ge(S["fill_evac"], NFILL)

            def rw_pe(g):
                m, h, key = rw_fills[g]
                b, lo, hi = cbs[h], HD * h, HD * h + HD
                ps = bank[6 + g % 2]
                o = ps.rearrange("p (q c) -> p q c", q=4)
                if g >= 2:
                    last = rw_operands(g)
                    if evacs["dve"][last]:
                        pe.wait_ge(S["rw_evac"], evacs["dve"][last])
                    pe.wait_ge(S["rw_copied"], evacs["act"][last])
                if key == "W0":
                    pe.wait_ge(S["rw_init"], 2 * m + h + 1)
                for q in range(4):
                    n2, j = q // 2, q % 2
                    n = 2 * m + n2
                    ck = slice(n * P, (n + 1) * P)
                    a_, b_, k_, r_ = S1[lo:hi, j, ck], S2[lo:hi, j, ck], rK[lo:hi, j, ck], rR[lo:hi, j, ck]
                    if key in ("Ta", "Tb", "Tk", "Tv"):
                        src = {"a": S1, "b": S2, "k": rK, "v": rV}[key[1]][:, j, ck]
                        last = turn(o[:, q, :], src)
                    elif key in ("LT", "L", "RbT", "AkT", "RkT"):
                        l_, m_ = {"LT": (b_, a_), "L": (a_, b_), "RbT": (b_, r_), "AkT": (k_, a_), "RkT": (k_, r_)}[key]
                        last = MM(o[:, q, :], l_, m_, start=True, stop=True)
                    elif key == "AkV":
                        last = MM(ps[:, q * HD:(q + 1) * HD], b["AkT"][:, q, :], tm["v"][:, q, lo:hi], start=True, stop=True)
                    elif key[0] in "WX":
                        l_, m_ = ("LT", "X") if key[0] == "W" else ("W", "XT") if key[1] == "T" else ("XT", "W")
                        last = MM(o[:, q, :], b[l_][:, q, :], b[m_][:, q, :], start=True, stop=True)
                    elif key == "U":
                        MM(o[:, q, 0:HD], b["XT"][:, q, :], tm["a"][:, q, lo:hi], start=True, stop=True)
                        last = MM(o[:, q, HD:P], b["XT"][:, q, :], b["AkV"][:, q, :], start=True, stop=True)
                    elif key == "RP":
                        last = MM(o[lo:hi, q, :], b["U"][:, q, 0:HD], b["RbT"][:, q, :], start=True, stop=True)
                    elif key == "NG":
                        MM(o[lo:hi, q, 0:HD], tm["b"][:, q, lo:hi], b["U"][:, q, HD:P], start=True, stop=False)
                        MM(o[lo:hi, q, 0:HD], tm["k"][:, q, lo:hi], tm["v"][:, q, lo:hi], start=False, stop=True)
                        last = MM(o[lo:hi, q, HD:P], b["U"][:, q, 0:HD], tm["b"][:, q, lo:hi], start=True, stop=True)
                    elif key[0] == "S":
                        if n2 == int(key[1]):
                            last = MM(o[lo:hi, j, 0:HD], b["NG"][lo:hi, q, HD:P], st[lo:hi, j, n, :], start=True, stop=True)
                    else:
                        MM(o[lo:hi, q, :], b["U"][:, q, HD:P], b["RbT"][:, q, :], start=True, stop=False)
                        MM(o[lo:hi, q, :], tm["v"][:, q, lo:hi], b["RkT"][:, q, :], start=False, stop=False)
                        last = MM(o[lo:hi, q, :], st[lo:hi, j, n, :], b["RP"][lo:hi, q, :], start=False, stop=True)
                last.then_inc(S["rw_fill"], 1)

            def rw_stats(_=0):
                pe.wait_ge(S["rw_evac"], evacs["dve"][NRW - 1])
                pe.wait_ge(S["rw_copied"], evacs["act"][NRW - 1])
                for q in range(4):
                    j, half = q // 2, q % 2
                    if q >= 2:
                        pe.wait_ge(S["centred"], q - 1)
                    MM(bank[6 + q % 2], C(BM), rV[:, j, half * 512:(half + 1) * 512], start=True, stop=True).then_inc(S["mean_done"], 1)
                for q in range(4):
                    j, half = q // 2, q % 2
                    pe.wait_ge(S["squared"], q + 1)
                    pe.wait_ge(S["centred"], 4)
                    if q >= 2:
                        pe.wait_ge(S["rw_vevac"], q - 1)
                    MM(bank[6 + q % 2], C(BM), S1[:, j, half * 512:(half + 1) * 512], start=True, stop=True).then_inc(S["var_done"], 1)

            def sb_scores(it):
                _, i, hh = items[it]
                h, j, n, p = hh % 2, hh // 2, (i + 1) * P, it % 2
                if it >= 2:
                    pe.wait_ge(S["sb_log"], it - 1)
                lo = HD * h
                for c in range(0, n, 512):
                    e = min(n, c + 512)
                    last = MM(pz[p][:, c:e], qk[lo:lo + HD, j, i * P:(i + 1) * P], qk[lo:lo + HD, 2 + j, c:e], start=True, stop=True)
                last.then_inc(S["sb_z"], 1)

            def da_scores(it, m):
                _, i, hh = items[it]
                h, j, n = hh % 2, hh // 2, (i + 1) * P
                back = 2 if i < 4 and it - 2 >= NSB else 1
                if it - back < NSB:
                    pe.wait_ge(S["sb_log"], NSB - 1 + m)
                else:
                    pe.wait_ge(S["da_prob"], 2 * (it - back - NSB) + m + 1)
                lo = HD * h + 32 * m
                for c in range(0, n, 512):
                    e = min(n, c + 512)
                    last = MM(da_logits(it, m)[:, c:e], qk[lo:lo + 32, 4 + j, i * P:(i + 1) * P], qk[lo:lo + 32, 6 + j, c:e], start=True, stop=True)
                last.then_inc(S["da_z"], 1)

            def turn_weights(it, part):
                kind, i, hh = items[it]
                p, u = it % 2, turn_at[it] + part
                if part == 0:
                    if kind == "sb":
                        pe.wait_ge(S["sb_w"], it + 1)
                    else:
                        pe.wait_ge(S["da_attn"], it - NSB + 1)
                if u >= 1:
                    pe.wait_ge(S["at_wT"], u)
                for k in range(4 * part, min(i + 1, 4 * part + 4)):
                    last = turn(bank[4][:, (k % 4) * P:(k % 4 + 1) * P], bufS[p][:, k * P:(k + 1) * P])
                last.then_inc(S["at_t"], 1)

            def values(it, part):
                kind, i, hh = items[it]
                h, p = hh % 2, it % 2
                lo, v0 = HD * h, (GW if kind == "da" else 0) + hh * HD
                pe.wait_ge(S["at_wT"], turn_at[it] + part + 1)
                if part == 0 and it >= 4:
                    pe.wait_ge(S["at_evac"], it - 3)
                for k in range(4 * part, min(i + 1, 4 * part + 4)):
                    last = MM(bank[5][lo:lo + HD, (it % 4) * P:(it % 4 + 1) * P], vt[:, k, v0:v0 + HD], bufT[p][:, k, :], start=k == 0, stop=k == i)
                if part == i // 4:
                    last.then_inc(S["at_o"], 1)

            for step, *which in plan["pe"]:
                {"rw": rw_pe, "rwpost": rw_stats, "z": sb_scores, "s": da_scores, "t": turn_weights, "v": values}[step](*which)
            pe.wait_ge(S["da_sq"], 1)
            for q in range(4):
                j, half = q // 2, q % 2
                MM(bank[q], C(BM), PT[:, j, half * 512:(half + 1) * 512], start=True, stop=True).then_inc(S["da_ms"], 1)

            pe.wait_ge(S["wout_in"], 16)
            pe.wait_ge(S["rw_out"], 1)
            pe.wait_ge(S["da_done"], 1)

            def project(i):
                if i >= 2:
                    pe.wait_ge(S["op_sum"], i - 1)
                for c in range(2):
                    for k in range(8):
                        last = MM(pz[i % 2][:, c * 512:(c + 1) * 512], mixT[:, k, i * P:(i + 1) * P], wout[:, k, c * 512:(c + 1) * 512], start=k == 0, stop=k == 7)
                last.then_inc(S["op_done"], 1)

            def router(i):
                pe.wait_ge(S["x1_ready"], i + 1)
                if i >= 1:
                    pe.wait_ge(S["x1_tev"], i)
                for k in range(KD):
                    last = turn(bank[4 + k // 4][:, (k % 4) * P:(k % 4 + 1) * P], x1[:, i, k * P:(k + 1) * P])
                last.then_inc(S["x1_t"], 1)
                pe.wait_ge(S["x1_tev"], i + 1)
                if i >= 1:
                    pe.wait_ge(S["rl_ev"], i)
                for k in range(KD):
                    last = MM(bank[6][:, 0:NE], x1T[:, k, :], rwr[:, k, :], start=k == 0, stop=k == KD - 1)
                last.then_inc(S["rl_done"], 1)

            project(0)
            project(1)
            for i in range(NT):
                if i + 2 < NT:
                    project(i + 2)
                router(i)
            pe.wait_ge(S["route_sel"], 1)
            selm = rt[:, 256:384]
            MM(bank[0][:, 0:128], C(SU), selm, start=True, stop=True)
            MM(bank[1][:, 0:128], C(ONES), selm, start=True, stop=True).then_inc(S["cnt_done"], 1)

            def gather_turn(b):
                pe.wait_ge(xg_in[b % 2], 16 * (b // 2 + 1))
                if b >= 1:
                    pe.wait_ge(S["xg_tev"], b)
                for k in range(KD):
                    last = turn(bank[k // 4][:, (k % 4) * P:(k % 4 + 1) * P], xg[b % 2][:, k * P:(k + 1) * P])
                last.then_inc(S["xg_t"], 1)

            def up(b):
                pe.wait_ge(S["xg_tev"], b + 1)
                pe.wait_ge(we_in[b % 2], 16 * (b // 2 + 1))
                if b >= 2:
                    pe.wait_ge(S["gated"], b - 1)
                for k in range(KD):
                    last = MM(bank[4 + b % 2], xgT[b % 2][:, k, :], weu[b % 2][:, k, :], start=k == 0, stop=k == KD - 1)
                last.then_inc(S["up_done"], 1)

            def down(b):
                pe.wait_ge(S["gated"], b + 1)
                if b >= 1:
                    pe.wait_ge(S["h_tev"], b)
                for k in range(2):
                    last = turn(bank[6][:, k * P:(k + 1) * P], hb[b % 2][:, k * P:(k + 1) * P])
                last.then_inc(S["h_t"], 1)
                pe.wait_ge(S["h_tev"], b + 1)
                pe.wait_ge(wd_in[b % 2], 16 * (b // 2 + 1))
                if b >= 1:
                    pe.wait_ge(S["y_ev"], 2 * b)
                for c in range(2):
                    for k in range(2):
                        last = MM(bank[2 + c], hTb[b % 2][:, k, :], wed[b % 2][:, k, c * 512:(c + 1) * 512], start=k == 0, stop=k == 1)
                last.then_inc(S["down_done"], 1)

            pe.wait_ge(S["ids_ready"], 1)
            used = used_blocks(pe)
            gather_turn(0)
            up(0)
            for b in range(BLOCKS):
                if b + 1 < BLOCKS:
                    with when_used(pe, used, b + 1):
                        gather_turn(b + 1)
                        up(b + 1)
                with when_used(pe, used, b):
                    down(b)


_INS = ['x', 'w_in', 'w_out', 'da_lambda', 'da_subln', 'sc_conv', 'rw_mu', 'rw_vecs', 'rw_w_up', 'rw_a_up', 'rw_g_up',
        'ln_gain', 'ln_bias', 'rel_bias', 'router_w', 'router_b', 'moe_w_in', 'moe_w_down']


def kernel(**inputs):
    import concourse.bacc as _bacc
    from concourse.bass_utils import run_bass_kernel_spmd as _run

    nc = _bacc.Bacc("TRN2", target_bir_lowering=False, num_devices=1)
    arrays, args = {}, []
    values = {n: np.ascontiguousarray(inputs[n]) for n in _INS}
    values.update(constants())
    for name, a in values.items():
        arrays[f"in_{name}"] = a
        args.append(nc.dram_tensor(f"in_{name}", a.shape, mybir.dt.from_np(a.dtype), kind="ExternalInput").ap())
    args.append(nc.dram_tensor("out_0", (1, T, D), F32, kind="ExternalOutput").ap())
    layer_kernel(nc, *args)
    r = _run(nc, [arrays], core_ids=[0])
    return r.results[0]["out_0"]
```

```python
import math
from contextlib import ExitStack, nullcontext

import numpy as np
import concourse.bass as bass
from concourse import mybir

F32 = mybir.dt.float32
I32 = mybir.dt.int32
ALU = mybir.AluOpType
ACT = mybir.ActivationFunctionType
AX = mybir.AxisListType

D, T, P = 1024, 1024, 128
KD = D // P
NT = T // P
GW = 256
HD = 64
RW_COLS = 3 * GW + 128
P_IN = 9 * GW + RW_COLS
NE, FE = 16, 256
EPG = 4
ALPHA = 2 ** 0.25
LAM_INIT = 0.8 - 0.6
DECAY = math.exp(-0.5)
NEG = -1e30
BLOCKS = NE + (2 * T - NE) // P
NBP = 32
SB0, DA0, SC0, RW0 = 0, 3 * GW, 6 * GW, 9 * GW
BUCKETS, MAX_DIST = 32, 128
LT5 = 3 * P

RW_SHARE = 3.0

IDENT, SU, UI, SL, ONES, BO, BM, M1, M1T, MB, NEGD, IOTA, NCST = 0, 1, 2, 3, 4, 5, 6, 7, 8, 9, 15, 16, 17


def constants():
    r = np.arange(P)
    row, col = r[:, None], r[None, :]
    c = np.zeros((P, NCST, P), np.float32)
    c[:, IDENT] = row == col
    c[:, SU] = row < col
    c[:, UI] = row <= col
    c[:, SL] = row > col
    c[:, ONES] = 1
    c[:, BO] = row // HD == col // HD
    c[:, BM] = (row // HD == col // HD) / HD

    def level(b):
        return (row // (2 * b) == col // (2 * b)) & (row // b % 2 == 1) & (col // b % 2 == 0)
    c[:, M1] = level(1)
    c[:, M1T] = level(1).T
    for n in range(6):
        c[:, MB + n] = level(2 << n)
    c[:, NEGD] = np.where(row > col, 0.0, NEG)
    c[:, IOTA] = np.broadcast_to(col, (P, P))
    d = 2 * P - 1 - np.arange(LT5)
    n = np.maximum(d, 0)
    nf = np.maximum(n, 1).astype(np.float32)
    big = 16 + (np.log(nf / np.float32(16)) / np.float32(math.log(MAX_DIST / 16)) * np.float32(16)).astype(np.int32)
    bucket = np.where(n < 16, n, np.minimum(big, BUCKETS - 1))
    hot = np.zeros((BUCKETS + 1, LT5), np.float32)
    hot[bucket[d >= 0], np.nonzero(d >= 0)[0]] = 1
    hot[BUCKETS, d < 0] = NEG
    s = np.zeros((P, 64), np.float32)
    s[:, 0:NBP] = np.arange(NBP)
    s[0:32, 32] = -2.0
    s[32:, 32] = -1.0
    s[:, 33], s[:, 34], s[:, 35] = 64e-5, 1e-5, 1.0
    tok = (np.arange(NT)[None, :] * P + r[:, None]).astype(np.int32)
    return {"c_mats": c.reshape(P, NCST * P), "c_hot": hot, "c_small": s, "c_tok": tok}


def layer_kernel(nc, x, w_in, w_out, da_lambda, da_subln, sc_conv, rw_mu, rw_vecs, rw_w_up, rw_a_up, rw_g_up,
                 ln_gain, ln_bias, rel_bias, router_w, router_b, moe_w_in, moe_w_down,
                 c_mats, c_hot, c_small, c_tok, out):
    ctx = ExitStack()
    with ctx:
        ctx.enter_context(nc.allow_non_contiguous_dma("small parameter columns"))

        def sb(name, shape, dt=F32):
            return ctx.enter_context(nc.sbuf_tensor(name, shape, dt))

        def sem(name):
            return ctx.enter_context(nc.semaphore(name))

        bias_d = nc.dram_tensor("bias_d", [4, P * LT5], F32)
        x1_d = nc.dram_tensor("x1_d", [T, D], F32)
        y_d = nc.dram_tensor("y_d", [BLOCKS * P, D], F32)

        cst = sb("cst", [P, NCST, P])
        small = sb("small", [P, 64])
        tok = sb("tok", [P, NT], I32)
        mu = sb("mu", [P, 7])
        vecs = sb("vecs", [P, 7, 2])
        conv = sb("conv", [P, 3, 2])
        subg = sb("subg", [P, 1])
        relb = sb("relb", [BUCKETS, 4])
        lp = sb("lp", [P, 4, 32])
        lam = sb("lam", [P, 8])
        low_up = sb("low_up", [P, GW])
        rwr = sb("rwr", [P, KD, NE])
        rbias = sb("rbias", [P, NE])
        dfac = sb("dfac", [P, 2, NT])
        smid = sb("smid", [P, 2, NT])
        stat = sb("stat", [P, 64])
        mixT = sb("mixT", [P, 8, T])
        qk = sb("qk", [P, 8, T])
        vt = sb("vt", [P, NT, 2 * GW])
        mid = sb("mid", [P, 6 * T + 7 * (T + 1)])
        sc = mid[:, 0:6 * T].rearrange("p (j t) -> p j t", j=6)
        rw = mid[:, 6 * T:].rearrange("p (j t) -> p j t", j=7)
        arena = sb("arena", [P, 16 * 1024])

        def region(at, *dims):
            n = 1
            for d in dims:
                n *= d
            v = arena[:, at:at + n]
            if len(dims) == 2:
                return v.rearrange("p (a b) -> p a b", a=dims[0])
            if len(dims) == 3:
                return v.rearrange("p (a b c) -> p a b c", a=dims[0], b=dims[1])
            return v

        def C(i):
            return cst[:, i, :]

        pz = [ctx.enter_context(nc.psum_tensor(f"pz{i}", [P, 1024], F32)) for i in range(2)]
        pb = [ctx.enter_context(nc.psum_tensor(f"pb{i}", [P, 512], F32)) for i in range(4)]
        bank = [pz[0][:, 0:512], pz[0][:, 512:1024], pz[1][:, 0:512], pz[1][:, 512:1024]] + [b[:, :] for b in pb]

        names = """kk_scale ln_done rw_rstd da_rstd mats_in consts zeroed x_turned xT_ready fill_done fill_evac mix_diff mixed low_exp low_ready aux_done aux_evac
            aux_devac conv_u sq_ready decay_ready decays bonus_ready rwe_done
            bias_up bias_rows bias_evac bias_st bias_far
            rw_init mean_done centred squared var_done rw_out
            sb_z sb_soft sb_log sb_w da_z da_max da_prob da_factor da_scaled da_attn at_t at_wT at_o at_evac
            da_sq da_ms da_done lam_prod lam_exp rw_fill rw_evac rw_copied rw_vevac
            wout_in xr_in op_done op_sum ln_stat ln_norm ln_gain x1_ready x1_st x1_t x1_tev rl_done rl_ev route_sel cnt_done
            slot_hot slot_sum up_done exp_g gate_step gated h_t h_tev down_done y_ev xg_t xg_tev
            y_zero y_scaled fin_stat fin_norm fin_gain fin_ready out_st gb_in ids_ready vchain achain pchain""".split()
        S = {n: sem(n) for n in names}
        x_in = [sem(f"x_in{i}") for i in range(4)]
        w_arr = [sem(f"w_arr{i}") for i in range(4)]
        wv_in = sem("wv_in")
        t5_in = sem("t5_in")
        wd_in = [sem(f"wd_in{i}") for i in range(3)]
        we_in = [sem(f"we_in{i}") for i in range(3)]
        xg_in = [sem(f"xg_in{i}") for i in range(2)]
        y_st = [sem(f"y_st{i}") for i in range(2)]
        yg_in = [sem(f"yg_in{i}") for i in range(4)]

        block = ctx.enter_context(nc.Block())

        xT = region(0, KD, T)
        wring = region(8192, 4, KD, P)
        xs = region(12288, 4, T)
        wv = region(12288, KD, 512)
        tiles = []
        for s, c in ((6, 768), (2, 256), (3, 384), (0, 0), (1, 128), (4, 512), (5, 640)):
            tiles.append((RW0 + c, rw[:, s, 1:T + 1], 1.0))
        for s in range(6):
            tiles.append((SC0 + s * P, sc[:, s, :], 1.0))
        for s in range(4):
            tiles.append((SB0 + s * P, qk[:, s, :], HD ** -0.5 if s < 2 else 1.0))
        for s in range(4):
            tiles.append((DA0 + s * P, qk[:, 4 + s, :], 32 ** -0.5 if s < 2 else 1.0))
        NTILE, V_AT = len(tiles), 13
        NFILL = 2 * NTILE + NT
        rw_order = [6, 2, 3, 0, 1, 4, 5]

        fills = [("f", t, half) for half in range(2) for t in range(4)]

        def fills_until(t):
            return t + 5 if t < 4 else 2 * t + 2 + (NT if t >= V_AT else 0)

        for t in range(4, NTILE):
            if t == V_AT:
                fills += [("v", i, 0) for i in range(NT)]
            fills += [("f", t, 0), ("f", t, 1)]
        M01, M23, M67 = mixT[:, 0:2, :], mixT[:, 2:4, :], mixT[:, 6:8, :]
        S1, S2, S3 = sc[:, 0:2, :], sc[:, 2:4, :], sc[:, 4:6, :]
        D1, D2 = qk[:, 4:6, :], qk[:, 6:8, :]
        rR, rK, rV = rw[:, 0:2, 1:T + 1], rw[:, 2:4, 1:T + 1], rw[:, 4:6, 1:T + 1]
        brows = qk[:, 0:2, :].rearrange("p j t -> p (j t)")[:, 0:4 * LT5].rearrange("p (h m) -> p h m", h=4)
        hot = qk[0:BUCKETS + 1, 2, 0:LT5]
        bias_l = qk[0:BUCKETS + 1, 4, 0:512].rearrange("p (h c) -> p h c", h=4)
        NCONST = 17

        shared = [("LT", "RP"), ("X", "U"), ("RbT",), ("RkT",), ("XT",), ("AkT", "W", "NG")]
        cbs = [{n: region(h * 3328 + i * 512, 4, P) for i, names_ in enumerate(shared) for n in names_} for h in range(2)]
        for h in range(2):
            cbs[h]["AkV"] = region(h * 3328 + 3072, 4, HD)
        tm = {n: region(6656 + i * 512, 4, P) for i, n in enumerate("abkv")}
        st = rw[:, 6, 1:T + 1].rearrange("p (j n c) -> p j n c", j=2, n=NT)
        KEYS = ["LT", "L", "RbT", "AkT", "RkT", "AkV"]
        for lev in range(6):
            KEYS += [f"W{lev}", f"X{lev}", f"XT{lev}"] if lev < 5 else ["W5", "XT5"]
        KEYS += ["U", "RP", "NG", "S0", "S1", "Y"]
        rw_fills = []
        for m in range(NT // 2):
            rw_fills += [(m, 0, key) for key in ("Ta", "Tb", "Tk", "Tv")]
            for key in KEYS:
                if key == "S1" and m == NT // 2 - 1:
                    continue
                rw_fills += [(m, 0, key), (m, 1, key)]
        at = {f: g for g, f in enumerate(rw_fills)}
        NRW = len(rw_fills)
        bufE = [region(8704 + i * 1024, T) for i in range(2)]
        bufS = [region(10752 + i * 1024, T) for i in range(2)]
        bufT = [region(12800 + i * 1024, NT, P) for i in range(2)]
        t5 = region(14848, 4, 2 * P)

        def da_logits(it, m):
            i = items[it][1]
            c0 = 512 * (it % 2) if i < 4 else 0
            return pz[m][:, c0:c0 + (i + 1) * P]
        items = [("sb", i, hh) for i in range(NT) for hh in range(4)] + [("da", i, hh) for i in range(NT) for hh in range(4)]
        NI, NSB = len(items), len(items) // 2
        turn_at, halves = [], 0
        for _, i, _ in items:
            turn_at.append(halves)
            halves += 1 + i // 4

        def evacuator(g):
            return "act" if rw_fills[g][2] in ("Ta", "Tb", "Tk", "Tv", "AkV", "U", "Y") else "dve"

        evacs = {e: [sum(evacuator(f) == e for f in range(g + 1)) for g in range(NRW)] for e in ("act", "dve")}

        def rw_operands(g):
            m, h, key = rw_fills[g]
            lev = int(key[-1]) if key[-1].isdigit() else 0
            need = {"AkV": "AkT", "U": "XT5", "RP": "U", "NG": "U", "S0": "NG", "S1": "S0", "Y": "S0"}.get(key)
            if key[0] == "W":
                need = f"X{lev - 1}" if lev else "LT"
            elif key[0] == "X":
                need = f"W{lev}"
            return max(g - 2, at[m, h, need] if need else 0)

        def parts(it):
            return 1 + items[it][1] // 4

        def make_plan():
            lanes = {}
            HOP = 0.4

            def add(eng, step, cost, *deps):
                lanes.setdefault((eng, step[0]), []).append((step, cost, [d for d in deps if d]))

            def vec(n):
                return 0.06 + n / 960

            def sca(n):
                return 0.2 + n / 1200

            for g in range(NRW):
                m, h, key = rw_fills[g]
                last = rw_operands(g)
                deps = [("rwe", f) for f in range(max(0, last - 3), last + 1)] if g >= 2 else []
                if key == "W0":
                    deps.append(("init", 2 * m + h))
                add("pe", ("rw", g), {"Y": 2.6, "NG": 1.3, "AkV": 0.43, "S0": 0.2, "S1": 0.2}.get(key, 0.86), *deps)
                add(evacuator(g), ("rwe", g), {"NG": 0.9, "S0": 0.3, "S1": 0.3}.get(key, 0.6), ("rw", g),
                    ("init", 2 * m + h) if key == "X0" else None, ("rwe", g - 2) if key[0] == "S" else None)
                if key == "L":
                    add("pool", ("init", 2 * m + h), 3.6, ("rwe", g))
            for q in range(4):
                add("pe", ("mn", q), 0.86, *[("rwe", NRW - 1 - k) for k in range(4)], ("ct", q - 1) if q else None)
                add("dve", ("ct", q), 0.65, ("mn", q))
                add("act", ("sq", q), 0.63, ("ct", q))
                add("pe", ("vr", q), 0.86, ("sq", q), ("le", q - 1) if q else None)
                add("act", ("le", q), 1.5, ("vr", q))
                add("dve", ("nf", q), 3.0, ("le", q))
            for it in range(NI):
                kind, i, _ = items[it]
                n, np_ = (i + 1) * P, parts(it)
                two_ago = it - 2 if it >= 2 else None
                freed = ("t", two_ago, parts(two_ago) - 1) if it >= 2 else None
                if kind == "sb":
                    add("pe", ("z", it), n / 600, ("l3", two_ago) if it >= 2 else None)
                    add("act", ("a", it), 3 * sca(n) + 0.2, ("z", it), ("l3", two_ago) if it >= 2 else None)
                    add("dve", ("l1", it), vec(n) + 0.5, ("a", it), freed)
                    add("dve", ("l2", it), vec(n) + 0.1, ("l1", it))
                    add("dve", ("l3", it), vec(n) + 0.4, ("l2", it))
                    add("act", ("e", it), sca(n), ("l3", it))
                    weights = ("e", it)
                else:
                    for m in range(2):
                        back = 2 if i < 4 and it - 2 >= NSB else 1
                        used = ("l3", NSB - 2 + m) if it - back < NSB else ("p", it - back, m)
                        add("pe", ("s", it, m), n / 600, used)
                        add("dve", ("x", it, m), vec(n) + 0.5, ("s", it, m))
                        add("act", ("p", it, m), sca(n) + 0.1, ("x", it, m), freed)
                    add("dve", ("c1", it), 0.4, ("p", it, 0), ("p", it, 1))
                    add("act", ("cs", it), sca(n) + 0.1, ("c1", it))
                    add("dve", ("c2", it), vec(n), ("cs", it))
                    weights = ("c2", it)
                prev = ("t", it - 1, parts(it - 1) - 1) if it else None
                for part in range(np_):
                    k = min(i + 1, 4 * part + 4) - 4 * part
                    before = ("cp", it, part - 1) if part else ("cp", it - 1, parts(it - 1) - 1) if it else None
                    add("pe", ("t", it, part), 0.213 * k, weights, before)
                    add("act", ("cp", it, part), sca(k * P), ("t", it, part), ("v", it - 2, parts(it - 2) - 1) if it >= 2 else None)
                    add("pe", ("v", it, part), 0.213 * k, ("cp", it, part), ("o", it - 2) if it >= 2 else None)
                add("dve", ("o", it), 0.2, ("v", it, np_ - 1))

            add("sp", ("wout", 0), 26.0, ("nf", 3), ("z", NSB - 1))
            for i in range(NT):
                add("act", ("dq", i), 0.4, ("o", NSB + 4 * i + 3), ("nf", 3), ("dm", i - 1) if i else None)
                add("pe", ("dm", i), 0.43, ("dq", i), ("dr", i - 1) if i else None, ("sum", i - 2, 1) if i >= 2 else None)
                add("act", ("dr", i), 1.1, ("dm", i), ("dn", i - 1) if i else None)
                add("dve", ("dn", i), 0.5, ("dr", i))
            for i in range(NT):
                for c in range(2):
                    for part in range(4):
                        add("pe", ("pj", i, c, part), 1.71, ("wout", 0), ("dn", i), ("dr", min(i + 1, NT - 1)) if c else None, ("sum", i - 1, c) if i else None)
                    add("dve", ("sum", i, c), 0.65, ("pj", i, c, 3))
                add("dve", ("st", i), 1.6, ("sum", i, 1), ("nm", i - 4) if i >= 4 else None)
                add("act", ("nm", i), 2.0, ("st", i))
                add("dve", ("gn", i), 1.15, ("nm", i))
                add("pool", ("bs", i), 2.4, ("gn", i))
                add("pe", ("ro", i), 0.9, ("bs", i), ("o", NI - 1), ("rc", i - 1) if i else None)
                add("act", ("rc", i), 1.3, ("ro", i), ("rm", i - 1) if i else None)
                add("pe", ("rm", i), 0.3, ("rc", i), ("re", i - 1) if i else None)
                add("act", ("re", i), 0.2, ("rm", i))

            counted = ("z", "s", "t", "v")
            work = {r: sum(c for (e, k), q in lanes.items() if e == "pe" and k in (("rw",) if r else counted) for _, c, _ in q) for r in (True, False)}
            spent = {True: 0.0, False: 0.0}
            done, free = {}, {e: 0.0 for e in ("pe", "dve", "act", "pool", "sp")}
            plan = {e: [] for e in free}
            head = {lane: 0 for lane in lanes}
            rank = {"o": 0, "v": 1, "cp": 1, "t": 2, "e": 3, "c2": 3, "cs": 3, "c1": 3, "l3": 4, "l2": 5, "l1": 6, "p": 6, "x": 6, "a": 7, "z": 8, "s": 8,
                    "dq": 2, "dm": 2, "dr": 2, "dn": 2, "sum": 7, "st": 7, "nm": 7, "gn": 7, "pj": 9, "ro": 3, "rc": 3, "rm": 3, "re": 3}
            while len(done) < sum(map(len, lanes.values())):
                best = None
                for (eng, kind), q in lanes.items():
                    h = head[eng, kind]
                    if h == len(q) or any(d not in done for d in q[h][2]):
                        continue
                    start = max([free[eng]] + [done[d] + HOP for d in q[h][2]])
                    rwkv = kind in ("rw", "rwe", "init", "mn", "ct", "sq", "vr", "le", "nf")
                    ahead = spent[True] / work[True] > RW_SHARE * spent[False] / work[False]
                    key = (start, kind == "pj", rwkv == ahead, rank.get(kind, 0), q[h][0][1])
                    if best is None or key < best[0]:
                        best = (key, eng, kind)
                key, eng, kind = best
                step, cost, _ = lanes[eng, kind][head[eng, kind]]
                head[eng, kind] += 1
                free[eng] = done[step] = key[0] + cost
                plan[eng].append(step)
                if eng == "pe" and kind in ("rw",) + counted:
                    spent[kind == "rw"] += cost
            return plan

        plan = make_plan()
        wout = mid[:, 0:8192].rearrange("p (k n) -> p k n", k=KD)
        x1T = mid[:, 8192:9216].rearrange("p (k t) -> p k t", k=KD)
        rms_sq, rms_dev = (mid[:, 9216 + 256 * k:9472 + 256 * k].rearrange("p (j t) -> p j t", j=2) for k in range(2))
        rms_bank = bank[7][:, 0:256]
        x1 = region(0, NT, T)
        gb = qk[:, 0:4, :]
        rt = region(8192, 768)
        rt2 = region(8960, 480)
        rl = region(9440, NT, NE)
        place_hot = region(10240, 2 * NT, P).rearrange("p (s i) c -> p s i c", s=2)
        blk_hot = region(12288, 2 * NT, NBP).rearrange("p (s i) b -> p s i b", s=2)
        weu = [mid[:, i * 6144:i * 6144 + 4096].rearrange("p (k n) -> p k n", k=KD) for i in range(2)] + [vt[:, :, :]]
        wed = [mid[:, i * 6144 + 4096:(i + 1) * 6144].rearrange("p (k n) -> p k n", k=2) for i in range(2)] + [qk[:, 4:6, :]]
        xg = [mixT[:, i, :] for i in range(2)]
        xgT = [mixT[:, 2 + i, :].rearrange("p (k t) -> p k t", k=KD) for i in range(2)]
        yb = [mixT[:, 4 + i, :] for i in range(2)]
        hb = [mixT[:, 6, i * 512:i * 512 + 256] for i in range(2)]
        eb = [mixT[:, 6, i * 512 + 256:i * 512 + 512] for i in range(2)]
        hTb = [mixT[:, 7, i * 256:(i + 1) * 256].rearrange("p (k t) -> p k t", k=2) for i in range(2)]
        slots = sb("slots", [P, 2, NT], I32)
        gates = sb("gates", [P, 2, NT])
        ids = sb("ids", [P, NBP], I32)
        slot_tok = sb("slot_tok", [P, NBP], I32)

        def used_blocks(eng):
            return eng.value_load(ids[0:1, NBP - 1:NBP], min_val=NE, max_val=BLOCKS)

        def when_used(eng, used, b):
            return eng.If(used > b) if b >= NE else nullcontext()

        def sum_bufs(i):
            return mixT[:, 2 * (i % 4), :], mixT[:, 2 * (i % 4) + 1, :]

        def fin_stat(i):
            return [stat[:, 48 + 4 * (i % 4) + k:49 + 4 * (i % 4) + k] for k in range(4)]

        @block.sync
        def _(sp):
            const = S["consts"]
            sp.dma_start(cst[:, :, :], c_mats.rearrange("p (i c) -> p i c", c=P)).then_inc(S["mats_in"], 16)

            def load_w(t):
                if t >= 4:
                    sp.wait_ge(S["fill_done"], fills_until(t - 4))
                c0 = tiles[t][0]
                sp.dma_start(wring[:, t % 4], w_in[0, :, c0:c0 + P].rearrange("(k p) c -> p k c", p=P)).then_inc(w_arr[t % 4], 16)

            for i in range(NT):
                if i >= 4:
                    sp.wait_ge(S["x_turned"], 2 * (i - 3))
                sp.dma_start(xs[:, i % 4], x[0, i * P:(i + 1) * P, :]).then_inc(x_in[i % 4], 16)
                if i % 2:
                    load_w(i // 2)
            sp.dma_start(small[:, :], c_small).then_inc(const, 16)
            sp.dma_start(tok[:, :], c_tok).then_inc(const, 16)
            sp.dma_start(mu[:, :], rw_mu.rearrange("o (j p) -> p (o j)", p=P)).then_inc(const, 16)
            sp.dma_start(hot, c_hot).then_inc(const, 16)
            sp.dma_start(relb[:, :], rel_bias).then_inc(const, 16)
            sp.dma_start(lp[:, :, :], da_lambda[0].rearrange("a b -> (a b)").partition_broadcast(P).rearrange("p (a b) -> p a b", a=4)).then_inc(S["consts"], 16)
            sp.dma_start(rbias[:, :], router_b.partition_broadcast(P)).then_inc(S["consts"], 16)
            sp.dma_start(vecs[:, :, 0], rw_vecs[0, :, 0:P].rearrange("v p -> p v")).then_inc(const, 16)
            sp.dma_start(vecs[:, :, 1], rw_vecs[0, :, P:GW].rearrange("v p -> p v")).then_inc(const, 16)
            sp.dma_start(low_up[0:32, :], rw_w_up[0]).then_inc(const, 16)
            sp.dma_start(low_up[32:64, :], rw_a_up[0]).then_inc(const, 16)
            sp.dma_start(low_up[64:128, :], rw_g_up[0]).then_inc(const, 16)
            sp.dma_start(conv[:, :, 0], sc_conv[0, :, 0:P].rearrange("v p -> p v")).then_inc(const, 16)
            sp.dma_start(conv[:, :, 1], sc_conv[0, :, P:GW].rearrange("v p -> p v")).then_inc(const, 16)
            sp.dma_start(rwr[:, :, :], router_w.rearrange("(k p) e -> p k e", p=P)).then_inc(const, 16)
            for h in range(2):
                sp.dma_start(subg[HD * h:HD * h + HD, :], da_subln.rearrange("o p -> p o")).then_inc(const, 16)
            sp.wait_ge(S["x_turned"], 16)
            sp.dma_start(wv[:, :, 0:GW], w_in[0, :, SB0 + 2 * GW:SB0 + 3 * GW].rearrange("(k p) c -> p k c", p=P)).then_inc(wv_in, 16)
            sp.dma_start(wv[:, :, GW:], w_in[0, :, DA0 + 2 * GW:DA0 + 3 * GW].rearrange("(k p) c -> p k c", p=P)).then_inc(wv_in, 16)
            for t in range(4, NTILE):
                if t == 6:
                    sp.wait_ge(S["zeroed"], 1)
                    zeros = vt[:, 0:2, :].rearrange("p a n -> p (a n)").unsqueeze(1).to_broadcast([P, BLOCKS - NE, D])
                    sp.dma_start(y_d[NE * P:, :].rearrange("(b p) n -> p b n", p=P), zeros).then_inc(S["y_zero"], 16)
                    sp.wait_ge(S["bias_evac"], 4)
                    sp.dma_start(bias_d[:, :].rearrange("h (p m) -> p h m", p=P), brows).then_inc(S["bias_st"], 16)
                load_w(t)
            sp.wait_ge(S["bias_st"], 16)
            sp.wait_ge(S["y_zero"], 16)
            sp.wait_ge(S["fill_done"], 2 * V_AT + NT)
            for h in range(4):
                src = bass.AP(bias_d, h * P * LT5 + P - 1, [[LT5 - 1, P], [1, 2 * P]])
                sp.dma_start(t5[:, h, :], src).then_inc(t5_in, 16)
            sp.wait_ge(S["sb_z"], NSB)
            for n, g in enumerate((ln_gain, ln_bias)):
                for l in range(2):
                    sp.dma_start(gb[:, 2 * l + n, :], g[0, l, :].partition_broadcast(P)).then_inc(S["gb_in"], 16)
            sp.wait_ge(S["rw_out"], 4)
            sp.dma_start(wout, w_out[0].rearrange("(k p) n -> p k n", p=P)).then_inc(S["wout_in"], 16)
            sp.dma_start(x1, x[0].rearrange("(i p) n -> p i n", p=P)).then_inc(S["xr_in"], 16)
            for i in range(NT):
                sp.wait_ge(S["x1_ready"], i + 1)
                sp.dma_start(x1_d[i * P:(i + 1) * P, :], x1[:, i, :]).then_inc(S["x1_st"], 16)
            def load_up(b, e):
                if b >= 3:
                    sp.wait_ge(S["up_done"], b - 2)
                sp.dma_start(weu[b % 3], moe_w_in[0, bass.ds(e, 1), :, :].rearrange("o (k p) n -> p (o k) n", p=P)).then_inc(we_in[b % 3], 16)

            def load_down(b, e):
                if b >= 3:
                    sp.wait_ge(S["down_done"], b - 2)
                sp.dma_start(wed[b % 3], moe_w_down[0, bass.ds(e, 1), :, :].rearrange("o (k p) n -> p (o k) n", p=P)).then_inc(wd_in[b % 3], 16)

            def store_y(b):
                sp.wait_ge(S["y_ev"], 2 * (b + 1))
                sp.dma_start(y_d[b * P:(b + 1) * P, :], yb[b % 2]).then_inc(y_st[b % 2], 16)

            sp.wait_ge(S["op_done"], 2 * NT)
            load_up(0, 0)
            load_down(0, 0)
            sp.wait_ge(S["ids_ready"], 1)
            used = used_blocks(sp)
            for i in range(2):
                sp.wait_ge(xg_in[i], 16)
            for b in range(1, BLOCKS):
                with when_used(sp, used, b):
                    e = sp.value_load(ids[0:1, b:b + 1], min_val=0, max_val=NE - 1)
                    load_up(b, e)
                    load_down(b, e)
                if b >= 2:
                    with when_used(sp, used, b - 2):
                        store_y(b - 2)
            for b in (BLOCKS - 2, BLOCKS - 1):
                with when_used(sp, used, b):
                    store_y(b)
            for i in range(NT):
                sp.wait_ge(S["fin_ready"], i + 1)
                sp.dma_start(out[0, i * P:(i + 1) * P, :], x1[:, i, :]).then_inc(S["out_st"], 16)
            sp.wait_ge(S["out_st"], 16 * NT)

        @block.gpsimd
        def _(pool):
            pool.memset(rw[:, :, 0:1], 0.0)
            pool.memset(vt[:, 0:2, :], 0.0).then_inc(S["zeroed"], 1)
            pool.wait_ge(S["zeroed"], 1)
            for m, s in enumerate(rw_order):
                pool.wait_ge(S["fill_evac"], fills_until(m))
                if m >= 4:
                    pool.wait_ge(S["mixed"], m - 3)
                pool.tensor_tensor(mixT[:, m % 4, :], rw[:, s, 0:T], rw[:, s, 1:T + 1], ALU.subtract).then_inc(S["mix_diff"], 1)
            pool.wait_ge(S["fill_evac"], 26)
            for j in range(2):
                pool.tensor_tensor(sc[:, 2 + j, :], sc[:, 2 + j, :], sc[:, 4 + j, :], ALU.mult).then_inc(S["conv_u"], 1)
            for step, n in plan["pool"]:
                if step == "init":
                    m, h = n // 2, n % 2
                    pool.wait_ge(S["rw_evac"], evacs["dve"][at[m, h, "L"]])
                    idb = C(IDENT).unsqueeze(1).to_broadcast([P, 4, P])
                    cb = cbs[h]
                    pool.tensor_tensor(cb["X"], cb["X"], idb, ALU.add)
                    pool.tensor_tensor(cb["XT"], cb["LT"], C(M1T).unsqueeze(1).to_broadcast([P, 4, P]), ALU.mult).then_inc(S["pchain"], 1)
                    pool.wait_ge(S["pchain"], n + 1)
                    pool.tensor_tensor(cb["XT"], cb["XT"], idb, ALU.add).then_inc(S["rw_init"], 1)
                else:
                    pool.wait_ge(S["ln_gain"], n + 1)
                    pool.tensor_tensor(x1[:, n, :], x1[:, n, :], gb[:, 1, :], ALU.add).then_inc(S["x1_ready"], 1)
            pool.wait_ge(S["ids_ready"], 1)
            pool.wait_ge(S["x1_st"], 16 * NT)
            used = used_blocks(pool)
            for b in range(BLOCKS):
                with when_used(pool, used, b):
                    if b >= 2:
                        pool.wait_ge(S["xg_t"], b - 1)
                    pool.indirect_dma_start(xg[b % 2], None, x1_d[:, :],
                                            bass.IndirectOffsetOnAxis(ap=slot_tok[:, b:b + 1], axis=0)).then_inc(xg_in[b % 2], 16)
            for b in range(NE - 2, BLOCKS):
                with when_used(pool, used, b):
                    pool.wait_ge(y_st[b % 2], 16 * (b // 2 + 1))

            def token_rows(i):
                if i >= 4:
                    pool.wait_ge(S["fin_stat"], i - 3)
                for s in range(2):
                    pool.indirect_dma_start(sum_bufs(i)[s], None, y_d[:, :],
                                            bass.IndirectOffsetOnAxis(ap=slots[:, s, i:i + 1], axis=0)).then_inc(yg_in[i % 4], 16)

            for i in range(4):
                token_rows(i)
            for i in range(NT):
                if i + 4 < NT:
                    token_rows(i + 4)
                pool.wait_ge(S["fin_gain"], i + 1)
                pool.tensor_tensor(x1[:, i, :], x1[:, i, :], gb[:, 3, :], ALU.add).then_inc(S["fin_ready"], 1)

        @block.scalar
        def _(act):
            nc.scalar.preload_act_table_set("natural_log_exp_and_others")
            A = nc.scalar.activation

            def evac(n):
                kind, t, half = fills[n]
                act.wait_ge(S["fill_done"], n + 1)
                src = bank[4 + n % 4]
                if kind == "v":
                    if t == 0:
                        act.wait_ge(S["y_zero"], 16)
                    A(vt[:, t, :], src, ACT.Copy).then_inc(S["fill_evac"], 1)
                else:
                    if t == V_AT and half == 0:
                        act.wait_ge(S["bias_st"], 16)
                    if n == NFILL - 8:
                        act.wait_ge(S["rwe_done"], 1)
                    A(tiles[t][1][:, half * 512:(half + 1) * 512], src, ACT.Copy, scale=tiles[t][2]).then_inc(S["fill_evac"], 1)

            for n in range(NFILL):
                evac(n)
                if n == 7:
                    act.wait_ge(S["lam_prod"], 1)
                    A(lam[:, 2:4], lam[:, 0:2], ACT.Exp).then_inc(S["lam_exp"], 1)
                if n == 15:
                    act.wait_ge(S["mixed"], 1)
                    A(rw[0:32, 6, 1:T + 1], rw[0:32, 6, 1:T + 1], ACT.Exp, scale=-2.0)
                    A(rw[64:128, 6, 1:T + 1], rw[64:128, 6, 1:T + 1], ACT.Exp, scale=-1.0).then_inc(S["low_exp"], 1)
                if n == 18:
                    act.wait_ge(S["mixed"], 7)
                    for a in range(12):
                        what, j, half = a // 4, a // 2 % 2, a % 2
                        act.wait_ge(S["aux_done"], a + 1)
                        dst = (M01, M23, M67)[what][:, j, half * 512:(half + 1) * 512]
                        if what < 2:
                            A(dst, bank[a % 4], ACT.Exp, bias=stat[:, 2 * what + j:2 * what + j + 1], scale=-1.0).then_inc(S["aux_evac"], 1)
                        else:
                            A(dst, bank[a % 4], ACT.Copy).then_inc(S["aux_evac"], 1)
                if n == 29:
                    act.wait_ge(S["aux_devac"], 4)
                    A(S2, S2, ACT.Ln).then_inc(S["ln_done"], 1)
                    act.wait_ge(S["ln_done"], 1)
                    A(S2, S2, ACT.Exp, scale=-0.5).then_inc(S["kk_scale"], 1)
                if n == 28:
                    act.wait_ge(S["decay_ready"], 1)
                    A(D2, D1, ACT.Exp, scale=DECAY)
                    A(M01, M01, ACT.Exp, scale=-DECAY)
                    A(dfac[:, :, :], dfac[:, :, :], ACT.Exp, scale=-DECAY).then_inc(S["achain"], 1)
                    act.wait_ge(S["achain"], 1)
                    A(D1, D1, ACT.Exp, scale=-DECAY).then_inc(S["decays"], 1)

            links = [1]

            def soft(it):
                n, p = (items[it][1] + 1) * P, it % 2
                act.wait_ge(S["sb_z"], it + 1)
                if it >= 2:
                    act.wait_ge(S["sb_log"], it - 1)
                A(bufE[p][:, 0:n], pz[p][:, 0:n], ACT.Abs).then_inc(S["achain"], 1)
                links[0] += 2
                act.wait_ge(S["achain"], links[0] - 1)
                A(bufE[p][:, 0:n], bufE[p][:, 0:n], ACT.Exp, scale=-1.0).then_inc(S["achain"], 1)
                act.wait_ge(S["achain"], links[0])
                A(bufE[p][:, 0:n], bufE[p][:, 0:n], ACT.Ln, bias=1.0).then_inc(S["sb_soft"], 1)

            def probs(it, m):
                _, i, _ = items[it]
                n, p = (i + 1) * P, it % 2
                act.wait_ge(S["da_max"], 2 * (it - NSB) + m + 1)
                act.wait_ge(S["at_t"], turn_at[it - 1])
                A((bufS, bufE)[m][p][:, 0:n], da_logits(it, m), ACT.Exp, bias=stat[:, 16 + 4 * p + m:17 + 4 * p + m],
                  accum_out=stat[:, 18 + 4 * p + m:19 + 4 * p + m]).then_inc(S["da_prob"], 1)

            def turned_act(it, part):
                i, p = items[it][1], it % 2
                act.wait_ge(S["at_t"], turn_at[it] + part + 1)
                if it >= 2:
                    act.wait_ge(S["at_o"], it - 1)
                k0, k1 = 4 * part, min(i + 1, 4 * part + 4)
                A(bufT[p][:, k0:k1, :], bank[4][:, 0:(k1 - k0) * P].rearrange("p (k t) -> p k t", t=P), ACT.Copy).then_inc(S["at_wT"], 1)

            def rw_copy(g):
                m, h, key = rw_fills[g]
                b, lo, hi = cbs[h], HD * h, HD * h + HD
                src = bank[6 + g % 2].rearrange("p (q c) -> p q c", q=4)
                act.wait_ge(S["rw_fill"], g + 1)
                if key in ("Ta", "Tb", "Tk", "Tv"):
                    A(tm[key[1]], src, ACT.Copy).then_inc(S["rw_copied"], 1)
                elif key == "AkV":
                    A(b["AkV"], bank[6 + g % 2][:, 0:4 * HD].rearrange("p (q c) -> p q c", q=4), ACT.Copy).then_inc(S["rw_copied"], 1)
                elif key == "U":
                    A(b["U"], src, ACT.Copy).then_inc(S["rw_copied"], 1)
                else:
                    for n2 in range(2):
                        c0 = (2 * m + n2) * P
                        last = A(rV[lo:hi, :, c0:c0 + P], src[lo:hi, 2 * n2:2 * n2 + 2, :], ACT.Copy)
                    last.then_inc(S["rw_copied"], 1)

            def norm_part(buf, q):
                return buf[:, q // 2, q % 2 * 512:(q % 2 + 1) * 512]

            def normalise(i, stat_sem, norm_sem):
                mean, var, minus, rstd = fin_stat(i)
                act.wait_ge(stat_sem, i + 1)
                A(rstd, var, ACT.Ln, bias=small[:, 34:35]).then_inc(S["achain"], 1)
                act.wait_ge(S["achain"], links[0] + 1)
                A(rstd, rstd, ACT.Exp, scale=-0.5).then_inc(S["achain"], 1)
                act.wait_ge(S["achain"], links[0] + 2)
                A(var, minus, ACT.Copy, scale=rstd).then_inc(S["achain"], 1)
                links[0] += 3
                act.wait_ge(S["achain"], links[0])
                A(x1[:, i, :], x1[:, i, :], ACT.Identity, bias=var, scale=rstd).then_inc(norm_sem, 1)

            for step, *which in plan["act"]:
                if step == "a":
                    soft(*which)
                elif step == "e":
                    it, = which
                    n, p = (items[it][1] + 1) * P, it % 2
                    act.wait_ge(S["sb_log"], it + 1)
                    A(bufS[p][:, 0:n], bufS[p][:, 0:n], ACT.Exp).then_inc(S["sb_w"], 1)
                elif step == "p":
                    probs(*which)
                elif step == "sq":
                    q, = which
                    act.wait_ge(S["centred"], q + 1)
                    A(norm_part(S1, q), norm_part(rV, q), ACT.Square).then_inc(S["squared"], 1)
                elif step == "le":
                    q, = which
                    act.wait_ge(S["var_done"], q + 1)
                    A(norm_part(S2, q), bank[7], ACT.Ln, bias=small[:, 33:34]).then_inc(S["rw_vevac"], 1)
                    act.wait_ge(S["rw_vevac"], q + 1)
                    A(norm_part(S2, q), norm_part(S2, q), ACT.Exp, scale=-0.5).then_inc(S["rw_rstd"], 1)
                elif step == "dq":
                    i, = which
                    act.wait_ge(S["at_evac"], NSB + 4 * i + 4)
                    act.wait_ge(S["rw_out"], 4)
                    if i >= 1:
                        act.wait_ge(S["da_ms"], i)
                    A(rms_sq, M23[:, :, i * P:(i + 1) * P], ACT.Square).then_inc(S["da_sq"], 1)
                elif step == "dr":
                    i, = which
                    act.wait_ge(S["da_ms"], i + 1)
                    if i >= 1:
                        act.wait_ge(S["da_done"], i)
                    A(rms_dev, rms_bank.rearrange("p (j t) -> p j t", j=2), ACT.Ln, bias=small[:, 34:35]).then_inc(S["achain"], 1)
                    links[0] += 1
                    act.wait_ge(S["achain"], links[0])
                    A(rms_dev, rms_dev, ACT.Exp, scale=-0.5).then_inc(S["da_rstd"], 1)
                elif step == "cs":
                    it, = which
                    n, p = (items[it][1] + 1) * P, it % 2
                    act.wait_ge(S["da_factor"], it - NSB + 1)
                    A(bufS[p][:, 0:n], bufS[p][:, 0:n], ACT.Copy, scale=stat[:, 40 + 4 * p:41 + 4 * p]).then_inc(S["da_scaled"], 1)
                elif step == "nm":
                    normalise(*which, S["ln_stat"], S["ln_norm"])
                elif step == "rc":
                    i, = which
                    act.wait_ge(S["x1_t"], i + 1)
                    if i >= 1:
                        act.wait_ge(S["rl_done"], i)
                    for c in range(2):
                        a = A(x1T[:, 4 * c:4 * c + 4, :], bank[4 + c].rearrange("p (k t) -> p k t", t=P), ACT.Copy)
                    a.then_inc(S["x1_tev"], 1)
                elif step == "re":
                    i, = which
                    act.wait_ge(S["rl_done"], i + 1)
                    A(rl[:, i, :], bank[0][:, 0:NE], ACT.Exp, scale=-1.0).then_inc(S["rl_ev"], 1)
                elif step == "cp":
                    turned_act(*which)
                elif step == "rwe":
                    rw_copy(*which)
            def xg_copy(b):
                act.wait_ge(S["xg_t"], b + 1)
                if b >= 2:
                    act.wait_ge(S["up_done"], b - 1)
                for c in range(2):
                    a = A(xgT[b % 2][:, 4 * c:4 * c + 4, :], bank[c].rearrange("p (k t) -> p k t", t=P), ACT.Copy)
                a.then_inc(S["xg_tev"], 1)

            def gate_exp(b):
                act.wait_ge(S["up_done"], b + 1)
                A(eb[b % 2], bank[4 + b % 2][:, 0:FE], ACT.Exp, scale=-1.0).then_inc(S["exp_g"], 1)

            act.wait_ge(S["ids_ready"], 1)
            used = used_blocks(act)
            xg_copy(0)
            xg_copy(1)
            gate_exp(0)
            for b in range(BLOCKS):
                with when_used(act, used, b):
                    act.wait_ge(S["h_t"], b + 1)
                    if b >= 2:
                        act.wait_ge(S["down_done"], b - 1)
                    A(hTb[b % 2], bank[6][:, 0:FE].rearrange("p (k t) -> p k t", t=P), ACT.Copy).then_inc(S["h_tev"], 1)
                if b + 2 < BLOCKS:
                    with when_used(act, used, b + 2):
                        xg_copy(b + 2)
                if b + 1 < BLOCKS:
                    with when_used(act, used, b + 1):
                        gate_exp(b + 1)
                with when_used(act, used, b):
                    act.wait_ge(S["down_done"], b + 1)
                    if b >= 2:
                        act.wait_ge(y_st[b % 2], 16 * (b // 2))
                    A(yb[b % 2][:, 0:512], bank[2], ACT.Copy).then_inc(S["y_ev"], 1)

            def scale_rows(i):
                act.wait_ge(yg_in[i % 4], 32 * (i // 4 + 1))
                ya, _ = sum_bufs(i)
                A(ya, ya, ACT.Copy, scale=gates[:, 0, i:i + 1]).then_inc(S["y_scaled"], 1)

            scale_rows(0)
            for i in range(NT):
                if i + 1 < NT:
                    scale_rows(i + 1)
                normalise(i, S["fin_stat"], S["fin_norm"])

        @block.vector
        def _(v):
            V = nc.vector
            chain = [0]

            def link(ins):
                chain[0] += 1
                ins.then_inc(S["vchain"], 1)
                v.wait_ge(S["vchain"], chain[0])

            TT, TS, STT = V.tensor_tensor, V.tensor_scalar, V.scalar_tensor_tensor

            def sigmoid(a):
                link(TS(a, a, 1.0, None, ALU.add))
                return V.reciprocal(a, a)

            for n in range(16):
                i, c = n // 2, n % 2
                v.wait_ge(S["x_turned"], n + 1)
                V.tensor_copy(xT[:, 4 * c:4 * c + 4, i * P:(i + 1) * P], bank[n % 4].rearrange("p (k t) -> p k t", t=P)).then_inc(S["xT_ready"], 1)
            v.wait_ge(S["consts"], 16 * NCONST)
            link(V.memset(bias_l, 1.0))
            V.tensor_copy(bias_l[0:BUCKETS], relb[:, :].unsqueeze(2).to_broadcast([BUCKETS, 4, P])).then_inc(S["bias_up"], 1)
            link(TT(lp[:, 0:3:2, :], lp[:, 0:3:2, :], lp[:, 1:4:2, :], ALU.mult))
            V.tensor_reduce(lam[:, 0:2], lp[:, 0:3:2, :], AX.X, ALU.add).then_inc(S["lam_prod"], 1)
            v.wait_ge(S["lam_exp"], 1)
            link(TT(lam[:, 4:5], lam[:, 3:4], lam[:, 2:3], ALU.subtract))
            link(TS(lam[:, 4:5], lam[:, 4:5], -LAM_INIT, None, ALU.add))
            for w in range(2):
                TS(stat[:, 2 * w:2 * w + 2], vecs[:, w, :], -1.0, None, ALU.mult)
            link(TS(stat[:, 4:6], vecs[:, 3, :], -1.0, 1.0, ALU.mult, ALU.add))
            link(TS(subg[:, :], subg[:, :], 1.0 - LAM_INIT, None, ALU.mult))
            for h in range(4):
                v.wait_ge(S["bias_rows"], h + 1)
                V.tensor_copy(stat[:, 8 + h:9 + h], bank[h][:, 0:1]).then_inc(S["bias_far"], 1)
                v.wait_ge(S["bias_far"], h + 1)
                TS(brows[:, h, :], bank[h][:, 0:LT5], stat[:, 8 + h:9 + h], None, ALU.subtract).then_inc(S["bias_evac"], 1)
            for m, s in enumerate(rw_order):
                v.wait_ge(S["mix_diff"], m + 1)
                STT(rw[:, s, 1:T + 1], mixT[:, m % 4, :], mu[:, s:s + 1], rw[:, s, 1:T + 1], ALU.mult, ALU.add).then_inc(S["mixed"], 1)
            v.wait_ge(S["low_exp"], 1)
            for lo, hi in ((0, 32), (64, 128)):
                last = sigmoid(rw[lo:hi, 6, 1:T + 1])
            link(last)
            TS(rw[0:32, 6, 1:T + 1], rw[0:32, 6, 1:T + 1], 2.0, -1.0, ALU.mult, ALU.add).then_inc(S["low_ready"], 1)
            v.wait_ge(S["aux_evac"], 4)
            link(sigmoid(M01))
            for j in range(2):
                for n in range(NT):
                    last = V.tensor_tensor_scan(D1[:, j, n * P:(n + 1) * P], C(ONES), M01[:, j, n * P:(n + 1) * P], 0.0, ALU.mult, ALU.add)
            link(last)
            d1c = D1.rearrange("p j (n c) -> p j n c", c=P)
            V.tensor_copy(smid[:, :, :], d1c[:, :, :, HD - 1])
            link(V.tensor_copy(dfac[:, :, :], d1c[:, :, :, P - 1]))
            link(TT(dfac[:, :, :], dfac[:, :, :], smid[:, :, :], ALU.subtract))
            link(TT(dfac[:, :, 0:NT - 1], dfac[:, :, 0:NT - 1], smid[:, :, 1:NT], ALU.add))
            for j in range(2):
                last = TT(D1[:, j, :].rearrange("p (n c) -> p n c", c=P), D1[:, j, :].rearrange("p (n c) -> p n c", c=P),
                          smid[:, j, :].unsqueeze(2).to_broadcast([P, NT, P]), ALU.subtract)
            link(last)
            TT(M01, D1, M01, ALU.subtract).then_inc(S["decay_ready"], 1)
            v.wait_ge(S["aux_evac"], 8)
            sigmoid(M23)
            v.wait_ge(S["conv_u"], 2)
            for j in range(2):
                y, u = mixT[:, 4 + j, :], sc[:, 2 + j, :]
                link(TS(y, u, conv[:, 2, j:j + 1], None, ALU.mult))
                link(STT(y[:, 1:], u[:, 0:T - 1], conv[:, 1, j:j + 1], y[:, 1:], ALU.mult, ALU.add))
                link(STT(y[:, 2:], u[:, 0:T - 2], conv[:, 0, j:j + 1], y[:, 2:], ALU.mult, ALU.add))
                link(TT(y, y, sc[:, j, :], ALU.mult))
            for j in range(2):
                last = TS(S1[:, j, :], rK[:, j, :], vecs[:, 2, j:j + 1], None, ALU.mult)
            link(last)
            TT(S2, S1, S1, ALU.mult).then_inc(S["sq_ready"], 1)
            for q in range(4):
                j, half = q // 2, q % 2
                v.wait_ge(S["aux_done"], 12 + q + 1)
                TS(S2[:, j, half * 512:(half + 1) * 512], bank[q], 1e-24, None, ALU.max).then_inc(S["aux_devac"], 1)
            v.wait_ge(S["kk_scale"], 1)
            link(TT(S1, S1, S2, ALU.mult))
            link(TT(S2, S1, M23, ALU.mult))
            for j in range(2):
                last = TS(M23[:, j, :], M23[:, j, :], vecs[:, 3, j:j + 1], stat[:, 4 + j:5 + j], ALU.mult, ALU.add)
            link(last)
            link(TT(rK, rK, M23, ALU.mult))
            for j in range(2):
                last = STT(S3[:, j, :], rR[:, j, :], vecs[:, 4, j:j + 1], rK[:, j, :], ALU.mult, ALU.mult)
            last.then_inc(S["bonus_ready"], 1)
            v.wait_ge(S["bonus_ready"], 1)
            v.wait_ge(S["decays"], 1)
            TT(S2, S2, D2, ALU.mult)
            TT(rK, rK, D2, ALU.mult)
            TT(rR, rR, D1, ALU.mult)
            for j in range(2):
                last = STT(S1[:, j, :], S1[:, j, :], -1.0, M01[:, j, :], ALU.mult, ALU.mult)
            last.then_inc(S["rwe_done"], 1)
            for q in range(4):
                j, half = q // 2, q % 2
                v.wait_ge(S["aux_done"], 16 + q + 1)
                h_ = slice(half * 512, (half + 1) * 512)
                TT(S3[:, j, h_], bank[q], rV[:, j, h_], ALU.mult).then_inc(S["aux_devac"], 1)

            v.wait_ge(S["fill_done"], NFILL)
            def bc(i):
                return C(i).unsqueeze(1).to_broadcast([P, 4, P])

            def rw_ev(g):
                m, h, key = rw_fills[g]
                b, lo, hi = cbs[h], HD * h, HD * h + HD
                src = bank[6 + g % 2].rearrange("p (q c) -> p q c", q=4)
                v.wait_ge(S["rw_fill"], g + 1)
                done = S["rw_evac"]
                if key == "LT":
                    TT(b["LT"], src, bc(SU), ALU.mult).then_inc(done, 1)
                elif key == "L":
                    TT(b["X"], src, bc(M1), ALU.mult).then_inc(done, 1)
                elif key in ("RbT", "AkT", "RkT"):
                    TT(b[key], src, bc(SU if key == "AkT" else UI), ALU.mult).then_inc(done, 1)
                elif key[0] == "W":
                    TT(b["W"], src, bc(MB + int(key[1])), ALU.mult).then_inc(done, 1)
                elif key[0] == "X":
                    if key == "X0":
                        v.wait_ge(S["rw_init"], 2 * m + h + 1)
                    x_ = b["XT" if key[1] == "T" else "X"]
                    TT(x_, x_, src, ALU.add).then_inc(done, 1)
                elif key == "RP":
                    for n2 in range(2):
                        c0 = (2 * m + n2) * P
                        last = TT(b["RP"][lo:hi, 2 * n2:2 * n2 + 2, :], src[lo:hi, 2 * n2:2 * n2 + 2, :], rR[lo:hi, :, c0:c0 + P], ALU.add)
                    last.then_inc(done, 1)
                elif key == "NG":
                    for n2 in range(2):
                        d = dfac[lo:hi, :, 2 * m + n2:2 * m + n2 + 1].to_broadcast([HD, 2, HD])
                        TT(b["NG"][lo:hi, 2 * n2:2 * n2 + 2, 0:HD], src[lo:hi, 2 * n2:2 * n2 + 2, 0:HD], d, ALU.mult)
                    TT(b["NG"][lo:hi, :, HD:P], src[lo:hi, :, HD:P], C(IDENT)[lo:hi, lo:hi].unsqueeze(1).to_broadcast([HD, 4, HD]), ALU.add).then_inc(done, 1)
                else:
                    n2 = int(key[1])
                    n = 2 * m + n2
                    v.wait_ge(done, evacs["dve"][g] - 1)
                    if n + 1 < NT:
                        for j in range(2):
                            last = STT(st[lo:hi, j, n + 1, :], src[lo:hi, j, 0:HD], dfac[lo:hi, j, n:n + 1], b["NG"][lo:hi, 2 * n2 + j, 0:HD], ALU.mult, ALU.add)
                        last.then_inc(done, 1)

            def centre(q):
                v_ = rV[:, q // 2, q % 2 * 512:(q % 2 + 1) * 512]
                v.wait_ge(S["mean_done"], q + 1)
                TT(v_, v_, bank[6], ALU.subtract).then_inc(S["centred"], 1)

            def rw_finish(q):
                j, h_ = q // 2, slice(q % 2 * 512, (q % 2 + 1) * 512)
                v_ = rV[:, j, h_]
                v.wait_ge(S["rw_rstd"], q + 1)
                link(TT(v_, v_, S2[:, j, h_], ALU.mult))
                link(TS(v_, v_, vecs[:, 5, j:j + 1], vecs[:, 6, j:j + 1], ALU.mult, ALU.add))
                link(TT(v_, v_, S3[:, j, h_], ALU.add))
                TT(M67[:, j, h_], v_, M67[:, j, h_], ALU.mult).then_inc(S["rw_out"], 1)

            def stick(it, step):
                _, i, hh = items[it]
                n, p, q0 = (i + 1) * P, it % 2, i * P
                if step == "l1":
                    v.wait_ge(S["sb_soft"], it + 1)
                    if it >= 2:
                        v.wait_ge(S["at_t"], turn_at[it - 1])
                    link(STT(bufS[p][:, 0:n], pz[p][:, 0:n], 0.0, bufE[p][:, 0:n], ALU.max, ALU.add))
                    link(TT(bufS[p][:, q0:n], bufS[p][:, q0:n], C(SL), ALU.mult))
                elif step == "l2":
                    rev = slice(n - 1, None, -1)
                    link(V.tensor_tensor_scan(bufE[p][:, rev], cst[:, ONES, 0:1].to_broadcast([P, n]), bufS[p][:, rev], 0.0, ALU.mult, ALU.add))
                else:
                    link(TT(bufS[p][:, 0:n], pz[p][:, 0:n], bufE[p][:, 0:n], ALU.subtract))
                    TT(bufS[p][:, q0:n], bufS[p][:, q0:n], C(NEGD), ALU.add).then_inc(S["sb_log"], 1)

            def logits(it, m):
                _, i, hh = items[it]
                n, p = (i + 1) * P, it % 2
                near = min(n, 2 * P)
                z = da_logits(it, m)
                if it == NSB and m == 0:
                    v.wait_ge(t5_in, 64)
                v.wait_ge(S["da_z"], 2 * (it - NSB) + m + 1)
                link(TT(z[:, n - near:n], z[:, n - near:n], t5[:, hh, 2 * P - near:2 * P], ALU.add))
                V.tensor_reduce(stat[:, 16 + 4 * p + m:17 + 4 * p + m], z, AX.X, ALU.max, negate=True).then_inc(S["da_max"], 1)

            def combine(it, step):
                _, i, hh = items[it]
                n, p = (i + 1) * P, it % 2
                r = stat[:, 40 + 4 * p:44 + 4 * p]
                if step == "c1":
                    v.wait_ge(S["da_prob"], 2 * (it - NSB) + 2)
                    link(V.reciprocal(r[:, 0:2], stat[:, 18 + 4 * p:20 + 4 * p]))
                    TT(r[:, 2:3], r[:, 1:2], lam[:, 4:5], ALU.mult).then_inc(S["da_factor"], 1)
                else:
                    v.wait_ge(S["da_scaled"], it - NSB + 1)
                    STT(bufS[p][:, 0:n], bufE[p][:, 0:n], r[:, 2:3], bufS[p][:, 0:n], ALU.mult, ALU.add).then_inc(S["da_attn"], 1)

            link(V.memset(st[:, :, 0, :], 0.0))
            def gain(i, l, norm_sem, done):
                v.wait_ge(norm_sem, i + 1)
                TT(x1[:, i, :], x1[:, i, :], gb[:, 2 * l, :], ALU.mult).then_inc(done, 1)

            def row_stats(i, done):
                bn = stat[:, 0:12].rearrange("p (c k) -> p c k", k=6)
                for c in range(2):
                    last = V.bn_stats(bn[:, c, :], x1[:, i, c * 512:(c + 1) * 512])
                link(last)
                mean, _, minus, _ = fin_stat(i)
                link(V.bn_aggr(stat[:, 48 + 4 * (i % 4):50 + 4 * (i % 4)], bn))
                TS(minus, mean, -1.0, None, ALU.mult).then_inc(done, 1)

            for step, *which in plan["dve"]:
                if step == "rwe":
                    rw_ev(*which)
                elif step == "ct":
                    centre(*which)
                elif step == "nf":
                    rw_finish(*which)
                elif step in ("l1", "l2", "l3"):
                    stick(*which, step)
                elif step in ("c1", "c2"):
                    combine(*which, step)
                elif step == "x":
                    logits(*which)
                elif step == "dn":
                    i, = which
                    ts = slice(i * P, (i + 1) * P)
                    v.wait_ge(S["da_rstd"], i + 1)
                    for j in range(2):
                        last = STT(M23[:, j, ts], M23[:, j, ts], subg[:, 0:1], rms_dev[:, j, :], ALU.mult, ALU.mult)
                    last.then_inc(S["da_done"], 1)
                elif step == "sum":
                    i, c = which
                    if i == 0 and c == 0:
                        v.wait_ge(S["xr_in"], 16)
                    v.wait_ge(S["op_done"], 2 * i + c + 1)
                    h_ = slice(c * 512, (c + 1) * 512)
                    STT(x1[:, i, h_], x1[:, i, h_], ALPHA, bank[6 + c], ALU.mult, ALU.add).then_inc(S["op_sum"], 1)
                elif step == "st":
                    i, = which
                    v.wait_ge(S["op_sum"], 2 * i + 2)
                    row_stats(i, S["ln_stat"])
                elif step == "gn":
                    if which[0] == 0:
                        v.wait_ge(S["gb_in"], 64)
                    gain(*which, 0, S["ln_norm"], S["ln_gain"])
                elif step == "o":
                    it, = which
                    kind, i, hh = items[it]
                    h, j = hh % 2, hh // 2
                    v.wait_ge(S["at_o"], it + 1)
                    V.tensor_copy(mixT[HD * h:HD * h + HD, j + (2 if kind == "da" else 0), i * P:(i + 1) * P],
                                  bank[5][HD * h:HD * h + HD, (it % 4) * P:(it % 4 + 1) * P]).then_inc(S["at_evac"], 1)
            def r3(n):
                return rt[:, n * 128:(n + 1) * 128].rearrange("p (i e) -> p i e", i=NT)

            aff, sel, rk, cmb, pos, tmp = r3(0), r3(1), r3(2), r3(3), r3(4), r3(5)
            gs, tq = rt2[:, 0:32], [rt2[:, 32 * (k + 1):32 * (k + 2)] for k in range(6)]
            grk = rt2[:, 256:288]
            rk4, grk4 = rk.rearrange("p i (g j) -> p (i g) j", j=EPG), grk.rearrange("p (i g) -> p i g", g=EPG)

            def pair_tests(n):
                return [place_hot[:, 0, d, 0:n * (EPG - d)].rearrange("p (i j) -> p i j", i=n) for d in range(1, EPG)]

            go_on = place_hot[:, 0, 6, :]
            link(V.memset(go_on, 1.0))
            V.memset(go_on[:, 0:P:NT], 0.0)
            for j in range(EPG):
                V.memset(rk4[:, :, j], float(EPG - 1 - j))
                V.memset(grk4[:, :, j], float(EPG - 1 - j))
            v.wait_ge(S["rl_ev"], NT)
            link(TS(rl, rl, 1.0, None, ALU.add))
            link(V.reciprocal(aff, rl))
            link(TT(sel, aff, rbias[:, :].unsqueeze(1).to_broadcast([P, NT, NE]), ALU.add))
            s4 = sel.rearrange("p i (g j) -> p (i g) j", j=EPG)
            TT(tq[0], s4[:, :, 0], s4[:, :, 1], ALU.max)
            TT(tq[1], s4[:, :, 0], s4[:, :, 1], ALU.min)
            TT(tq[2], s4[:, :, 2], s4[:, :, 3], ALU.max)
            link(TT(tq[3], s4[:, :, 2], s4[:, :, 3], ALU.min))
            TT(gs, tq[0], tq[2], ALU.max)
            TT(tq[4], tq[0], tq[2], ALU.min)
            link(TT(tq[5], tq[1], tq[3], ALU.max))
            link(TT(tq[4], tq[4], tq[5], ALU.max))
            link(TT(gs, gs, tq[4], ALU.add))

            def ranks(val, rank, cmps):
                for d, c in enumerate(cmps, 1):
                    last = TT(c, val[:, :, 0:EPG - d], val[:, :, d:EPG], ALU.is_ge)
                link(last)
                for d, c in enumerate(cmps, 1):
                    link(TT(rank[:, :, d:EPG], rank[:, :, d:EPG], c, ALU.add))
                    link(TT(rank[:, :, 0:EPG - d], rank[:, :, 0:EPG - d], c, ALU.subtract))

            ranks(s4, rk4, pair_tests(4 * NT))
            ranks(gs.rearrange("p (i g) -> p i g", g=EPG), grk4, pair_tests(NT))
            link(TS(rk, rk, 2.0, None, ALU.is_lt))
            link(TS(grk, grk, 1.0, None, ALU.is_lt))
            TT(rk4, rk4, grk.unsqueeze(2).to_broadcast([P, 32, EPG]), ALU.mult).then_inc(S["route_sel"], 1)
            v.wait_ge(S["route_sel"], 1)
            link(TT(cmb, aff, rk, ALU.mult))
            den = rt2[:, 320:328]
            link(V.tensor_reduce(den, cmb, AX.X, ALU.add))
            link(V.reciprocal(den, den))
            cnt, nb, ends, starts = (rt2[:, 336 + 16 * k:352 + 16 * k] for k in range(4))
            more = place_hot[:, 0, 4, 0:NE * (NT - 1)].rearrange("p (e j) -> p e j", e=NE)
            v.wait_ge(S["cnt_done"], 1)
            tot, upto = bank[1][:, 0:NT * NE], place_hot[:, 0, 7, :]
            link(V.tensor_tensor_scan(upto, go_on, tot, 0.0, ALU.mult, ALU.add))
            TT(pos, upto.rearrange("p (e i) -> p i e", e=NE), tot.rearrange("p (e i) -> p i e", e=NE), ALU.subtract)
            link(TS(cnt, upto[:, NT - 1:NT * NE:NT], 1.0 / P, None, ALU.mult))
            link(TT(more, cnt.unsqueeze(2).to_broadcast([P, NE, NT - 1]), small[:, 1:NT].unsqueeze(1).to_broadcast([P, NE, NT - 1]), ALU.is_gt))
            link(V.tensor_reduce(nb, more, AX.X, ALU.add))
            link(TS(nb, nb, 1.0, None, ALU.add))
            link(V.tensor_tensor_scan(ends, cst[:, ONES, 0:NE], nb, 0.0, ALU.mult, ALU.add))
            link(TT(starts, ends, nb, ALU.subtract))
            link(TS(starts, starts, float(P), 1.0, ALU.mult, ALU.add))
            link(TT(pos, pos, bank[0][:, 0:NT * NE].rearrange("p (i e) -> p i e", i=NT), ALU.add))
            link(TT(pos, pos, starts.unsqueeze(1).to_broadcast([P, NT, NE]), ALU.add))
            link(TT(pos, pos, rk, ALU.mult))
            hi, lo = rt2[:, 400:408], rt2[:, 408:416]
            V.tensor_reduce(hi, pos, AX.X, ALU.max)
            link(V.tensor_reduce(lo, pos, AX.X, ALU.add))
            link(TT(lo, lo, hi, ALU.subtract))
            place, blk = (rt2[:, 448 + 16 * k:464 + 16 * k] for k in range(2))
            tokf = rt2[:, 288:296]
            for s, w in enumerate((hi, lo)):
                link(TT(tmp, pos, w.unsqueeze(2).to_broadcast([P, NT, NE]), ALU.is_equal))
                link(TT(tmp, tmp, cmb, ALU.mult))
                link(V.tensor_reduce(gates[:, s, :], tmp, AX.X, ALU.add))
                link(TT(gates[:, s, :], gates[:, s, :], den, ALU.mult))
                link(TS(w, w, -1.0, None, ALU.add))
                V.tensor_copy(slots[:, s, :], w)
            both = rt2[:, 400:416]
            link(TS(blk, both, 1.0 / P, None, ALU.mult))
            starts_before = blk_hot.rearrange("p s i b -> p (s i) b")
            link(TT(starts_before, blk.unsqueeze(2).to_broadcast([P, 2 * NT, NBP]), small[:, 0:NBP].unsqueeze(1).to_broadcast([P, 2 * NT, NBP]), ALU.is_ge))
            link(V.tensor_reduce(blk, starts_before, AX.X, ALU.add))
            link(TS(blk, blk, -1.0, None, ALU.add))
            link(STT(place, blk, -float(P), both, ALU.mult, ALU.add))
            link(V.tensor_copy(tokf, tok[:, :]))
            for s in range(2):
                TT(place_hot[:, s], C(IOTA).unsqueeze(1).to_broadcast([P, NT, P]), place[:, s * NT:(s + 1) * NT].unsqueeze(2).to_broadcast([P, NT, P]), ALU.is_equal)
                link(TT(blk_hot[:, s], small[:, 0:NBP].unsqueeze(1).to_broadcast([P, NT, NBP]), blk[:, s * NT:(s + 1) * NT].unsqueeze(2).to_broadcast([P, NT, NBP]), ALU.is_equal))
                TT(blk_hot[:, s], blk_hot[:, s], tokf.unsqueeze(2).to_broadcast([P, NT, NBP]), ALU.mult).then_inc(S["slot_hot"], 1)
            eh = mixT[:, 7, 0:NBP * NE].rearrange("p (b e) -> p b e", b=NBP)
            v.wait_ge(S["op_done"], 2 * NT)
            link(TT(eh, small[:, 0:NBP].unsqueeze(2).to_broadcast([P, NBP, NE]), ends.unsqueeze(1).to_broadcast([P, NBP, NE]), ALU.is_ge))
            ef = rt2[:, 416:448]
            link(V.tensor_reduce(ef, eh, AX.X, ALU.add))
            link(TS(ef, ef, float(NE - 1), None, ALU.min))
            link(V.tensor_copy(ef[:, NBP - 1:NBP], ends[:, NE - 1:NE]))
            v.wait_ge(S["slot_sum"], 1)
            V.tensor_copy(slot_tok[:, :], bank[2][:, 0:NBP])
            V.tensor_copy(ids[:, :], ef).then_inc(S["ids_ready"], 1)

            def gated(b):
                v.wait_ge(S["exp_g"], b + 1)
                g, e, h = bank[4 + b % 2], eb[b % 2], hb[b % 2]
                if b >= 2:
                    v.wait_ge(S["h_t"], b - 1)
                TS(e, e, 1.0, None, ALU.add).then_inc(S["gate_step"], 1)
                v.wait_ge(S["gate_step"], 3 * b + 1)
                V.reciprocal(e, e).then_inc(S["gate_step"], 1)
                v.wait_ge(S["gate_step"], 3 * b + 2)
                TT(e, e, g[:, 0:FE], ALU.mult).then_inc(S["gate_step"], 1)
                v.wait_ge(S["gate_step"], 3 * b + 3)
                TT(h, e, g[:, FE:2 * FE], ALU.mult).then_inc(S["gated"], 1)

            v.wait_ge(S["ids_ready"], 1)
            used = used_blocks(v)
            gated(0)
            for b in range(BLOCKS):
                if b + 1 < BLOCKS:
                    with when_used(v, used, b + 1):
                        gated(b + 1)
                with when_used(v, used, b):
                    v.wait_ge(S["down_done"], b + 1)
                    if b >= 2:
                        v.wait_ge(y_st[b % 2], 16 * (b // 2))
                    V.tensor_copy(yb[b % 2][:, 512:1024], bank[3]).then_inc(S["y_ev"], 1)

            for i in range(NT):
                v.wait_ge(S["y_scaled"], i + 1)
                ya, yb2 = sum_bufs(i)
                s = x1[:, i, :]
                link(STT(ya, yb2, gates[:, 1, i:i + 1], ya, ALU.mult, ALU.add))
                link(STT(s, s, ALPHA, ya, ALU.mult, ALU.add))
                row_stats(i, S["fin_stat"])
                if i >= 1:
                    gain(i - 1, 1, S["fin_norm"], S["fin_gain"])
            gain(NT - 1, 1, S["fin_norm"], S["fin_gain"])

        @block.tensor
        def _(pe):
            MM = nc.tensor.matmul

            def turn(o, i):
                return nc.tensor.transpose(o, i, C(IDENT))

            pe.wait_ge(S["mats_in"], 16)

            def turn_x(n):
                i, c = n // 2, n % 2
                if c == 0:
                    pe.wait_ge(x_in[i % 4], 16 * (i // 4 + 1))
                if n >= 4:
                    pe.wait_ge(S["xT_ready"], n - 3)
                for k in range(4):
                    last = turn(bank[n % 4][:, k * P:(k + 1) * P], xs[:, i % 4, (4 * c + k) * P:(4 * c + k + 1) * P])
                last.then_inc(S["x_turned"], 1)

            def fill(n):
                kind, t, half = fills[n]
                if n >= 4:
                    pe.wait_ge(S["fill_evac"], n - 3)
                o = bank[4 + n % 4]
                if n in (0, 4):
                    pe.wait_ge(S["xT_ready"], 8 if n == 0 else 16)
                if kind == "v":
                    if t == 0:
                        pe.wait_ge(wv_in, 32)
                    for k in range(KD):
                        last = MM(o, xT[:, k, t * P:(t + 1) * P], wv[:, k, :], start=k == 0, stop=k == KD - 1)
                else:
                    if half == 0:
                        pe.wait_ge(w_arr[t % 4], 16 * (t // 4 + 1))
                    for k in range(KD):
                        last = MM(o, wring[:, t % 4, k, :], xT[:, k, half * 512:(half + 1) * 512], start=k == 0, stop=k == KD - 1)
                last.then_inc(S["fill_done"], 1)

            def aux(a):
                j, half = a // 2 % 2, a % 2
                h_ = slice(half * 512, (half + 1) * 512)
                if a < 12:
                    if a >= 4:
                        pe.wait_ge(S["aux_evac"], a - 3)
                    lo, hi = ((0, 32), (32, 64), (64, 128))[a // 4]
                    mm = MM(bank[a % 4], low_up[lo:hi, j * P:(j + 1) * P], rw[lo:hi, 6, 1 + half * 512:1 + (half + 1) * 512], start=True, stop=True)
                elif a < 16:
                    pe.wait_ge(S["aux_evac"], a - 3)
                    mm = MM(bank[a % 4], C(BO), S2[:, j, h_], start=True, stop=True)
                else:
                    pe.wait_ge(S["aux_devac"], a - 15)
                    mm = MM(bank[a % 4], C(BO), S3[:, j, h_], start=True, stop=True)
                mm.then_inc(S["aux_done"], 1)

            for n in range(8):
                turn_x(n)
            for n in range(NFILL):
                fill(n)
                if n < 4:
                    turn_x(8 + 2 * n)
                    turn_x(9 + 2 * n)
                if n == 7:
                    pe.wait_ge(S["bias_up"], 1)
                    for h in range(4):
                        MM(bank[h][:, 0:LT5], bias_l[:, h, :], hot, start=True, stop=True).then_inc(S["bias_rows"], 1)
                if n == 18:
                    pe.wait_ge(S["low_ready"], 1)
                    pe.wait_ge(S["bias_evac"], 4)
                    for a in range(12):
                        aux(a)
                if n == 29:
                    pe.wait_ge(S["sq_ready"], 1)
                    for a in range(12, 16):
                        aux(a)
                if n == 36:
                    pe.wait_ge(S["bonus_ready"], 1)
                    for a in range(16, 20):
                        aux(a)

            pe.wait_ge(S["rwe_done"], 1)
            pe.wait_ge(S["aux_devac"], 8)
            pe.wait_ge(S["fill_evac"], NFILL)

            def rw_pe(g):
                m, h, key = rw_fills[g]
                b, lo, hi = cbs[h], HD * h, HD * h + HD
                ps = bank[6 + g % 2]
                o = ps.rearrange("p (q c) -> p q c", q=4)
                if g >= 2:
                    last = rw_operands(g)
                    if evacs["dve"][last]:
                        pe.wait_ge(S["rw_evac"], evacs["dve"][last])
                    pe.wait_ge(S["rw_copied"], evacs["act"][last])
                if key == "W0":
                    pe.wait_ge(S["rw_init"], 2 * m + h + 1)
                for q in range(4):
                    n2, j = q // 2, q % 2
                    n = 2 * m + n2
                    ck = slice(n * P, (n + 1) * P)
                    a_, b_, k_, r_ = S1[lo:hi, j, ck], S2[lo:hi, j, ck], rK[lo:hi, j, ck], rR[lo:hi, j, ck]
                    if key in ("Ta", "Tb", "Tk", "Tv"):
                        src = {"a": S1, "b": S2, "k": rK, "v": rV}[key[1]][:, j, ck]
                        last = turn(o[:, q, :], src)
                    elif key in ("LT", "L", "RbT", "AkT", "RkT"):
                        l_, m_ = {"LT": (b_, a_), "L": (a_, b_), "RbT": (b_, r_), "AkT": (k_, a_), "RkT": (k_, r_)}[key]
                        last = MM(o[:, q, :], l_, m_, start=True, stop=True)
                    elif key == "AkV":
                        last = MM(ps[:, q * HD:(q + 1) * HD], b["AkT"][:, q, :], tm["v"][:, q, lo:hi], start=True, stop=True)
                    elif key[0] in "WX":
                        l_, m_ = ("LT", "X") if key[0] == "W" else ("W", "XT") if key[1] == "T" else ("XT", "W")
                        last = MM(o[:, q, :], b[l_][:, q, :], b[m_][:, q, :], start=True, stop=True)
                    elif key == "U":
                        MM(o[:, q, 0:HD], b["XT"][:, q, :], tm["a"][:, q, lo:hi], start=True, stop=True)
                        last = MM(o[:, q, HD:P], b["XT"][:, q, :], b["AkV"][:, q, :], start=True, stop=True)
                    elif key == "RP":
                        last = MM(o[lo:hi, q, :], b["U"][:, q, 0:HD], b["RbT"][:, q, :], start=True, stop=True)
                    elif key == "NG":
                        MM(o[lo:hi, q, 0:HD], tm["b"][:, q, lo:hi], b["U"][:, q, HD:P], start=True, stop=False)
                        MM(o[lo:hi, q, 0:HD], tm["k"][:, q, lo:hi], tm["v"][:, q, lo:hi], start=False, stop=True)
                        last = MM(o[lo:hi, q, HD:P], b["U"][:, q, 0:HD], tm["b"][:, q, lo:hi], start=True, stop=True)
                    elif key[0] == "S":
                        if n2 == int(key[1]):
                            last = MM(o[lo:hi, j, 0:HD], b["NG"][lo:hi, q, HD:P], st[lo:hi, j, n, :], start=True, stop=True)
                    else:
                        MM(o[lo:hi, q, :], b["U"][:, q, HD:P], b["RbT"][:, q, :], start=True, stop=False)
                        MM(o[lo:hi, q, :], tm["v"][:, q, lo:hi], b["RkT"][:, q, :], start=False, stop=False)
                        last = MM(o[lo:hi, q, :], st[lo:hi, j, n, :], b["RP"][lo:hi, q, :], start=False, stop=True)
                last.then_inc(S["rw_fill"], 1)

            def rw_means(q):
                if q == 0:
                    pe.wait_ge(S["rw_evac"], evacs["dve"][NRW - 1])
                    pe.wait_ge(S["rw_copied"], evacs["act"][NRW - 1])
                else:
                    pe.wait_ge(S["centred"], q)
                MM(bank[6], C(BM), rV[:, q // 2, q % 2 * 512:(q % 2 + 1) * 512], start=True, stop=True).then_inc(S["mean_done"], 1)

            def rw_variances(q):
                pe.wait_ge(S["squared"], q + 1)
                if q >= 1:
                    pe.wait_ge(S["rw_vevac"], q)
                MM(bank[7], C(BM), S1[:, q // 2, q % 2 * 512:(q % 2 + 1) * 512], start=True, stop=True).then_inc(S["var_done"], 1)

            def sb_scores(it):
                _, i, hh = items[it]
                h, j, n, p = hh % 2, hh // 2, (i + 1) * P, it % 2
                if it >= 2:
                    pe.wait_ge(S["sb_log"], it - 1)
                lo = HD * h
                for c in range(0, n, 512):
                    e = min(n, c + 512)
                    last = MM(pz[p][:, c:e], qk[lo:lo + HD, j, i * P:(i + 1) * P], qk[lo:lo + HD, 2 + j, c:e], start=True, stop=True)
                last.then_inc(S["sb_z"], 1)

            def da_scores(it, m):
                _, i, hh = items[it]
                h, j, n = hh % 2, hh // 2, (i + 1) * P
                back = 2 if i < 4 and it - 2 >= NSB else 1
                if it - back < NSB:
                    pe.wait_ge(S["sb_log"], NSB - 1 + m)
                else:
                    pe.wait_ge(S["da_prob"], 2 * (it - back - NSB) + m + 1)
                lo = HD * h + 32 * m
                for c in range(0, n, 512):
                    e = min(n, c + 512)
                    last = MM(da_logits(it, m)[:, c:e], qk[lo:lo + 32, 4 + j, i * P:(i + 1) * P], qk[lo:lo + 32, 6 + j, c:e], start=True, stop=True)
                last.then_inc(S["da_z"], 1)

            def turn_weights(it, part):
                kind, i, hh = items[it]
                p, u = it % 2, turn_at[it] + part
                if part == 0:
                    if kind == "sb":
                        pe.wait_ge(S["sb_w"], it + 1)
                    else:
                        pe.wait_ge(S["da_attn"], it - NSB + 1)
                if u >= 1:
                    pe.wait_ge(S["at_wT"], u)
                for k in range(4 * part, min(i + 1, 4 * part + 4)):
                    last = turn(bank[4][:, (k % 4) * P:(k % 4 + 1) * P], bufS[p][:, k * P:(k + 1) * P])
                last.then_inc(S["at_t"], 1)

            def values(it, part):
                kind, i, hh = items[it]
                h, p = hh % 2, it % 2
                lo, v0 = HD * h, (GW if kind == "da" else 0) + hh * HD
                pe.wait_ge(S["at_wT"], turn_at[it] + part + 1)
                if part == 0 and it >= 2:
                    pe.wait_ge(S["at_evac"], it - 1)
                for k in range(4 * part, min(i + 1, 4 * part + 4)):
                    last = MM(bank[5][lo:lo + HD, (it % 4) * P:(it % 4 + 1) * P], vt[:, k, v0:v0 + HD], bufT[p][:, k, :], start=k == 0, stop=k == i)
                if part == i // 4:
                    last.then_inc(S["at_o"], 1)

            def mean_squares(i):
                pe.wait_ge(S["da_sq"], i + 1)
                if i >= 1:
                    pe.wait_ge(S["da_rstd"], i)
                if i >= 2:
                    pe.wait_ge(S["op_sum"], 2 * i - 2)
                MM(rms_bank, C(BM), mid[:, 9216:9472], start=True, stop=True).then_inc(S["da_ms"], 1)

            def project(i, c, part):
                if part == 0:
                    if i == 0 and c == 0:
                        pe.wait_ge(S["wout_in"], 16)
                        pe.wait_ge(S["centred"], 4)
                    if c == 1:
                        pe.wait_ge(S["da_rstd"], min(i + 2, NT))
                    pe.wait_ge(S["da_done"], i + 1)
                    if i >= 1:
                        pe.wait_ge(S["op_sum"], 2 * i + c - 1)
                for k in range(2 * part, 2 * part + 2):
                    last = MM(bank[6 + c], mixT[:, k, i * P:(i + 1) * P], wout[:, k, c * 512:(c + 1) * 512], start=k == 0, stop=k == 7)
                if part == 3:
                    last.then_inc(S["op_done"], 1)

            def turn_x1(i):
                pe.wait_ge(S["x1_ready"], i + 1)
                pe.wait_ge(S["at_evac"], NI)
                if i >= 1:
                    pe.wait_ge(S["x1_tev"], i)
                for k in range(KD):
                    last = turn(bank[4 + k // 4][:, (k % 4) * P:(k % 4 + 1) * P], x1[:, i, k * P:(k + 1) * P])
                last.then_inc(S["x1_t"], 1)

            def router(i):
                pe.wait_ge(S["x1_tev"], i + 1)
                if i >= 1:
                    pe.wait_ge(S["rl_ev"], i)
                for k in range(KD):
                    last = MM(bank[0][:, 0:NE], x1T[:, k, :], rwr[:, k, :], start=k == 0, stop=k == KD - 1)
                last.then_inc(S["rl_done"], 1)

            steps = {"rw": rw_pe, "mn": rw_means, "vr": rw_variances, "z": sb_scores, "s": da_scores, "t": turn_weights, "v": values,
                     "dm": mean_squares, "pj": project, "ro": turn_x1, "rm": router}
            for step, *which in plan["pe"]:
                steps[step](*which)
            pe.wait_ge(S["route_sel"], 1)
            selm = rt[:, 256:384]
            pe.wait_ge(S["rl_ev"], NT)
            MM(bank[0][:, 0:NT * NE], C(SU), selm, start=True, stop=True)
            by_expert = bank[1][:, 0:NT * NE].rearrange("p (e i) -> p e i", e=NE)
            MM(by_expert, C(ONES), selm.rearrange("p (i e) -> p e i", i=NT), start=True, stop=True).then_inc(S["cnt_done"], 1)
            for s in range(2):
                pe.wait_ge(S["slot_hot"], s + 1)
                for i in range(NT):
                    last = MM(bank[2][:, 0:NBP], place_hot[:, s, i, :], blk_hot[:, s, i, :], start=s == 0 and i == 0, stop=s == 1 and i == NT - 1)
            last.then_inc(S["slot_sum"], 1)

            def gather_turn(b):
                pe.wait_ge(xg_in[b % 2], 16 * (b // 2 + 1))
                if b >= 1:
                    pe.wait_ge(S["xg_tev"], b)
                for k in range(KD):
                    last = turn(bank[k // 4][:, (k % 4) * P:(k % 4 + 1) * P], xg[b % 2][:, k * P:(k + 1) * P])
                last.then_inc(S["xg_t"], 1)

            def up(b):
                pe.wait_ge(S["xg_tev"], b + 1)
                pe.wait_ge(we_in[b % 3], 16 * (b // 3 + 1))
                if b >= 2:
                    pe.wait_ge(S["gated"], b - 1)
                for k in range(KD):
                    last = MM(bank[4 + b % 2], xgT[b % 2][:, k, :], weu[b % 3][:, k, :], start=k == 0, stop=k == KD - 1)
                last.then_inc(S["up_done"], 1)

            def turn_h(b):
                pe.wait_ge(S["gated"], b + 1)
                if b >= 1:
                    pe.wait_ge(S["h_tev"], b)
                for k in range(2):
                    last = turn(bank[6][:, k * P:(k + 1) * P], hb[b % 2][:, k * P:(k + 1) * P])
                last.then_inc(S["h_t"], 1)

            def down(b):
                pe.wait_ge(S["h_tev"], b + 1)
                pe.wait_ge(wd_in[b % 3], 16 * (b // 3 + 1))
                if b >= 1:
                    pe.wait_ge(S["y_ev"], 2 * b)
                for c in range(2):
                    for k in range(2):
                        last = MM(bank[2 + c], hTb[b % 2][:, k, :], wed[b % 3][:, k, c * 512:(c + 1) * 512], start=k == 0, stop=k == 1)
                last.then_inc(S["down_done"], 1)

            pe.wait_ge(S["ids_ready"], 1)
            used = used_blocks(pe)
            gather_turn(0)
            gather_turn(1)
            up(0)
            for b in range(BLOCKS):
                with when_used(pe, used, b):
                    turn_h(b)
                if b + 2 < BLOCKS:
                    with when_used(pe, used, b + 2):
                        gather_turn(b + 2)
                if b + 1 < BLOCKS:
                    with when_used(pe, used, b + 1):
                        up(b + 1)
                with when_used(pe, used, b):
                    down(b)


_INS = ['x', 'w_in', 'w_out', 'da_lambda', 'da_subln', 'sc_conv', 'rw_mu', 'rw_vecs', 'rw_w_up', 'rw_a_up', 'rw_g_up',
        'ln_gain', 'ln_bias', 'rel_bias', 'router_w', 'router_b', 'moe_w_in', 'moe_w_down']


def kernel(**inputs):
    import concourse.bacc as _bacc
    from concourse.bass_utils import run_bass_kernel_spmd as _run

    nc = _bacc.Bacc("TRN2", target_bir_lowering=False, num_devices=1)
    arrays, args = {}, []
    values = {n: np.ascontiguousarray(inputs[n]) for n in _INS}
    values.update(constants())
    for name, a in values.items():
        arrays[f"in_{name}"] = a
        args.append(nc.dram_tensor(f"in_{name}", a.shape, mybir.dt.from_np(a.dtype), kind="ExternalInput").ap())
    args.append(nc.dram_tensor("out_0", (1, T, D), F32, kind="ExternalOutput").ap())
    layer_kernel(nc, *args)
    r = _run(nc, [arrays], core_ids=[0])
    return r.results[0]["out_0"]
```
